# Optimizing a Trainium2 kernel written in Bass

```python
import math
import jax
import jax.numpy as jnp
from jax import lax
import numpy as np
import jax, jax.numpy as jnp

D_MODEL = 1024
BATCH = 1
SEQ = 256
DEPTH = 2

N_EVEN = (DEPTH + 1) // 2
N_ODD = DEPTH // 2
NORM_EPS = 1e-6

SSD_HEAD_DIM = 64
SSD_HEADS = 16
SSD_GROUPS = 2
SSD_HEADS_PER_GROUP = SSD_HEADS // SSD_GROUPS
SSD_STATE = 128
SSD_CHUNK = 128
CONV_WIDTH = 4
D_SSM = SSD_HEADS * SSD_HEAD_DIM
CONV_DIM = D_SSM + 2 * SSD_GROUPS * SSD_STATE

GLA_HEADS = 4
GLA_KEY_DIM = D_MODEL // 2
GLA_VAL_DIM = D_MODEL
GLA_HEAD_K = GLA_KEY_DIM // GLA_HEADS
GLA_HEAD_V = GLA_VAL_DIM // GLA_HEADS
GLA_GATE_RANK = 16
GLA_GATE_NORM = 16.0
GLA_CHUNK = 64

IN_SIZES = (D_SSM, CONV_DIM, SSD_HEADS, GLA_KEY_DIM, GLA_KEY_DIM, GLA_VAL_DIM, GLA_VAL_DIM, GLA_GATE_RANK)
IN_COLS = sum(IN_SIZES)
MIX_WIDTH = D_SSM + GLA_VAL_DIM

MLA_HEADS = 16
MLA_NOPE = 64
MLA_ROPE = 32
MLA_V = 64
MLA_Q_RANK = 384
MLA_KV_RANK = 256
ROPE_THETA = 10000.0
ATTN_BLOCK = 128

FFN_HIDDEN = -(-(8 * D_MODEL) // (3 * 256)) * 256


def _offsets(sizes):
    out, acc = [], 0
    for s in sizes[:-1]:
        acc += s
        out.append(acc)
    return out

def rms_norm(x, w):
    xf = x.astype(jnp.float32)
    y = xf * lax.rsqrt(jnp.mean(xf * xf, axis=-1, keepdims=True) + NORM_EPS)
    return (y * w.astype(jnp.float32)).astype(x.dtype)

def causal_depthwise_conv(x, w, b):
    c = x.shape[-1]
    y = lax.conv_general_dilated(x, w[:, None, :].astype(x.dtype), window_strides=(1,),
                                 padding=[(CONV_WIDTH - 1, 0)],
                                 dimension_numbers=('NWC', 'WIO', 'NWC'),
                                 feature_group_count=c)
    return y + b

def ssd_mixer(z, xbc, dt_raw, conv_w, conv_b, dt_bias, a_log, d_skip, norm_w):
    bsz, seqlen, _ = z.shape
    G, K, P, N, Q = SSD_GROUPS, SSD_HEADS_PER_GROUP, SSD_HEAD_DIM, SSD_STATE, SSD_CHUNK
    nc = seqlen // Q
    xbc = jax.nn.silu(causal_depthwise_conv(xbc, conv_w, conv_b))
    xs, bm, cm = jnp.split(xbc, [D_SSM, D_SSM + G * N], axis=-1)
    xs = xs.reshape(bsz, nc, Q, G, K, P)
    bm = bm.reshape(bsz, nc, Q, G, N)
    cm = cm.reshape(bsz, nc, Q, G, N)
    dt = jax.nn.softplus(dt_raw + dt_bias).reshape(bsz, nc, Q, G, K)
    a = dt * (-jnp.exp(a_log)).reshape(G, K)
    a_cum = jnp.cumsum(a, axis=2)
    xdt = xs * dt[..., None]
    causal = jnp.tril(jnp.ones((Q, Q), dtype=bool))
    seg = a_cum[:, :, :, None] - a_cum[:, :, None, :]
    decay = jnp.exp(jnp.where(causal[:, :, None, None], seg, -jnp.inf))
    cb = jnp.einsum('bclgn,bcsgn->bclsg', cm, bm)
    y_diag = jnp.einsum('bclsg,bclsgk,bcsgkp->bclgkp', cb, decay, xdt)
    to_end = jnp.exp(a_cum[:, :, -1:] - a_cum)
    states = jnp.einsum('bcsgn,bcsgk,bcsgkp->bcgkpn', bm, to_end, xdt)
    chunk_decay = jnp.exp(a_cum[:, :, -1])

    def step(h, inp):
        s_c, d_c = inp
        return h * d_c[..., None, None] + s_c, h

    h0 = jnp.zeros((bsz, G, K, P, N), states.dtype)
    _, prev = lax.scan(step, h0, (jnp.moveaxis(states, 1, 0), jnp.moveaxis(chunk_decay, 1, 0)))
    prev = jnp.moveaxis(prev, 0, 1)
    y_off = jnp.einsum('bclgn,bcgkpn,bclgk->bclgkp', cm, prev, jnp.exp(a_cum))
    y = y_diag + y_off + xs * d_skip.reshape(G, K)[:, :, None]
    y = y.reshape(bsz, seqlen, D_SSM) * jax.nn.silu(z)
    gsz = D_SSM // G
    y = rms_norm(y.reshape(bsz, seqlen, G, gsz), norm_w.reshape(G, gsz))
    return y.reshape(bsz, seqlen, D_SSM)

def gla_mixer(q, k, v, g, gk_low, gk_w2, gk_b, norm_w):
    bsz, seqlen, _ = q.shape
    H, DK, DV, Q = GLA_HEADS, GLA_HEAD_K, GLA_HEAD_V, GLA_CHUNK
    nc = seqlen // Q
    dtype = q.dtype
    gk = jax.nn.log_sigmoid((gk_low @ gk_w2 + gk_b).astype(jnp.float32)) / GLA_GATE_NORM
    gcum = jnp.cumsum(gk.reshape(bsz, nc, Q, H, DK), axis=2)
    g_last = gcum[:, :, -1]
    q = q.reshape(bsz, nc, Q, H, DK) * (DK ** -0.5)
    k = k.reshape(bsz, nc, Q, H, DK)
    v = v.reshape(bsz, nc, Q, H, DV)
    q_dec = q * jnp.exp(gcum).astype(dtype)
    k_inv = k * jnp.exp(-gcum).astype(dtype)
    k_end = k * jnp.exp(g_last[:, :, None] - gcum).astype(dtype)
    causal = jnp.tril(jnp.ones((Q, Q), dtype=bool))
    scores = jnp.where(causal, jnp.einsum('bcihd,bcjhd->bchij', q_dec, k_inv), 0)
    o_intra = jnp.einsum('bchij,bcjhv->bcihv', scores, v)
    chunk_kv = jnp.einsum('bcjhd,bcjhv->bchdv', k_end, v)
    chunk_decay = jnp.exp(g_last).astype(dtype)

    def step(s, inp):
        kv_c, d_c = inp
        return s * d_c[..., None] + kv_c, s

    s0 = jnp.zeros((bsz, H, DK, DV), chunk_kv.dtype)
    _, prev = lax.scan(step, s0, (jnp.moveaxis(chunk_kv, 1, 0), jnp.moveaxis(chunk_decay, 1, 0)))
    prev = jnp.moveaxis(prev, 0, 1)
    o_inter = jnp.einsum('bcihd,bchdv->bcihv', q_dec, prev)
    o = (o_intra + o_inter).reshape(bsz, seqlen, H, DV)
    o = rms_norm(o, norm_w) * jax.nn.silu(g.reshape(bsz, seqlen, H, DV))
    return o.reshape(bsz, seqlen, GLA_VAL_DIM)

def ssd_gla_layer(h, w_in, conv_w, conv_b, dt_bias, a_log, d_skip, ssd_norm,
                  gla_gk_w2, gla_gk_b, gla_norm, w_out):
    bsz, seqlen, _ = h.shape
    proj = h @ w_in
    z, xbc, dt_raw, q, k, v, g, gk_low = jnp.split(proj, _offsets(IN_SIZES), axis=-1)
    y_ssd = ssd_mixer(z, xbc, dt_raw, conv_w, conv_b, dt_bias, a_log, d_skip, ssd_norm)
    y_gla = gla_mixer(q, k, v, g, gk_low, gla_gk_w2, gla_gk_b, gla_norm)
    return jnp.concatenate([y_ssd, y_gla], axis=-1) @ w_out

def rope_tables(seqlen):
    pos = jnp.arange(seqlen, dtype=jnp.float32)
    inv = 1.0 / (ROPE_THETA ** (jnp.arange(0, MLA_ROPE, 2, dtype=jnp.float32) / MLA_ROPE))
    ang = pos[:, None] * inv[None, :]
    return jnp.cos(ang), jnp.sin(ang)

def apply_rope(x, cos, sin):
    x1, x2 = jnp.split(x, 2, axis=-1)
    cos = cos.astype(x.dtype)
    sin = sin.astype(x.dtype)
    return jnp.concatenate([x1 * cos - x2 * sin, x2 * cos + x1 * sin], axis=-1)

def mla_layer(h, w_dqkv, q_lora_norm, w_uq, kv_lora_norm, w_ukv,
              q_nope_norm, q_rope_norm, k_nope_norm, k_rope_norm, w_o):
    bsz, seqlen, _ = h.shape
    H = MLA_HEADS
    cq, ckv, k_rope = jnp.split(h @ w_dqkv, [MLA_Q_RANK, MLA_Q_RANK + MLA_KV_RANK], axis=-1)
    q = (rms_norm(cq, q_lora_norm) @ w_uq).reshape(bsz, seqlen, H, MLA_NOPE + MLA_ROPE)
    q_nope, q_rope = jnp.split(q, [MLA_NOPE], axis=-1)
    kv = (rms_norm(ckv, kv_lora_norm) @ w_ukv).reshape(bsz, seqlen, H, MLA_NOPE + MLA_V)
    k_nope, v = jnp.split(kv, [MLA_NOPE], axis=-1)
    cos, sin = rope_tables(seqlen)
    q_nope = rms_norm(q_nope, q_nope_norm)
    q_rope = apply_rope(rms_norm(q_rope, q_rope_norm), cos[:, None, :], sin[:, None, :])
    k_nope = rms_norm(k_nope, k_nope_norm)
    k_rope = apply_rope(rms_norm(k_rope, k_rope_norm), cos, sin)
    scale = (MLA_NOPE + MLA_ROPE) ** -0.5
    kpos = jnp.arange(seqlen)

    def block(i):
        start = i * ATTN_BLOCK
        qn = lax.dynamic_slice_in_dim(q_nope, start, ATTN_BLOCK, axis=1)
        qr = lax.dynamic_slice_in_dim(q_rope, start, ATTN_BLOCK, axis=1)
        s = jnp.einsum('bqhd,bkhd->bhqk', qn, k_nope) + jnp.einsum('bqhr,bkr->bhqk', qr, k_rope)
        s = s.astype(jnp.float32) * scale
        qpos = start + jnp.arange(ATTN_BLOCK)
        mask = kpos[None, :] <= qpos[:, None]
        p = jax.nn.softmax(jnp.where(mask, s, -jnp.inf), axis=-1).astype(v.dtype)
        return jnp.einsum('bhqk,bkhv->bqhv', p, v)

    o = lax.map(block, jnp.arange(seqlen // ATTN_BLOCK))
    o = jnp.moveaxis(o, 0, 1).reshape(bsz, seqlen, H * MLA_V)
    return o @ w_o

def swiglu(h, w_gate, w_up, w_down):
    return (jax.nn.silu(h @ w_gate) * (h @ w_up)) @ w_down

def first_inputs(seed: int = 0) -> dict:
    key = jax.random.key(seed)
    keys = iter(jax.random.split(key, 40))

    def nrm(shape, scale):
        return jax.random.normal(next(keys), shape, jnp.float32) * scale

    def gain(shape):
        return 1.0 + nrm(shape, 0.02)

    NE, NO = N_EVEN, N_ODD
    x = nrm((BATCH, SEQ, D_MODEL), 1.0)
    u = jax.random.uniform(next(keys), (NE, SSD_HEADS), jnp.float32)
    dt0 = jnp.exp(u * (math.log(0.1) - math.log(0.001)) + math.log(0.001))
    dt_bias = dt0 + jnp.log(-jnp.expm1(-dt0))
    a_log = jnp.log(jax.random.uniform(next(keys), (NE, SSD_HEADS), jnp.float32, 1.0, 16.0))
    return {
        'x': x,
        'mix_norm_even': gain((NE, D_MODEL)),
        'w_in_even': nrm((NE, D_MODEL, IN_COLS), D_MODEL ** -0.5),
        'conv_w': nrm((NE, CONV_WIDTH, CONV_DIM), CONV_WIDTH ** -0.5),
        'conv_b': nrm((NE, CONV_DIM), 0.02),
        'dt_bias': dt_bias,
        'a_log': a_log,
        'd_skip': 1.0 + nrm((NE, SSD_HEADS), 0.1),
        'ssd_norm': gain((NE, D_SSM)),
        'gla_gk_w2': nrm((NE, GLA_GATE_RANK, GLA_KEY_DIM), GLA_GATE_RANK ** -0.5),
        'gla_gk_b': nrm((NE, GLA_KEY_DIM), 0.1),
        'gla_norm': gain((NE, GLA_HEAD_V)),
        'w_out_even': nrm((NE, MIX_WIDTH, D_MODEL), MIX_WIDTH ** -0.5),
        'mix_norm_odd': gain((NO, D_MODEL)),
        'w_dqkv': nrm((NO, D_MODEL, MLA_Q_RANK + MLA_KV_RANK + MLA_ROPE), D_MODEL ** -0.5),
        'q_lora_norm': gain((NO, MLA_Q_RANK)),
        'w_uq': nrm((NO, MLA_Q_RANK, MLA_HEADS * (MLA_NOPE + MLA_ROPE)), MLA_Q_RANK ** -0.5),
        'kv_lora_norm': gain((NO, MLA_KV_RANK)),
        'w_ukv': nrm((NO, MLA_KV_RANK, MLA_HEADS * (MLA_NOPE + MLA_V)), MLA_KV_RANK ** -0.5),
        'q_nope_norm': gain((NO, MLA_NOPE)),
        'q_rope_norm': gain((NO, MLA_ROPE)),
        'k_nope_norm': gain((NO, MLA_NOPE)),
        'k_rope_norm': gain((NO, MLA_ROPE)),
        'w_o_mla': nrm((NO, MLA_HEADS * MLA_V, D_MODEL), (MLA_HEADS * MLA_V) ** -0.5),
        'ffn_norm': gain((DEPTH, D_MODEL)),
        'w_gate': nrm((DEPTH, D_MODEL, FFN_HIDDEN), D_MODEL ** -0.5),
        'w_up': nrm((DEPTH, D_MODEL, FFN_HIDDEN), D_MODEL ** -0.5),
        'w_down': nrm((DEPTH, FFN_HIDDEN, D_MODEL), FFN_HIDDEN ** -0.5),
    }

def first_block(x, mix_norm_even, w_in_even, conv_w, conv_b, dt_bias, a_log, d_skip, ssd_norm,
              gla_gk_w2, gla_gk_b, gla_norm, w_out_even,
              mix_norm_odd, w_dqkv, q_lora_norm, w_uq, kv_lora_norm, w_ukv,
              q_nope_norm, q_rope_norm, k_nope_norm, k_rope_norm, w_o_mla,
              ffn_norm, w_gate, w_up, w_down):
    for i in range(DEPTH):
        j = i // 2
        if i % 2 == 0:
            h = rms_norm(x, mix_norm_even[j])
            x = x + ssd_gla_layer(h, w_in_even[j], conv_w[j], conv_b[j], dt_bias[j], a_log[j],
                                  d_skip[j], ssd_norm[j], gla_gk_w2[j], gla_gk_b[j], gla_norm[j],
                                  w_out_even[j])
        else:
            h = rms_norm(x, mix_norm_odd[j])
            x = x + mla_layer(h, w_dqkv[j], q_lora_norm[j], w_uq[j], kv_lora_norm[j], w_ukv[j],
                              q_nope_norm[j], q_rope_norm[j], k_nope_norm[j], k_rope_norm[j],
                              w_o_mla[j])
        x = x + swiglu(rms_norm(x, ffn_norm[i]), w_gate[i], w_up[i], w_down[i])
    return x


N_RET_HEADS = 4
RET_HEAD_DIM = 128
RET_WIDTH = N_RET_HEADS * RET_HEAD_DIM
POOL_WINDOWS = (2, 4, 8, 16)
POOL_GROUP_DIM = 128
POOL_WIDTH = len(POOL_WINDOWS) * POOL_GROUP_DIM
MIX_WIDTH_2 = RET_WIDTH + POOL_WIDTH
IN_WIDTH = 4 * RET_WIDTH + POOL_WIDTH
CHUNK = 128
ROPE_BASE = 10000.0
CONV_WIDTH_2 = 31
D_FF = -(-8 * D_MODEL // (3 * 256)) * 256
EPS = 1e-6
N_EVEN_2 = (DEPTH + 1) // 2
N_ODD_2 = DEPTH // 2


def rms_norm_2(x, g):
    x32 = x.astype(jnp.float32)
    y = x32 * lax.rsqrt(jnp.mean(x32 * x32, axis=-1, keepdims=True) + EPS)
    return (y * g).astype(x.dtype)

def rope(t, positions):
    half = t.shape[-1] // 2
    inv_freq = ROPE_BASE ** (-jnp.arange(half, dtype=jnp.float32) / half)
    ang = positions.astype(jnp.float32)[..., None] * inv_freq
    cos = jnp.cos(ang)[:, :, None, :]
    sin = jnp.sin(ang)[:, :, None, :]
    t1, t2 = t[..., :half], t[..., half:]
    return jnp.concatenate([t1 * cos - t2 * sin, t1 * sin + t2 * cos], axis=-1)

def retention(q, k, v, positions):
    B, S, H, Dh = q.shape
    n_chunks = S // CHUNK
    q = rope(q, positions)
    k = rope(k, positions) * (Dh ** -0.5)
    log_gamma = jnp.log1p(-(2.0 ** (-5.0 - jnp.arange(H, dtype=jnp.float32))))
    idx = jnp.arange(CHUNK, dtype=jnp.float32)
    rel = idx[:, None] - idx[None, :]
    decay_mask = jnp.where(rel >= 0, jnp.exp(log_gamma[:, None, None] * jnp.maximum(rel, 0.0)), 0.0)
    q_decay = jnp.exp(log_gamma[:, None] * (idx + 1.0))
    k_decay = jnp.exp(log_gamma[:, None] * (CHUNK - 1.0 - idx))
    chunk_decay = jnp.exp(log_gamma * CHUNK)

    def to_chunks(t):
        return t.reshape(B, n_chunks, CHUNK, H, Dh).transpose(0, 3, 1, 2, 4)

    qc, kc, vc = to_chunks(q), to_chunks(k), to_chunks(v)
    scores = jnp.einsum('bhncd,bhnmd->bhncm', qc, kc) * decay_mask[:, None]
    o_intra = jnp.einsum('bhncm,bhnme->bhnce', scores, vc)
    kv = jnp.einsum('bhnmd,bhnme->nbhde', kc * k_decay[:, None, :, None], vc)

    def step(state, kv_n):
        return state * chunk_decay[None, :, None, None] + kv_n, state

    _, prev_states = lax.scan(step, jnp.zeros((B, H, Dh, Dh), jnp.float32), kv)
    o_cross = jnp.einsum('bhncd,nbhde->bhnce', qc * q_decay[:, None, :, None], prev_states)
    return (o_intra + o_cross).transpose(0, 2, 3, 1, 4).reshape(B, S, H, Dh)

def multiscale_pool(u, pool_w, pool_scale):
    B, S, _ = u.shape
    u32 = u.astype(jnp.float32)
    cs0 = jnp.pad(jnp.cumsum(u32, axis=1), ((0, 0), (1, 0), (0, 0)))
    t = jnp.arange(S)
    outs = []
    for gi, w in enumerate(POOL_WINDOWS):
        c = cs0[:, :, gi * POOL_GROUP_DIM:(gi + 1) * POOL_GROUP_DIM]
        lower = jnp.pad(c[:, :S + 1 - w], ((0, 0), (w - 1, 0), (0, 0)))
        count = jnp.minimum(t + 1, w).astype(jnp.float32)[None, :, None]
        y = (c[:, 1:] - lower) / count - u32[:, :, gi * POOL_GROUP_DIM:(gi + 1) * POOL_GROUP_DIM]
        outs.append(jnp.einsum('bsc,cd->bsd', y.astype(u.dtype), pool_w[gi]))
    return jnp.concatenate(outs, axis=-1) * pool_scale

def retention_pool_mixer(h, positions, w_in, ret_norm_g, pool_w, pool_scale, w_out):
    B, S, _ = h.shape
    proj = h @ w_in
    q, k, v, g, u = jnp.split(proj, [RET_WIDTH, 2 * RET_WIDTH, 3 * RET_WIDTH, 4 * RET_WIDTH], axis=-1)

    def heads(t):
        return t.reshape(B, S, N_RET_HEADS, RET_HEAD_DIM).astype(jnp.float32)

    o = retention(heads(q), heads(k), heads(v), positions)
    mu = jnp.mean(o, axis=-1, keepdims=True)
    var = jnp.mean(jnp.square(o - mu), axis=-1, keepdims=True)
    o = ((o - mu) * lax.rsqrt(var + EPS)).reshape(B, S, RET_WIDTH) * ret_norm_g
    ret_out = (jax.nn.silu(g.astype(jnp.float32)) * o).astype(h.dtype)
    pool_out = multiscale_pool(u, pool_w, pool_scale).astype(h.dtype)
    return jnp.concatenate([ret_out, pool_out], axis=-1) @ w_out

def conformer_conv(h, w_pw1, b_pw1, w_dw, b_dw, ln_g, ln_b, w_pw2, b_pw2):
    a, gate = jnp.split(h @ w_pw1 + b_pw1, 2, axis=-1)
    u = a * jax.nn.sigmoid(gate)
    dw = lax.conv_general_dilated(
        u, w_dw[:, None, :], window_strides=(1,), padding=((CONV_WIDTH_2 - 1, 0),),
        dimension_numbers=('NWC', 'WIO', 'NWC'), feature_group_count=D_MODEL) + b_dw
    d32 = dw.astype(jnp.float32)
    mu = jnp.mean(d32, axis=-1, keepdims=True)
    var = jnp.mean(jnp.square(d32 - mu), axis=-1, keepdims=True)
    z = (d32 - mu) * lax.rsqrt(var + EPS) * ln_g + ln_b
    z = jax.nn.silu(z).astype(h.dtype)
    return z @ w_pw2 + b_pw2

def swiglu_2(h, w_gate, w_up, w_down):
    return (jax.nn.silu(h @ w_gate) * (h @ w_up)) @ w_down

def second_inputs(seed: int = 0) -> dict:
    key = jax.random.key(seed)
    ks = jax.random.split(key, 24)
    f32 = jnp.float32

    def dense(k, shape, fan_in):
        return jax.random.normal(k, shape, f32) * (fan_in ** -0.5)

    def gain(k, shape):
        return 1.0 + 0.05 * jax.random.normal(k, shape, f32)

    def bias(k, shape):
        return 0.01 * jax.random.normal(k, shape, f32)

    return {
        "x": jax.random.normal(ks[0], (BATCH, SEQ, D_MODEL), f32),
        "positions": jnp.broadcast_to(jnp.arange(SEQ, dtype=jnp.int32), (BATCH, SEQ)),
        "mixer_norm_g": gain(ks[1], (DEPTH, D_MODEL)),
        "ffn_norm_g": gain(ks[2], (DEPTH, D_MODEL)),
        "final_norm_g": gain(ks[3], (D_MODEL,)),
        "ret_w_in": dense(ks[4], (N_EVEN_2, D_MODEL, IN_WIDTH), D_MODEL),
        "ret_norm_g": gain(ks[5], (N_EVEN_2, RET_WIDTH)),
        "pool_w": dense(ks[6], (N_EVEN_2, len(POOL_WINDOWS), POOL_GROUP_DIM, POOL_GROUP_DIM), POOL_GROUP_DIM),
        "pool_scale": gain(ks[7], (N_EVEN_2, POOL_WIDTH)),
        "mix_w_out": dense(ks[8], (N_EVEN_2, MIX_WIDTH_2, D_MODEL), MIX_WIDTH_2),
        "conv_w_pw1": dense(ks[9], (N_ODD_2, D_MODEL, 2 * D_MODEL), D_MODEL),
        "conv_b_pw1": bias(ks[10], (N_ODD_2, 2 * D_MODEL)),
        "conv_w_dw": dense(ks[11], (N_ODD_2, CONV_WIDTH_2, D_MODEL), CONV_WIDTH_2),
        "conv_b_dw": bias(ks[12], (N_ODD_2, D_MODEL)),
        "conv_ln_g": gain(ks[13], (N_ODD_2, D_MODEL)),
        "conv_ln_b": bias(ks[14], (N_ODD_2, D_MODEL)),
        "conv_w_pw2": dense(ks[15], (N_ODD_2, D_MODEL, D_MODEL), D_MODEL),
        "conv_b_pw2": bias(ks[16], (N_ODD_2, D_MODEL)),
        "ffn_w_gate": dense(ks[17], (DEPTH, D_MODEL, D_FF), D_MODEL),
        "ffn_w_up": dense(ks[18], (DEPTH, D_MODEL, D_FF), D_MODEL),
        "ffn_w_down": dense(ks[19], (DEPTH, D_FF, D_MODEL), D_FF),
    }

def second_block(x, positions, mixer_norm_g, ffn_norm_g, final_norm_g, ret_w_in, ret_norm_g,
              pool_w, pool_scale, mix_w_out, conv_w_pw1, conv_b_pw1, conv_w_dw, conv_b_dw,
              conv_ln_g, conv_ln_b, conv_w_pw2, conv_b_pw2, ffn_w_gate, ffn_w_up, ffn_w_down):
    h = x
    for layer in range(DEPTH):
        i = layer // 2
        hn = rms_norm_2(h, mixer_norm_g[layer])
        if layer % 2 == 0:
            h = h + retention_pool_mixer(hn, positions, ret_w_in[i], ret_norm_g[i],
                                         pool_w[i], pool_scale[i], mix_w_out[i])
        else:
            h = h + conformer_conv(hn, conv_w_pw1[i], conv_b_pw1[i], conv_w_dw[i], conv_b_dw[i],
                                   conv_ln_g[i], conv_ln_b[i], conv_w_pw2[i], conv_b_pw2[i])
        h = h + swiglu_2(rms_norm_2(h, ffn_norm_g[layer]), ffn_w_gate[layer], ffn_w_up[layer], ffn_w_down[layer])
    return rms_norm_2(h, final_norm_g)


def setup_inputs(seed=0):
    out = dict(first_inputs(seed))
    for name, value in second_inputs(seed + 1).items():
        if name != "x":
            out[name + "_2"] = value
    return out


def reference(
    x, mix_norm_even, w_in_even, conv_w, conv_b, dt_bias, a_log, d_skip, ssd_norm, gla_gk_w2,
    gla_gk_b, gla_norm, w_out_even, mix_norm_odd, w_dqkv, q_lora_norm, w_uq, kv_lora_norm,
    w_ukv, q_nope_norm, q_rope_norm, k_nope_norm, k_rope_norm, w_o_mla, ffn_norm, w_gate, w_up,
    w_down, positions_2, mixer_norm_g_2, ffn_norm_g_2, final_norm_g_2, ret_w_in_2, ret_norm_g_2,
    pool_w_2, pool_scale_2, mix_w_out_2, conv_w_pw1_2, conv_b_pw1_2, conv_w_dw_2, conv_b_dw_2,
    conv_ln_g_2, conv_ln_b_2, conv_w_pw2_2, conv_b_pw2_2, ffn_w_gate_2, ffn_w_up_2,
    ffn_w_down_2,
):
    x = first_block(
        x, mix_norm_even, w_in_even, conv_w, conv_b, dt_bias, a_log, d_skip, ssd_norm,
        gla_gk_w2, gla_gk_b, gla_norm, w_out_even, mix_norm_odd, w_dqkv, q_lora_norm, w_uq,
        kv_lora_norm, w_ukv, q_nope_norm, q_rope_norm, k_nope_norm, k_rope_norm, w_o_mla,
        ffn_norm, w_gate, w_up, w_down,
    )
    return second_block(
        x, positions_2, mixer_norm_g_2, ffn_norm_g_2, final_norm_g_2, ret_w_in_2, ret_norm_g_2,
        pool_w_2, pool_scale_2, mix_w_out_2, conv_w_pw1_2, conv_b_pw1_2, conv_w_dw_2,
        conv_b_dw_2, conv_ln_g_2, conv_ln_b_2, conv_w_pw2_2, conv_b_pw2_2, ffn_w_gate_2,
        ffn_w_up_2, ffn_w_down_2,
    )


_drawn_inputs = setup_inputs


def setup_inputs(seed=0):
    import zlib

    import numpy as np

    out = dict(_drawn_inputs(seed))
    spreads = {}
    factors = {'ssd_norm': 3.811,
     'gla_gk_b': 2.731,
     'gla_norm': 6.016,
     'mix_norm_odd': 8.0,
     'q_lora_norm': 8.0,
     'kv_lora_norm': 8.0,
     'q_nope_norm': 8.0,
     'q_rope_norm': 8.0,
     'k_nope_norm': 8.0,
     'k_rope_norm': 8.0,
     'ffn_norm': 2.72,
     'ret_norm_g_2': 31.237,
     'pool_scale_2': 22.693,
     'conv_b_pw1_2': 31.591,
     'conv_b_dw_2': 46.308,
     'conv_ln_g_2': 108.736,
     'conv_ln_b_2': 200.0,
     'conv_b_pw2_2': 200.0,
     'mixer_norm_g_2': 2.877,
     'ffn_norm_g_2': 8.0}
    for name, (base, spread) in spreads.items():
        noise = np.random.default_rng([zlib.crc32(name.encode()), seed]).standard_normal(out[name].shape)
        drawn = base * np.exp(spread * noise) if base else spread * noise
        out[name] = jnp.asarray(drawn.astype(out[name].dtype))
    for name, factor in factors.items():
        out[name] = (out[name] * factor).astype(out[name].dtype)
    return out
```

```python
from contextlib import ExitStack

import numpy as np
import concourse.bass as bass
from concourse import mybir

F32 = mybir.dt.float32
F32R = mybir.dt.float32r
I32 = mybir.dt.int32
U32 = mybir.dt.uint32
ALU = mybir.AluOpType
ACT = mybir.ActivationFunctionType
AX = mybir.AxisListType.X

P = 128
EPS = 1e-6
NR = 3
NH = 3
CH = 2048
SLOTS = 12

COLS = {}
_at = 0
for _name, _n in (("mix_norm_even", 8), ("conv_w", 48), ("conv_b", 12), ("ssd_norm", 8), ("gk_b", 4),
                  ("gla_norm", 2), ("ffn_norm", 16), ("mix_norm_odd", 8), ("q_lora", 3), ("kv_lora", 2),
                  ("qfull", 1), ("kfull", 1), ("mixer_norm_g", 16), ("ffn_norm_g", 16), ("ret_norm", 4),
                  ("pool_scale", 4), ("b_pw1", 16), ("w_dw", 248), ("b_dw", 8), ("ln_g", 8), ("ln_b", 8),
                  ("dt_bias", 16), ("a_log", 16), ("d_skip", 16), ("q_rope_norm", 32), ("k_rope_norm", 32)):
    COLS[_name] = (_at, _n)
    _at += _n
NCOL = _at
C0 = {"ident": (0, 128), "U": (128, 128), "gmask": (256, 128), "reset": (384, 256), "mhalf": (640, 1)}
NC0 = 641
C1 = {"maskadd": (0, 256), "cos": (256, 32), "sin": (288, 32)}
NC1 = 320
C2 = {"rmask": (0, 512), "kdec": (512, 4), "qdec": (516, 4), "invf": (520, 64), "bands": (584, 1536)}
NC2 = 2120


def weight_plan():
    plan = [("w_in_s", 0, 8, 0, 32)]

    def stationary(w, c0, n):
        return [(w, 0, 8, c0 + 256 * j, 256) for j in range(n // 256)]

    def moving(w, c0, n):
        return [(w, 4 * k, 4, c0 + 512 * j, 512) for j in range(n // 512) for k in range(2)]

    def rows(w, n):
        return [(w, 2 * k, 2, 0, 1024) for k in range(n)]

    def ffn(tag):
        out = []
        for j in range(11):
            out += [("gate" + tag, 0, 8, 256 * j, 256), ("up" + tag, 0, 8, 256 * j, 256)]
            if j:
                out.append(("down" + tag, 2 * (j - 1), 2, 0, 1024))
        return out + [("down" + tag, 20, 2, 0, 1024)]

    plan += stationary("w_in", 1024, 1536)
    plan += moving("w_in", 0, 1024)
    plan += moving("w_in", 4624, 1024)
    plan += stationary("w_in", 3088, 512) + stationary("w_in", 2576, 512)
    plan += moving("w_in", 3600, 1024)
    plan += rows("w_out", 8) + ffn("0")
    plan += moving("w_dqkv", 0, 512) + [("w_dqkv", 0, 8, 512, 160)]
    plan += [("w_uq", 0, 3, 512 * j, 512) for j in range(3)]
    plan += [("w_ukv", 0, 2, 1024 * j, 1024) for j in range(2)]
    plan += rows("w_o", 4) + ffn("1")
    plan += moving("ret_w_in", 0, 2560) + rows("mix_w_out", 4) + ffn("2")
    for j in range(4):
        plan += stationary("pw1", 256 * j, 256) + stationary("pw1", 1024 + 256 * j, 256)
    plan += rows("pw2", 4) + ffn("3")
    return plan


PLAN = weight_plan()


class Lane:

    def __init__(self, sem, linked):
        self.sem, self.linked = sem, linked
        self.ops, self.n, self.seen = [], 0, {}

    def wait(self, *toks):
        for t in toks:
            if t is None:
                continue
            if isinstance(t, list):
                self.wait(*t)
                continue
            sem, v = t
            if self.seen.get(id(sem), 0) < v:
                self.seen[id(sem)] = v
                self.ops.append((None, sem, v))

    def quiet(self, fn, *toks):
        self.wait(*toks)
        self.ops.append((fn, None, 0))

    def do(self, fn, *toks):
        self.wait(*toks)
        if self.linked and self.n:
            self.wait((self.sem, self.n))
        self.n += 1
        self.ops.append((fn, self.sem, 1))
        return (self.sem, self.n)

    def emit(self, eng):
        for fn, sem, v in self.ops:
            if fn is None:
                eng.wait_ge(sem, v)
            else:
                i = fn(eng)
                if sem is not None:
                    i.then_inc(sem, v)


def build(nc, d_x, d_ws, d_cols, d_c0, d_c1, d_c2, d_gkw2, d_poolw, d_rows, d_pos, d_out, stop=99):
    ctx = ExitStack()
    with ctx:
        def sb(name, shape, dt=F32):
            return ctx.enter_context(nc.sbuf_tensor(name, shape, dt))

        def sem(name):
            return ctx.enter_context(nc.semaphore(name))

        raw = sb("raw", [P, NR, CH])
        whi = sb("whi", [P, NH, CH], F32R)
        wlo = sb("wlo", [P, NH, CH], F32R)
        ahi = sb("ahi", [P, SLOTS, 256], F32R)
        alo = sb("alo", [P, SLOTS, 256], F32R)
        xt = sb("xt", [P, 2, 1024])
        cols = sb("cols", [P, NCOL])
        c0 = sb("c0", [P, NC0])
        st = sb("st", [P, 256])
        NA = 24700
        arena = sb("arena", [P, NA])
        banks = [ctx.enter_context(nc.psum_tensor(f"pb{i}", [P, 512], F32)) for i in range(8)]

        PE, DV, AC, PO, SP = (Lane(sem("s_pe"), False), Lane(sem("s_dve"), True), Lane(sem("s_act"), True),
                              Lane(sem("s_pool"), True), Lane(None, False))
        s_raw = [sem(f"s_raw{i}") for i in range(NR)]
        dma_sems = iter([sem(f"s_in{i}") for i in range(12)])
        s_out = sem("s_out")

        def load(dst, src, *toks):
            s = next(dma_sems)
            SP.quiet(lambda e: e.dma_start(dst, src).then_inc(s, 16), *toks)
            return (s, 16)

        def col(name, i=0, n=1, parts=P):
            a = COLS[name][0] + i
            return cols[0:parts, a:a + n]

        def cst(name):
            a, n = C0[name]
            return c0[:, a:a + n]

        def tt(out, a, b, op, *w):
            return DV.do(lambda e: e.tensor_tensor(out, a, b, op), *w)

        def ts(out, a, s1, s2, op0, op1, *w):
            if op1 is None:
                return DV.do(lambda e: e.tensor_scalar(out, a, s1, None, op0), *w)
            return DV.do(lambda e: e.tensor_scalar(out, a, s1, s2, op0, op1), *w)

        def stt(out, a, s, b, op0, op1, *w):
            return DV.do(lambda e: e.scalar_tensor_tensor(out=out, in0=a, scalar=s, in1=b, op0=op0, op1=op1), *w)

        def vcopy(out, a, *w):
            return DV.do(lambda e: e.tensor_copy(out, a), *w)

        def act(out, a, func, *w, **kw):
            return AC.do(lambda e: e.activation(out, a, func, **kw), *w)

        def ptt(out, a, b, op, *w):
            return PO.do(lambda e: e.tensor_tensor(out, a, b, op), *w)

        def bc(ap, shape, axis):
            return ap.unsqueeze(axis).to_broadcast(shape)

        def f32(ap):
            return ap.bitcast(F32)

        def cut(ap, a, b=None):
            if b is None:
                return ap.rearrange("p (a b) -> p a b", a=a)
            return ap.rearrange("p (a b c) -> p a b c", a=a, b=b)

        def mm(out, l, r, start, stop, skip=False):
            PE.quiet(lambda e: e.matmul(out, l, r, start=start, stop=stop, skip_group_check=skip))

        def mms(out, l, r, start, stop, skip=False):
            return PE.do(lambda e: e.matmul(out, l, r, start=start, stop=stop, skip_group_check=skip))

        def mm3(out, lh, ll, rh, rl, start, stop):
            mm(out, lh, rh, start, False)
            mm(out, lh, rl, False, False)
            return PE.do(lambda e: e.matmul(out, ll, rh, start=False, stop=stop))

        ident = cst("ident")

        def tr(out, a, sig=False):
            k = a.shape[0]
            f = lambda e: e.transpose(out, a, ident[0:k, 0:k])
            return PE.do(f) if sig else PE.quiet(f)

        free = [[] for _ in range(8)]
        held = set()
        turn = [0]

        def take():
            while turn[0] % 8 in held:
                turn[0] += 1
            b = turn[0] % 8
            turn[0] += 1
            PE.wait(*free[b])
            free[b] = []
            return b

        t_x = [load(xt[:, t, :], d_x[0, t * P:(t + 1) * P, :]) for t in range(2)]
        t_cols = load(cols[:, :], d_cols)
        t_c0 = load(c0[:, :], d_c0)
        for lane in (PE, DV, AC, PO):
            lane.wait(t_c0, t_cols)

        sent = [0]
        split = [0]
        lo_tok, done = {}, {}

        def send(n):
            w = PLAN[n][2] * PLAN[n][4]
            SP.quiet(lambda e: e.dma_start(raw[:, n % NR, 0:w], d_ws[n, :, 0:w]).then_inc(s_raw[n % NR], 16),
                     lo_tok.get(n - NR))

        def split_chunk(n):
            w = PLAN[n][2] * PLAN[n][4]
            r, h, l = raw[:, n % NR, 0:w], whi[:, n % NH, 0:w], wlo[:, n % NH, 0:w]
            arrived = (s_raw[n % NR], 16 * (n // NR + 1))
            t = act(h, r, ACT.Copy, arrived, done.get(n - NH))
            lo_tok[n] = tt(l, r, f32(h), ALU.subtract, arrived, t)

        def ahead(n):
            while split[0] <= min(n, len(PLAN) - 1):
                while sent[0] <= min(split[0] + NR - 1, len(PLAN) - 1):
                    send(sent[0])
                    sent[0] += 1
                split_chunk(split[0])
                split[0] += 1

        used = [0]

        def chunk():
            n = used[0]
            used[0] += 1
            ahead(n + NH - 1)
            PE.wait(lo_tok[n])
            w = PLAN[n][2] * PLAN[n][4]
            k = PLAN[n][2]
            return n, cut(whi[:, n % NH, 0:w], k), cut(wlo[:, n % NH, 0:w], k)

        slot_ready = [None] * SLOTS
        slot_free = [[] for _ in range(SLOTS)]

        def rstd(ap, width, *w):
            PO.do(lambda e: e.tensor_scalar(ap, ap, 1.0 / width, EPS, ALU.mult, ALU.add), *w)
            n = ap.shape[1]
            return ptt(ap, ap, cst("mhalf").to_broadcast([P, n]), ALU.pow)

        def fill_slots(parts, *w):
            for s, src, gain in parts:
                kw = {} if gain is None else {"scale": gain}
                t_hi = act(ahi[:, s, :], src, ACT.Copy, slot_free[s], *w, **kw)
            for s, src, gain in parts:
                h, l = f32(ahi[:, s, :]), alo[:, s, :]
                if gain is None:
                    t_lo = tt(l, src, h, ALU.subtract, t_hi)
                else:
                    t_lo = stt(l, src, gain, h, ALU.mult, ALU.subtract, t_hi)
                slot_free[s] = []
                slot_ready[s] = t_lo
            return t_lo

        def turn_to_slot(srcs, gains, slots, *w):
            for j in range(0, len(slots), 2):
                b = take()
                PE.wait(*w)
                m = min(2, len(slots) - j)
                for i in range(m):
                    for t in range(2):
                        k = tr(banks[b][:, 256 * i + 128 * t:256 * i + 128 * t + 128], srcs(t, j + i),
                               sig=(i == m - 1 and t == 1))
                free[b] = [fill_slots([(slots[j + i], banks[b][:, 256 * i:256 * i + 256], gains(j + i))
                                       for i in range(m)], k)]

        def norm_x(gname, g0, xn):
            a = act(xn[:, 0, :], xt[:, 0, :], ACT.Square, t_x[0], accum_out=st[:, 0:1])
            b = DV.do(lambda e: e.tensor_tensor_reduce(xn[:, 1, :], xt[:, 1, :], xt[:, 1, :], 1.0, 0.0,
                                                       ALU.mult, ALU.add, st[:, 1:2]), t_x[1])
            r = rstd(st[:, 0:2], 1024, a, b)
            na = act(xn[:, 0, :], xt[:, 0, :], ACT.Copy, r, scale=st[:, 0:1])
            nb = ts(xn[:, 1, :], xt[:, 1, :], st[:, 1:2], None, ALU.mult, None, r)
            turn_to_slot(lambda t, j: xn[:, t, 128 * j:128 * j + 128], lambda j: col(gname, g0 + j),
                         list(range(8)), na, nb)

        def project_moving(ncols):
            bs = [take(), take()]
            k0, n_chunks = 0, 0
            while k0 < 8:
                n, wh, wl = chunk()
                kk = PLAN[n][2]
                for k in range(kk):
                    PE.wait(slot_ready[k0 + k])
                    for t in range(2):
                        t_done = mm3(banks[bs[t]][:, 0:ncols], ahi[:, k0 + k, 128 * t:128 * t + 128],
                                     alo[:, k0 + k, 128 * t:128 * t + 128], wh[:, k, :], wl[:, k, :],
                                     k0 + k == 0, k0 + k == 7)
                    slot_free[k0 + k] = [t_done]
                done[n] = t_done
                k0 += kk
            return bs, t_done

        def project_stationary():
            b = take()
            n, wh, wl = chunk()
            for i in range(2):
                for k in range(8):
                    PE.wait(slot_ready[k])
                    t_done = mm3(banks[b][:, 256 * i:256 * i + 256], wh[:, k, 128 * i:128 * i + 128],
                                 wl[:, k, 128 * i:128 * i + 128], ahi[:, k, :], alo[:, k, :], k == 0, k == 7)
                    slot_free[k] = [t_done]
            done[n] = t_done
            return b, t_done

        def open_out():
            bs = [take() for _ in range(4)]
            held.update(bs)
            return bs

        def rows_out(bs, slots, first, last):
            n, wh, wl = chunk()
            for k, s in enumerate(slots):
                PE.wait(slot_ready[s])
                for t in range(2):
                    for c in range(2):
                        f, l = first and k == 0, last and k == len(slots) - 1
                        t_done = mm3(banks[bs[2 * t + c]][:, :], ahi[:, s, 128 * t:128 * t + 128],
                                     alo[:, s, 128 * t:128 * t + 128], wh[:, k, 512 * c:512 * c + 512],
                                     wl[:, k, 512 * c:512 * c + 512], f, l)
                slot_free[s] = [t_done]
            done[n] = t_done
            return t_done

        def close_out(bs, t_done):
            for t in range(2):
                for c in range(2):
                    v = xt[:, t, 512 * c:512 * c + 512]
                    k = tt(v, v, banks[bs[2 * t + c]][:, :], ALU.add, t_done)
                    free[bs[2 * t + c]] = [k]
                t_x[t] = k
            held.difference_update(bs)

        def ffn(gname, g0):
            norm_x(gname, g0, cut(arena[:, 0:2048], 2))
            sg = cut(arena[:, 2048:3072], 2)
            hh = cut(arena[:, 3072:4096], 2)
            hf = [None, None]
            bs = open_out()
            for j in range(12):
                if j < 11:
                    bg, tg = project_stationary()
                    bu, tu = project_stationary()
                    a = act(sg[:, j % 2, :], banks[bg][:, :], ACT.Silu, tg, hf[j % 2])
                    free[bg] = [a]
                    h = tt(hh[:, j % 2, :], sg[:, j % 2, :], banks[bu][:, :], ALU.mult, a, tu)
                    free[bu] = [h]
                    hf[j % 2] = fill_slots([(8 + (2 * j + i) % 4, hh[:, j % 2, 256 * i:256 * i + 256], None)
                                            for i in range(2)], h)
                if j:
                    s = 8 + (2 * (j - 1)) % 4
                    t_done = rows_out(bs, [s, s + 1], j == 1, j == 11)
            close_out(bs, t_done)

        class Room:
            def __init__(self):
                self.at = 0

            def __call__(self, n, *shape):
                a = arena[:, self.at:self.at + n]
                self.at += n
                assert self.at <= NA, self.at
                return cut(a, *shape) if shape else a

        def ssd_gla():
            room = Room()
            xbc = room(12 * 259, 12)
            xs = room(2048, 2)
            bt = room(256, 2)
            zs, gs, v = room(2048, 2), room(2048, 2), room(2048, 2)
            q, k, X, U_ = (room(1024) for _ in range(4))
            kend = room(1024, 2)
            S = room(1536, 2, 3)
            sT = room(1024)
            xdte = room(1024)
            M = room(1536, 3)
            pv = room(1024, 2)
            acc = room(512, 2)
            small = room(32 * 14)
            w2 = room(512)
            t_w2 = load(w2[0:16, :], d_gkw2)
            xn = cut(arena[:, 12 * 259 + 2304:12 * 259 + 4352], 2)
            norm_x("mix_norm_even", 0, xn)
            UM = cst("U")
            sm = [small[:, 32 * i:32 * i + 32] for i in range(14)]
            dtr, nabs, u, w1, lw, dm, e0, dt, a_, ea, acol, eac = sm[:12]
            gl = sm[12]
            dec = sm[13]
            z_pad = DV.do(lambda e: e.memset(xbc[:, :, 0:3], 0.0), t_x[0])
            z_sT = DV.do(lambda e: e.memset(sT[:, :], 0.0))
            w_xn = PE.n

            b0, b1 = take(), take()
            n, wh, wl = chunk()
            for t, b in enumerate((b0, b1)):
                for kk in range(8):
                    PE.wait(slot_ready[kk])
                    t_done = mm3(banks[b][:, 0:32], ahi[:, kk, 128 * t:128 * t + 128],
                                 alo[:, kk, 128 * t:128 * t + 128], wh[:, kk, :], wl[:, kk, :], kk == 0, kk == 7)
            done[n] = t_done
            for t, b in enumerate((b0, b1)):
                tt(dtr[:, 16 * t:16 * t + 16], banks[b][:, 0:16], col("dt_bias", 0, 16), ALU.add, t_done)
                o = vcopy(gl[:, 16 * t:16 * t + 16], banks[b][:, 16:32])
                free[b] = [o]
            b = take()
            PE.wait(o)
            for t in range(2):
                ti = tr(banks[b][0:16, 128 * t:128 * t + 128], gl[:, 16 * t:16 * t + 16], sig=True)
            glT = acc[0:16, 0, :]
            t_gl = vcopy(glT, banks[b][0:16, 0:256], ti)
            free[b] = [t_gl]
            stt(nabs, dtr, -1.0, dtr, ALU.mult, ALU.min)
            eu = act(u, nabs, ACT.Exp, (DV.sem, DV.n))
            t_ea = act(ea[:, 0:16], col("a_log", 0, 16), ACT.Exp)
            t1 = ts(w1, u, 1.0, None, ALU.add, None, eu)
            t2 = act(lw, w1, ACT.Ln, t1)
            ts(dm, w1, 1.0, None, ALU.subtract, None)
            ts(e0, dm, 0.0, None, ALU.is_equal, None)
            tt(dm, dm, e0, ALU.add)
            DV.do(lambda e: e.reciprocal(dm, dm))
            tt(lw, lw, e0, ALU.add, t2)
            tt(lw, lw, u, ALU.mult)
            tt(lw, lw, dm, ALU.mult)
            stt(dt, dtr, 0.0, lw, ALU.max, ALU.add)
            t_a = stt(cut(a_, 2), cut(dt, 2), -1.0, bc(ea[:, 0:16], [P, 2, 16], 1), ALU.mult, ALU.mult, t_ea)
            gb = [take(), take()]
            PE.wait(t_gl, t_w2)
            for h in range(4):
                t_g = mms(banks[gb[h // 2]][:, 256 * (h % 2):256 * (h % 2) + 256], w2[0:16, 128 * h:128 * h + 128],
                          glT, True, True)
            for h in range(4):
                o = ts(X[:, 256 * h:256 * h + 256], banks[gb[h // 2]][:, 256 * (h % 2):256 * (h % 2) + 256],
                       col("gk_b", h), None, ALU.add, None, t_g)
                free[gb[h // 2]] = [o]
            o = stt(U_, X, -1.0, X, ALU.mult, ALU.min)
            o = act(U_, U_, ACT.Exp, o)
            o = ts(U_, U_, 1.0, None, ALU.add, None, o)
            o = act(U_, U_, ACT.Ln, o)
            ts(X, X, 0.0, None, ALU.min, None)
            tt(U_, X, U_, ALU.subtract, o)
            for h in range(4):
                hs = slice(256 * h, 256 * h + 256)
                t_cum = DV.do(lambda e, hs=hs: e.tensor_tensor_scan(X[:, hs], cst("reset"), U_[:, hs], 0.0,
                                                                    ALU.mult, ALU.add))
            b = take()
            PE.wait(t_a)
            ta = mms(banks[b][:, 0:32], UM, a_, True, True)
            t_acol = vcopy(acol, banks[b][:, 0:32], ta)
            free[b] = [t_acol]
            t_eac = act(eac, acol, ACT.Exp, t_acol)
            for j in range(6):
                b, td = project_stationary()
                for i in range(2):
                    ft = 2 * j + i
                    o = act(xbc[:, ft, 3:259], banks[b][:, 256 * i:256 * i + 256], ACT.Copy, td, z_pad)
                    free[b] = [o]
                    ac = acc[:, i, :]
                    c = ts(ac, xbc[:, ft, 0:256], col("conv_w", ft), col("conv_b", ft), ALU.mult, ALU.add, o, t_g)
                    for w in range(1, 4):
                        c = stt(ac, xbc[:, ft, w:w + 256], col("conv_w", 12 * w + ft), ac, ALU.mult, ALU.add)
                    t_conv = act(xbc[:, ft, 3:259], ac, ACT.Silu, c)
            DV.wait(t_conv)
            for dst in (zs, gs):
                for c in range(2):
                    bs, td = project_moving(512)
                    for t in range(2):
                        o = act(dst[:, t, 512 * c:512 * c + 512], banks[bs[t]][:, :], ACT.Silu, td,
                                (PE.sem, PE.n))
                        free[bs[t]] = [o]
            t_zg = o
            for t in range(2):
                for c in range(2):
                    b = take()
                    PE.wait(t_conv)
                    for i in range(4):
                        k_ = tr(banks[b][:, 128 * i:128 * i + 128], xbc[:, 4 * c + i, 3 + 128 * t:131 + 128 * t],
                                sig=(i == 3))
                    o = vcopy(xs[:, t, 512 * c:512 * c + 512], banks[b][:, :], k_)
                    free[b] = [o]
            b = take()
            for g in range(2):
                k_ = tr(banks[b][:, 128 * g:128 * g + 128], xbc[:, 8 + g, 3:131], sig=True)
            t_bt = vcopy(bt[:, :, :], cut(banks[b][:, 0:256], 2), k_)
            free[b] = [t_bt]
            xdt = cut(arena[:, 0:2048], 2)
            for t in range(2):
                t_xdt = tt(cut(xdt[:, t, :], 16), cut(xs[:, t, :], 16),
                           bc(dt[:, 16 * t:16 * t + 16], [P, 16, 64], 2), ALU.mult, k_)
            for t in range(2):
                tt(cut(xs[:, t, :], 16), cut(xs[:, t, :], 16), bc(col("d_skip", 0, 16), [P, 16, 64], 2), ALU.mult)
            for dst in (k, q):
                for j in range(2):
                    b, td = project_stationary()
                    o = act(dst[:, 512 * j:512 * j + 512], banks[b][:, :], ACT.Copy, td)
                    free[b] = [o]
            t_kq = o
            cbm = kend
            t_m = [None] * 3
            mi = 0
            t_cb_free = None
            t_yo = {}
            for c in range(2):
                for g in range(2):
                    b = take()
                    cs = slice(3 + 128 * c, 131 + 128 * c)
                    tc = mms(banks[b][:, 0:128], xbc[:, 8 + g, cs], xbc[:, 10 + g, cs], True, True)
                    cb = cbm[:, 0, 0:128]
                    t_cb = tt(cb, banks[b][:, 0:128], UM, ALU.mult, tc)
                    free[b] = [t_cb]
                    by = take()
                    held.add(by)
                    for hh in range(2):
                        b = take()
                        PE.wait(t_a)
                        for i in range(4):
                            h = 16 * c + 8 * g + 4 * hh + i
                            tb = mms(banks[b][:, 128 * i:128 * i + 128], a_[:, h:h + 1].to_broadcast([P, P]), UM,
                                     True, True)
                        m = M[:, mi % 3, :]
                        for i in range(4):
                            h = 16 * c + 8 * g + 4 * hh + i
                            o = ts(m[:, 128 * i:128 * i + 128], banks[b][:, 128 * i:128 * i + 128],
                                   acol[:, h:h + 1], 0.0, ALU.subtract, ALU.min, tb, t_m[mi % 3])
                        free[b] = [o]
                        o = act(m, m, ACT.Exp, o)
                        if c == 0:
                            tt(cut(xdte[:, 512 * g + 256 * hh:512 * g + 256 * hh + 256], 4),
                               cut(xdt[:, 0, 512 * g + 256 * hh:512 * g + 256 * hh + 256], 4),
                               cut(m, 4)[:, :, 127:128].to_broadcast([P, 4, 64]), ALU.mult, o)
                        o = tt(cut(m, 4), cut(m, 4), bc(cb, [P, 4, 128], 1), ALU.mult, o)
                        PE.wait(o, t_xdt)
                        for i in range(4):
                            h = 8 * g + 4 * hh + i
                            ty = mms(banks[by][:, 64 * (4 * hh + i):64 * (4 * hh + i) + 64],
                                     m[:, 128 * i:128 * i + 128], xdt[:, c, 64 * h:64 * h + 64], True, True)
                        t_m[mi % 3] = ty
                        mi += 1
                    gsl = slice(512 * g, 512 * g + 512)
                    if c == 0:
                        b = take()
                        PE.wait((DV.sem, DV.n), t_bt)
                        tp = mms(banks[b][:, :], bt[:, g, :], xdte[:, gsl], True, True)
                        t_pv = act(pv[:, g, :], banks[b][:, :], ACT.Copy, tp)
                        free[b] = [t_pv]
                    else:
                        b = take()
                        PE.wait(t_pv)
                        to = mms(banks[b][:, :], xbc[:, 10 + g, cs], pv[:, g, :], True, True)
                        tmp = xdte[:, gsl]
                        o = tt(cut(tmp, 8), cut(banks[b][:, :], 8),
                               bc(eac[:, 16 + 8 * g:24 + 8 * g], [P, 8, 64], 2), ALU.mult, to, t_eac, t_pv)
                        free[b] = [o]
                        tt(xs[:, 1, gsl], xs[:, 1, gsl], tmp, ALU.add)
                    o = tt(xs[:, c, gsl], xs[:, c, gsl], banks[by][:, :], ALU.add, ty)
                    free[by] = [o]
                    held.discard(by)
                    o = tt(zs[:, c, gsl], zs[:, c, gsl], xs[:, c, gsl], ALU.mult, t_zg)
                    t_ss = act(xs[:, c, gsl], zs[:, c, gsl], ACT.Square, o,
                               accum_out=st[:, 2 + 2 * c + g:3 + 2 * c + g])
            r = rstd(st[:, 2:6], 512, t_ss)
            for c in range(2):
                for g in range(2):
                    gsl = slice(512 * g, 512 * g + 512)
                    t_y = ts(zs[:, c, gsl], zs[:, c, gsl], st[:, 2 + 2 * c + g:3 + 2 * c + g], None, ALU.mult,
                             None, r)
            for c in range(2):
                bs, td = project_moving(512)
                for t in range(2):
                    o = act(v[:, t, 512 * c:512 * c + 512], banks[bs[t]][:, :], ACT.Copy, td)
                    free[bs[t]] = [o]
            t_v = o
            e1 = act(U_, X, ACT.Exp, t_cum, scale=1.0 / 16)
            vcopy(dec[:, 0:16], cut(U_, 16)[:, :, 63], e1)
            t_q = stt(q, q, 128.0 ** -0.5, U_, ALU.mult, ALU.mult, t_kq)
            o = tt(cut(U_, 16), cut(X, 16)[:, :, 63:64].to_broadcast([P, 16, 64]), cut(X, 16), ALU.subtract)
            e3 = act(U_, U_, ACT.Exp, o, scale=1.0 / 16)
            e2 = act(X, X, ACT.Exp, o, scale=-1.0 / 16)
            t_ke = tt(U_, U_, k, ALU.mult, e3)
            t_k = tt(k, k, X, ALU.mult, e2)
            for t in range(2):
                b = take()
                PE.wait(t_ke)
                for h in range(4):
                    k_ = tr(banks[b][:, 128 * h:128 * h + 128], U_[:, 256 * h + 128 * t:256 * h + 128 * t + 128],
                            sig=(h == 3))
                t_kt = act(kend[:, t, :], banks[b][:, :], ACT.Copy, k_, t_cb)
                free[b] = [t_kt]
            gm = cst("gmask").bitcast(U32)
            for t in range(2):
                b = take()
                PE.wait(t_k, t_q)
                for h in range(4):
                    sl = slice(256 * h + 128 * t, 256 * h + 128 * t + 128)
                    ti = mms(banks[b][:, 128 * h:128 * h + 128], k[:, sl], q[:, sl], True, True)
                for h in range(4):
                    t_s = DV.do(lambda e, b=b, h=h, t=t: e.copy_predicated(
                        sT[:, 512 * t + 128 * h:512 * t + 128 * h + 128], gm, banks[b][:, 128 * h:128 * h + 128]),
                        ti, z_sT)
                free[b] = [t_s]
            for h in range(4):
                vs = slice(256 * h, 256 * h + 256)
                bb = [take(), take()]
                PE.wait(t_kt, t_v)
                for c in (0, 2, 1):
                    rows = slice(64 * (c % 2), 64 * (c % 2) + 64)
                    tk = mms(banks[bb[c % 2]][:, 256 * (c // 2):256 * (c // 2) + 256],
                             kend[rows, c // 2, 128 * h:128 * h + 128], v[rows, c // 2, vs], True, True)
                s_ = S[:, h % 2]
                vcopy(s_[:, 0, :], banks[bb[0]][:, 0:256], tk, t_s if h < 2 else t_o[h - 2])
                stt(s_[:, 1, :], s_[:, 0, :], dec[:, 4 * h + 1:4 * h + 2], banks[bb[1]][:, 0:256], ALU.mult, ALU.add)
                t_S = stt(s_[:, 2, :], s_[:, 1, :], dec[:, 4 * h + 2:4 * h + 3], banks[bb[0]][:, 256:512],
                          ALU.mult, ALU.add)
                free[bb[0]], free[bb[1]] = [t_S], [t_S]
                if h == 0:
                    t_o = []
                b = take()
                PE.wait(t_S)
                for t in range(2):
                    out = banks[b][:, 256 * t:256 * t + 256]
                    mm(out, sT[:, 512 * t + 128 * h:512 * t + 128 * h + 128], v[:, t, vs], True, True, True)
                    for c in (2 * t, 2 * t + 1):
                        if c == 0:
                            continue
                        r0 = 64 * (c % 2)
                        to = mms(banks[b][r0:r0 + 64, 256 * t:256 * t + 256],
                                 q[:, 256 * h + 64 * c:256 * h + 64 * c + 64], s_[:, c - 1, :], False, True, True)
                t_o.append(to)
                for t in range(2):
                    i = 6 + 2 * h + t
                    a2 = act(X[:, 0:256], banks[b][:, 256 * t:256 * t + 256], ACT.Square, to, t_k,
                             accum_out=st[:, i:i + 1])
                r = rstd(st[:, 6 + 2 * h:8 + 2 * h], 256, a2)
                for t in range(2):
                    i = 6 + 2 * h + t
                    t_yg = stt(gs[:, t, vs], banks[b][:, 256 * t:256 * t + 256], st[:, i:i + 1], gs[:, t, vs],
                               ALU.mult, ALU.mult, r)
                free[b] = [t_yg]
            bs = open_out()
            for j in range(8):
                src, base = (zs, 0) if j < 4 else (gs, 8)
                slots = [(8 + 2 * j) % 12, (9 + 2 * j) % 12]
                turn_to_slot(lambda t, i, j=j, src=src, base=base:
                             src[:, t, 128 * (2 * j + i - base):128 * (2 * j + i - base) + 128],
                             lambda i, j=j: col("ssd_norm", 2 * j + i) if j < 4 else col("gla_norm", i),
                             slots, t_yg)
                td = rows_out(bs, slots, j == 0, j == 7)
            close_out(bs, td)

        def mla():
            room = Room()
            c1 = room(NC1)
            cq = room(1344, 2)
            qt = room(3072, 2, 16)
            kf = room(3072, 2, 16)
            v = room(2048, 2)
            o_ = room(2048, 2)
            sq = o_
            sqq = room(1536)
            qT = room(4096, 16)
            kT = room(4096, 16)
            Sb = [room(512) for _ in range(2)]
            PT = [room(512) for _ in range(2)]
            stats = room(32 * 4)
            kr = room(64, 2)
            rt = Sb
            t_c1 = load(c1[:, :], d_c1, t_x)
            maskadd = c1[:, 0:256]
            cos, sin = cut(c1[:, 256:288], 2), cut(c1[:, 288:320], 2)
            norm_x("mix_norm_odd", 0, o_)
            for c, n in ((0, 512), (512, 160)):
                bs, td = project_moving(n)
                for t in range(2):
                    o = act(cq[:, t, c:c + n], banks[bs[t]][:, 0:n], ACT.Copy, td)
                    free[bs[t]] = [o]
            a_ = None
            for t in range(2):
                for i, (lo, hi) in enumerate(((0, 384), (384, 640))):
                    a_ = act(sqq[:, 0:hi - lo], cq[:, t, lo:hi], ACT.Square,
                             accum_out=st[:, 2 + 2 * i + t:3 + 2 * i + t])
                b_ = act(sqq[:, 0:32], cq[:, t, 640:672], ACT.Square, accum_out=st[:, 6 + t:7 + t])
            rstd(st[:, 2:4], 384, b_)
            rstd(st[:, 4:6], 256)
            r = rstd(st[:, 6:8], 32)
            for t in range(2):
                ts(cq[:, t, 0:384], cq[:, t, 0:384], st[:, 2 + t:3 + t], None, ALU.mult, None, r)
                n_ = ts(cq[:, t, 384:640], cq[:, t, 384:640], st[:, 4 + t:5 + t], None, ALU.mult, None)
                stt(kr[:, t, :], cq[:, t, 640:672], st[:, 6 + t:7 + t], col("k_rope_norm", 0, 32), ALU.mult,
                    ALU.mult)
            sl5 = [8, 9, 10, 11, 0]
            turn_to_slot(lambda t, j: cq[:, t, 128 * j:128 * j + 128],
                         lambda j: col("q_lora", j) if j < 3 else col("kv_lora", j - 3), sl5, n_)
            for c in range(3):
                n, wh, wl = chunk()
                bs = [take(), take()]
                for t in range(2):
                    for k_ in range(3):
                        PE.wait(slot_ready[sl5[k_]])
                        td = mm3(banks[bs[t]][:, :], ahi[:, sl5[k_], 128 * t:128 * t + 128],
                                 alo[:, sl5[k_], 128 * t:128 * t + 128], wh[:, k_, :], wl[:, k_, :], k_ == 0,
                                 k_ == 2)
                        slot_free[sl5[k_]] = [td]
                done[n] = td
                for t in range(2):
                    flat = qt[:, t].rearrange("p a b -> p (a b)")
                    t_q = act(flat[:, 512 * c:512 * c + 512], banks[bs[t]][:, :], ACT.Copy, td)
                    free[bs[t]] = [t_q]
            t_kk = None
            for c in range(2):
                n, wh, wl = chunk()
                for hc in range(2):
                    bs = [take(), take()]
                    for t in range(2):
                        for k_ in range(2):
                            s = sl5[3 + k_]
                            PE.wait(slot_ready[s])
                            td = mm3(banks[bs[t]][:, :], ahi[:, s, 128 * t:128 * t + 128],
                                     alo[:, s, 128 * t:128 * t + 128], wh[:, k_, 512 * hc:512 * hc + 512],
                                     wl[:, k_, 512 * hc:512 * hc + 512], k_ == 0, k_ == 1)
                            slot_free[s] = [td]
                    for t in range(2):
                        h0 = 8 * c + 4 * hc
                        pb = cut(banks[bs[t]][:, :], 4)
                        o1 = act(kf[:, t, h0:h0 + 4, 0:64], pb[:, :, 0:64], ACT.Copy, td)
                        t_v = vcopy(cut(v[:, t, 64 * h0:64 * h0 + 256], 4), pb[:, :, 64:128], td, o1)
                        free[bs[t]] = [t_v]
                        t_kk = o1
                done[n] = td
            for t in range(2):
                s3 = cut(sqq, 16)
                tt(s3, qt[:, t], qt[:, t], ALU.mult, t_q)
                DV.do(lambda e, s3=s3, t=t: e.tensor_reduce(stats[:, 16 * t:16 * t + 16], s3[:, :, 0:64], AX, ALU.add))
                DV.do(lambda e, s3=s3, t=t: e.tensor_reduce(stats[:, 64 + 16 * t:80 + 16 * t], s3[:, :, 64:96], AX,
                                                            ALU.add))
                s4 = cut(sqq[:, 0:1024], 16)
                tt(s4, kf[:, t, :, 0:64], kf[:, t, :, 0:64], ALU.mult, t_kk)
                DV.do(lambda e, s4=s4, t=t: e.tensor_reduce(stats[:, 32 + 16 * t:48 + 16 * t], s4, AX, ALU.add))
            rstd(stats[:, 0:64], 64, (DV.sem, DV.n))
            r = rstd(stats[:, 64:96], 32)
            for t in range(2):
                tt(kf[:, t, :, 0:64], kf[:, t, :, 0:64], bc(stats[:, 32 + 16 * t:48 + 16 * t], [P, 16, 64], 2),
                   ALU.mult, r)
                tt(qt[:, t, :, 0:64], qt[:, t, :, 0:64], bc(stats[:, 16 * t:16 * t + 16], [P, 16, 64], 2), ALU.mult)
                tt(qt[:, t, :, 64:96], qt[:, t, :, 64:96], bc(stats[:, 64 + 16 * t:80 + 16 * t], [P, 16, 32], 2),
                   ALU.mult)
                tt(qt[:, t, :, 64:96], qt[:, t, :, 64:96], bc(col("q_rope_norm", 0, 32), [P, 16, 32], 1), ALU.mult)
            DV.wait(t_c1)
            for t in range(2):
                x1, x2 = qt[:, t, :, 64:80], qt[:, t, :, 80:96]
                cb, sb_ = bc(cos[:, t, :], [P, 16, 16], 1), bc(sin[:, t, :], [P, 16, 16], 1)
                ra, rb = cut(rt[0][:, 0:256], 16), cut(rt[1][:, 0:256], 16)
                tt(ra, x2, sb_, ALU.mult)
                tt(rb, x1, sb_, ALU.mult)
                tt(x1, x1, cb, ALU.mult)
                tt(x1, x1, ra, ALU.subtract)
                tt(x2, x2, cb, ALU.mult)
                tt(x2, x2, rb, ALU.add)
            x1, x2 = kr[:, :, 0:16], kr[:, :, 16:32]
            ra, rb = cut(rt[0][:, 0:32], 2), cut(rt[1][:, 0:32], 2)
            tt(ra, x2, sin, ALU.mult)
            tt(rb, x1, sin, ALU.mult)
            tt(x1, x1, cos, ALU.mult)
            tt(x1, x1, ra, ALU.subtract)
            tt(x2, x2, cos, ALU.mult)
            tt(x2, x2, rb, ALU.add)
            for t in range(2):
                t_r = vcopy(kf[:, t, :, 64:96], bc(kr[:, t, :], [P, 16, 32], 1))
            for src, dst, g in ((qt, qT, "qfull"), (kf, kT, "kfull")):
                for hp in range(8):
                    b = take()
                    PE.wait(t_r)
                    for i in range(2):
                        for t in range(2):
                            k_ = tr(banks[b][0:96, 256 * i + 128 * t:256 * i + 128 * t + 128],
                                    src[:, t, 2 * hp + i, :], sig=(i == 1 and t == 1))
                    o = dst[0:96, 2 * hp:2 * hp + 2, :]
                    pb = cut(banks[b][0:96, :], 2)
                    if hp % 2:
                        t_T1 = act(o, pb, ACT.Copy, k_, scale=col(g, 0, 1, 96))
                        free[b] = [t_T1]
                    else:
                        t_T2 = ts(o, pb, col(g, 0, 1, 96), None, ALU.mult, None, k_)
                        free[b] = [t_T2]
            sc = 96.0 ** -0.5
            mx, sums = stats[:, 0:32], stats[:, 32:64]
            bo = {}
            t_pt = [None, None]
            rounds = [(0, 4 * i, 4) for i in range(4)] + [(1, 2 * i, 2) for i in range(8)]
            t_sb = [None, None]

            def attend(i):
                t, h0, nh = rounds[i]
                nk = 128 * (t + 1)
                b = take()
                PE.wait(t_T1, t_T2)
                for h in range(nh):
                    ti = mms(banks[b][:, nk * h:nk * h + nk], qT[0:96, h0 + h, 128 * t:128 * t + 128],
                             kT[0:96, h0 + h, 0:nk], True, True)
                S_ = Sb[i % 2]
                o = tt(cut(S_, nh), cut(banks[b][:, :], nh), bc(maskadd[:, 256 - nk:256], [P, nh, nk], 1), ALU.add,
                       ti, t_sb[i % 2], t_c1)
                free[b] = [o]
                m = mx[:, 16 * t + h0:16 * t + h0 + nh]
                DV.do(lambda e: e.tensor_reduce(m, cut(S_, nh), AX, ALU.max))
                o = ts(m, m, -sc, None, ALU.mult, None)
                for h in range(nh):
                    c = 16 * t + h0 + h
                    o = act(S_[:, nk * h:nk * h + nk], S_[:, nk * h:nk * h + nk], ACT.Exp, o,
                            bias=mx[:, c:c + 1], scale=sc, accum_out=sums[:, c:c + 1])
                return o

            def mix(i, t_e):
                t, h0, nh = rounds[i]
                nk = 128 * (t + 1)
                b = take()
                PE.wait(t_e)
                for j in range(4):
                    k_ = tr(banks[b][:, 128 * j:128 * j + 128], Sb[i % 2][:, 128 * j:128 * j + 128], sig=(j == 3))
                t_sb[i % 2] = k_
                if i % 2:
                    o = vcopy(PT[i % 2], banks[b][:, :], k_, t_pt[i % 2])
                else:
                    o = act(PT[i % 2], banks[b][:, :], ACT.Copy, k_, t_pt[i % 2])
                free[b] = [o]
                if (t, h0 // 8) not in bo:
                    bo[(t, h0 // 8)] = take()
                    held.add(bo[(t, h0 // 8)])
                ob = banks[bo[(t, h0 // 8)]]
                PE.wait(o, t_v)
                for h in range(nh):
                    hh = (h0 + h) % 8
                    for kt in range(t + 1):
                        j = h * (t + 1) + kt
                        to = mms(ob[:, 64 * hh:64 * hh + 64], PT[i % 2][:, 128 * j:128 * j + 128],
                                 v[:, kt, 64 * (h0 + h):64 * (h0 + h) + 64], kt == 0, kt == t)
                t_pt[i % 2] = to
                if (h0 + nh) % 8 == 0:
                    g = h0 // 8
                    c = 16 * t + 8 * g
                    DV.do(lambda e: e.reciprocal(sums[:, c:c + 8], sums[:, c:c + 8]), to)
                    o = tt(cut(o_[:, t, 512 * g:512 * g + 512], 8), cut(ob[:, :], 8),
                           bc(sums[:, c:c + 8], [P, 8, 64], 2), ALU.mult)
                    free[bo[(t, g)]] = [o]
                    held.discard(bo[(t, g)])
                    return o

            prev = attend(0)
            for i in range(12):
                nxt = attend(i + 1) if i < 11 else None
                t_on = mix(i, prev) or t_kk
                prev = nxt
            bs = open_out()
            for j in range(4):
                slots = [8 + (2 * j) % 4, 9 + (2 * j) % 4]
                turn_to_slot(lambda t, i, j=j: o_[:, t, 128 * (2 * j + i):128 * (2 * j + i) + 128],
                             lambda i: None, slots, t_on)
                td = rows_out(bs, slots, j == 0, j == 3)
            close_out(bs, td)

        def ret_pool():
            room = Room()
            c2 = room(NC2)
            xn = room(2048, 2)
            q, k, v, g, u, tq, tk = (room(1024, 2) for _ in range(7))
            qT, kT = room(1024, 4), room(1024, 4)
            Ms = room(1024, 2)
            kd, sta = room(512), room(512)
            tmp = room(512)
            pw = room(512)
            yT = room(1024, 4)
            cs, sn = room(128, 2), room(128, 2)
            ang, kk = room(128), room(128)
            ps = room(4)
            bst = room(48)
            mv = room(16)
            t_c2 = load(c2[:, :], d_c2, t_x)
            t_pw = load(pw, d_poolw, t_x)
            pi = ps[:, 0:2].bitcast(I32)
            t_ps = load(pi, d_pos, t_x)

            def c2s(name):
                a, n = C2[name]
                return c2[:, a:a + n]

            norm_x("mixer_norm_g", 0, xn)
            DV.wait(t_c2, t_ps)
            vcopy(ps[:, 2:4], pi)
            for t in range(2):
                ts(ang[:, 64 * t:64 * t + 64], c2s("invf"), ps[:, 2 + t:3 + t], None, ALU.mult, None)
            big = 12582912.0
            p1, p2 = 6.28125, 0.0019340515136718750
            p3 = 2 * np.pi - p1 - p2
            for off, dst in ((0.0, sn), (0.25, cs)):
                fl = dst.rearrange("p a b -> p (a b)")
                ts(kk, ang, 1 / (2 * np.pi), off, ALU.mult, ALU.add)
                ts(kk, kk, big, None, ALU.add, None)
                ts(kk, kk, big, None, ALU.subtract, None)
                stt(fl, kk, -p1, ang, ALU.mult, ALU.add)
                stt(fl, kk, -p2, fl, ALU.mult, ALU.add)
                stt(fl, kk, -p3, fl, ALU.mult, ALU.add)
                ts(fl, fl, off * 2 * np.pi, None, ALU.add, None)
                o = ts(fl, fl, 3.1415925, -3.1415925, ALU.min, ALU.max)
                t_sc = act(fl, fl, ACT.Sin, o)
            for dst, f in ((q, ACT.Copy), (k, ACT.Copy), (v, ACT.Copy), (g, ACT.Silu), (u, ACT.Copy)):
                bs, td = project_moving(512)
                for t in range(2):
                    o = act(dst[:, t, :], banks[bs[t]][:, :], f, td)
                    free[bs[t]] = [o]
                if dst is q or dst is k:
                    rot = tq if dst is q else tk
                    for t in range(2):
                        s4, r4 = cut(dst[:, t, :], 4), cut(rot[:, t, :], 4)
                        x1, x2 = s4[:, :, 0:64], s4[:, :, 64:128]
                        cb, sb_ = bc(cs[:, t, :], [P, 4, 64], 1), bc(sn[:, t, :], [P, 4, 64], 1)
                        tmp4 = cut(tmp[:, 0:256], 4)
                        tt(r4[:, :, 0:64], x1, cb, ALU.mult, o, t_sc)
                        tt(tmp4, x2, sb_, ALU.mult)
                        tt(r4[:, :, 0:64], r4[:, :, 0:64], tmp4, ALU.subtract)
                        tt(r4[:, :, 64:128], x1, sb_, ALU.mult)
                        tt(tmp4, x2, cb, ALU.mult)
                        t_rot = tt(r4[:, :, 64:128], r4[:, :, 64:128], tmp4, ALU.add)
            t_u = o
            for src, dst in ((tq, qT), (tk, kT)):
                for hp in range(2):
                    b = take()
                    PE.wait(t_rot)
                    for i in range(2):
                        for t in range(2):
                            h = 2 * hp + i
                            k_ = tr(banks[b][:, 256 * i + 128 * t:256 * i + 128 * t + 128],
                                    src[:, t, 128 * h:128 * h + 128], sig=(i == 1 and t == 1))
                    t_T = act(dst[:, 2 * hp:2 * hp + 2, :], cut(banks[b][:, :], 2), ACT.Copy, k_)
                    free[b] = [t_T]
            bd = c2s("bands")
            for i in range(4):
                b = take()
                PE.wait(t_u, t_c2)
                mm(banks[b][:, 0:256], u[:, 0, 128 * i:128 * i + 128], bd[:, 384 * i:384 * i + 256], True, False)
                to = mms(banks[b][:, 128:256], u[:, 1, 128 * i:128 * i + 128], bd[:, 384 * i + 256:384 * i + 384],
                         False, True)
                o = vcopy(yT[:, i, :], banks[b][:, 0:256], to)
                free[b] = [o]
            for i in range(4):
                b = take()
                PE.wait(o, t_pw)
                to = mms(banks[b][:, 0:256], pw[:, 128 * i:128 * i + 128], yT[:, i, :], True, True)
                free[b] = [fill_slots([(4 + i, banks[b][:, 0:256], col("pool_scale", i))], to)]
            bi = []
            for t in range(2):
                b = take()
                PE.wait(t_T)
                for h in range(4):
                    sl = slice(128 * t, 128 * t + 128)
                    to = mms(banks[b][:, 128 * h:128 * h + 128], kT[:, h, sl], qT[:, h, sl], True, True)
                o = tt(Ms[:, t, :], banks[b][:, :], c2s("rmask"), ALU.mult, to)
                free[b] = [o]
                b = take()
                held.add(b)
                bi.append(b)
                PE.wait(o)
                for h in range(4):
                    t_in = mms(banks[b][:, 128 * h:128 * h + 128], Ms[:, t, 128 * h:128 * h + 128],
                               v[:, t, 128 * h:128 * h + 128], True, True)
            o = tt(cut(kd, 4), cut(tk[:, 0, :], 4), bc(c2s("kdec"), [P, 4, 128], 2), ALU.mult)
            b = take()
            PE.wait(o)
            for h in range(4):
                to = mms(banks[b][:, 128 * h:128 * h + 128], kd[:, 128 * h:128 * h + 128],
                         v[:, 0, 128 * h:128 * h + 128], True, True)
            o = act(sta, banks[b][:, :], ACT.Copy, to)
            free[b] = [o]
            b = take()
            PE.wait(o)
            for h in range(4):
                to = mms(banks[b][:, 128 * h:128 * h + 128], qT[:, h, 128:256], sta[:, 128 * h:128 * h + 128],
                         True, True)
            ro = q
            o = vcopy(ro[:, 0, :], banks[bi[0]][:, :], t_in)
            free[bi[0]] = [o]
            o = tt(cut(ro[:, 1, :], 4), cut(banks[b][:, :], 4), bc(c2s("qdec"), [P, 4, 128], 2), ALU.mult, to)
            free[b] = [o]
            o = tt(ro[:, 1, :], ro[:, 1, :], banks[bi[1]][:, :], ALU.add)
            free[bi[1]] = [o]
            held.difference_update(bi)
            for t in range(2):
                for h in range(4):
                    i = 4 * t + h
                    DV.do(lambda e, t=t, h=h, i=i: e.bn_stats(bst[:, 6 * i:6 * i + 6],
                                                              ro[:, t, 128 * h:128 * h + 128]))
                    o = DV.do(lambda e, i=i: e.bn_aggr(mv[:, 2 * i:2 * i + 2], bst[:, 6 * i:6 * i + 6]))
            vv = cut(mv, 8)[:, :, 1]
            PO.do(lambda e: e.tensor_scalar(vv, vv, EPS, None, ALU.add), o)
            r = ptt(vv, vv, cst("mhalf").to_broadcast([P, 8]), ALU.pow)
            for t in range(2):
                for h in range(4):
                    i = 4 * t + h
                    a = ro[:, t, 128 * h:128 * h + 128]
                    ts(a, a, mv[:, 2 * i:2 * i + 1], mv[:, 2 * i + 1:2 * i + 2], ALU.subtract, ALU.mult, r)
                o = tt(ro[:, t, :], ro[:, t, :], g[:, t, :], ALU.mult)
            turn_to_slot(lambda t, j: ro[:, t, 128 * j:128 * j + 128], lambda j: col("ret_norm", j),
                         [0, 1, 2, 3], o)
            bs = open_out()
            for j in range(4):
                td = rows_out(bs, [2 * j, 2 * j + 1], j == 0, j == 3)
            close_out(bs, td)

        def conformer():
            room = Room()
            xn = room(2048, 2)
            rows = room(1024)
            up = room(8 * 286, 8)
            cv = room(2048, 8)
            dn = room(2048, 2)
            sg = room(512, 2)
            bst = room(24)
            mv = room(4)
            t_r = load(rows, d_rows[:, 0:1024], t_x)
            norm_x("mixer_norm_g", 8, xn)
            z = DV.do(lambda e: e.memset(up[:, :, 0:30], 0.0))
            for j in range(4):
                ba, ta = project_stationary()
                bg, tg = project_stationary()
                for i in range(2):
                    ft = 2 * j + i
                    o = act(sg[:, i, :], banks[bg][:, 256 * i:256 * i + 256], ACT.Sigmoid, tg, z,
                            bias=col("b_pw1", 8 + ft))
                    z = stt(up[:, ft, 30:286], banks[ba][:, 256 * i:256 * i + 256], col("b_pw1", ft), sg[:, i, :],
                            ALU.add, ALU.mult, o, ta)
                free[bg], free[ba] = [o], [z]
                for i in range(2):
                    ft = 2 * j + i
                    ts(cv[:, ft, :], up[:, ft, 0:256], col("w_dw", ft), col("b_dw", ft), ALU.mult, ALU.add)
                    for w in range(1, 31):
                        t_cv = stt(cv[:, ft, :], up[:, ft, w:w + 256], col("w_dw", 8 * w + ft), cv[:, ft, :],
                                   ALU.mult, ALU.add)
            bb = {}
            for t in range(2):
                for c in range(2):
                    b = take()
                    PE.wait(t_cv)
                    for i in range(4):
                        k_ = tr(banks[b][:, 128 * i:128 * i + 128], cv[:, 4 * c + i, 128 * t:128 * t + 128],
                                sig=(i == 3))
                    bb[(t, c)] = b
                    DV.do(lambda e, t=t, c=c, b=b: e.bn_stats(bst[:, 12 * t + 6 * c:12 * t + 6 * c + 6],
                                                              banks[b][:, :]), k_)
                o = DV.do(lambda e, t=t: e.bn_aggr(mv[:, 2 * t:2 * t + 2], bst[:, 12 * t:12 * t + 12]))
            vv = cut(mv, 2)[:, :, 1]
            PO.do(lambda e: e.tensor_scalar(vv, vv, EPS, None, ALU.add), o)
            r = ptt(vv, vv, cst("mhalf").to_broadcast([P, 2]), ALU.pow)
            for t in range(2):
                for c in range(2):
                    b = bb[(t, c)]
                    o = ts(dn[:, t, 512 * c:512 * c + 512], banks[b][:, :], mv[:, 2 * t:2 * t + 1],
                           mv[:, 2 * t + 1:2 * t + 2], ALU.subtract, ALU.mult, r)
                    free[b] = [o]
            for t in range(2):
                t_x[t] = tt(xt[:, t, :], xt[:, t, :], rows, ALU.add, t_r)
            bs = open_out()
            for j in range(4):
                b = take()
                PE.wait(o)
                for i in range(2):
                    for t in range(2):
                        ft = 2 * j + i
                        k_ = tr(banks[b][:, 256 * i + 128 * t:256 * i + 128 * t + 128],
                                dn[:, t, 128 * ft:128 * ft + 128], sig=(i == 1 and t == 1))
                for i in range(2):
                    ft = 2 * j + i
                    a = act(cv[:, ft, :], banks[b][:, 256 * i:256 * i + 256], ACT.Silu, k_,
                            scale=col("ln_g", ft), bias=col("ln_b", ft))
                    fill_slots([(ft, cv[:, ft, :], None)], a)
                free[b] = [a]
            for j in range(4):
                td = rows_out(bs, [2 * j, 2 * j + 1], j == 0, j == 3)
            close_out(bs, td)

        def final():
            room = Room()
            xn = room(2048, 2)
            rows = room(1024)
            t_r = load(rows, d_rows[:, 1024:2048], t_x)
            a = act(xn[:, 0, :], xt[:, 0, :], ACT.Square, t_x[0], accum_out=st[:, 0:1])
            b = act(xn[:, 1, :], xt[:, 1, :], ACT.Square, t_x[1], accum_out=st[:, 1:2])
            r = rstd(st[:, 0:2], 1024, a, b)
            for t in range(2):
                o = stt(xn[:, t, :], xt[:, t, :], st[:, t:t + 1], rows, ALU.mult, ALU.mult, r, t_r)
                SP.quiet(lambda e, t=t: e.dma_start(d_out[0, t * P:(t + 1) * P, :], xn[:, t, :]).then_inc(s_out, 16),
                         o)
            SP.wait((s_out, 32))

        stages = [ssd_gla, lambda: ffn("ffn_norm", 0), mla, lambda: ffn("ffn_norm", 8), ret_pool,
                  lambda: ffn("ffn_norm_g", 0), conformer, lambda: ffn("ffn_norm_g", 8), final]
        for i, f in enumerate(stages):
            if i < stop or (stop == 99):
                f()
        if stop != 99:
            for t in range(2):
                SP.quiet(lambda e, t=t: e.dma_start(d_out[0, t * P:(t + 1) * P, :], xt[:, t, :]).then_inc(s_out, 16),
                         t_x)
            for s in range(NR):
                SP.wait((s_raw[s], 16 * ((sent[0] - s + NR - 1) // NR)))
            SP.wait((s_out, 32))

        block = ctx.enter_context(nc.Block())

        @block.sync
        def _(e):
            SP.emit(e)

        @block.tensor
        def _(e):
            PE.emit(e)

        @block.vector
        def _(e):
            DV.emit(e)

        @block.scalar
        def _(e):
            AC.emit(e)

        @block.gpsimd
        def _(e):
            PO.emit(e)


def shape_constants():
    i = np.arange(P)
    c0 = np.zeros((P, NC0), np.float32)
    c0[:, 0:128] = np.eye(P)
    c0[:, 128:256] = i[:, None] <= i[None, :]
    c0[:, 256:384] = (i[:, None] <= i[None, :]) & (i[:, None] // 64 == i[None, :] // 64)
    c0[:, 384:640] = (np.arange(256) % 64 != 0)[None, :]
    c0[:, 640] = -0.5
    c1 = np.zeros((P, NC1), np.float32)
    c1[:, 128:256] = np.where(i[None, :] <= i[:, None], 0.0, -1e30)
    inv = (1.0 / (np.float32(10000.0) ** (np.arange(0, 32, 2, dtype=np.float32) / np.float32(32)))).astype(np.float32)
    ang = (np.arange(256, dtype=np.float32)[:, None] * inv[None, :]).astype(np.float32).astype(np.float64)
    c1[:, 256:288] = np.cos(ang).reshape(2, P, 16).transpose(1, 0, 2).reshape(P, 32)
    c1[:, 288:320] = np.sin(ang).reshape(2, P, 16).transpose(1, 0, 2).reshape(P, 32)
    c2 = np.zeros((P, NC2), np.float32)
    lg = np.log1p(-(2.0 ** (-5.0 - np.arange(4))))
    rel = i[None, :] - i[:, None]
    for h in range(4):
        c2[:, 128 * h:128 * h + 128] = np.where(rel >= 0, np.exp(lg[h] * np.maximum(rel, 0)), 0.0) * 128.0 ** -0.5
        c2[:, 512 + h] = np.exp(lg[h] * (127.0 - i)) * 128.0 ** -0.5
        c2[:, 516 + h] = np.exp(lg[h] * (i + 1.0))
    f = np.arange(64, dtype=np.float32)
    c2[:, 520:584] = (np.float32(10000.0) ** (-f / np.float32(64)))[None, :]
    t = np.arange(256)
    for gi, w in enumerate((2, 4, 8, 16)):
        s = t[:, None]
        band = ((s <= t[None, :]) & (s > t[None, :] - w)) / np.minimum(t + 1, w)[None, :] - (s == t[None, :])
        c2[:, 584 + 384 * gi:584 + 384 * gi + 256] = band[0:128]
        c2[:, 584 + 384 * gi + 256:584 + 384 * gi + 384] = band[128:256, 128:256]
    return c0, c1, c2


def pack_inputs(a):
    w = {
        "w_in": a["w_in_even"][0], "w_out": a["w_out_even"][0], "w_dqkv": a["w_dqkv"][0], "w_uq": a["w_uq"][0],
        "w_ukv": a["w_ukv"][0], "w_o": a["w_o_mla"][0], "ret_w_in": a["ret_w_in_2"][0],
        "mix_w_out": a["mix_w_out_2"][0], "pw1": a["conv_w_pw1_2"][0], "pw2": a["conv_w_pw2_2"][0],
    }
    w["w_in_s"] = np.concatenate([w["w_in"][:, 2560:2576], w["w_in"][:, 5648:5664]], axis=1)
    for i in range(4):
        src = ("w_gate", "w_up", "w_down") if i < 2 else ("ffn_w_gate_2", "ffn_w_up_2", "ffn_w_down_2")
        for tag, name in zip(("gate", "up", "down"), src):
            w[f"{tag}{i}"] = a[name][i % 2]
    ws = np.zeros((len(PLAN), P, CH), np.float32)
    for n, (name, k0, kn, c0, cn) in enumerate(PLAN):
        part = w[name][128 * k0:128 * (k0 + kn), c0:c0 + cn].reshape(kn, P, cn)
        ws[n, :, 0:kn * cn] = part.transpose(1, 0, 2).reshape(P, kn * cn)
    cols = np.zeros((P, NCOL), np.float32)

    def put(name, v, off=0):
        o = COLS[name][0] + off
        v = np.asarray(v).reshape(-1, P).T
        cols[:, o:o + v.shape[1]] = v

    put("mix_norm_even", a["mix_norm_even"])
    put("conv_w", a["conv_w"])
    put("conv_b", a["conv_b"])
    put("ssd_norm", a["ssd_norm"])
    put("gk_b", a["gla_gk_b"])
    put("gla_norm", a["gla_norm"])
    put("ffn_norm", a["ffn_norm"])
    put("mix_norm_odd", a["mix_norm_odd"])
    put("q_lora", a["q_lora_norm"])
    put("kv_lora", a["kv_lora_norm"])
    put("mixer_norm_g", a["mixer_norm_g_2"])
    put("ffn_norm_g", a["ffn_norm_g_2"])
    put("ret_norm", a["ret_norm_g_2"])
    put("pool_scale", a["pool_scale_2"])
    put("b_pw1", a["conv_b_pw1_2"])
    put("w_dw", a["conv_w_dw_2"])
    put("b_dw", a["conv_b_dw_2"])
    put("ln_g", a["conv_ln_g_2"])
    put("ln_b", a["conv_ln_b_2"])
    for name, key in (("qfull", "q_nope_norm"), ("kfull", "k_nope_norm")):
        cols[:, COLS[name][0]] = 1.0
        cols[0:64, COLS[name][0]] = a[key][0]
    for name in ("dt_bias", "a_log", "d_skip", "q_rope_norm", "k_rope_norm"):
        o, n = COLS[name]
        cols[:, o:o + n] = a[name][0][None, :]
    rows = np.zeros((P, 2048), np.float32)
    rows[:, 0:1024] = a["conv_b_pw2_2"][0][None, :]
    rows[:, 1024:2048] = a["final_norm_g_2"][None, :]
    c0, c1, c2 = shape_constants()
    return {
        "d_x": np.ascontiguousarray(a["x"]), "d_ws": ws, "d_cols": cols, "d_c0": c0, "d_c1": c1, "d_c2": c2,
        "d_gkw2": np.ascontiguousarray(a["gla_gk_w2"][0]),
        "d_poolw": np.ascontiguousarray(a["pool_w_2"][0].transpose(1, 0, 2).reshape(P, 512)),
        "d_rows": rows,
        "d_pos": np.ascontiguousarray(a["positions_2"].reshape(2, P).T),
    }


def kernel(**inputs):
    import concourse.bacc as _bacc
    from concourse.bass_utils import run_bass_kernel_spmd as _run

    nc = _bacc.Bacc("TRN2", target_bir_lowering=False, num_devices=1)
    arrays = pack_inputs({n: np.asarray(v) for n, v in inputs.items()})
    args = [nc.dram_tensor(n, v.shape, mybir.dt.from_np(v.dtype), kind="ExternalInput").ap()
            for n, v in arrays.items()]
    out = nc.dram_tensor("out", (1, 256, 1024), F32, kind="ExternalOutput").ap()
    build(nc, *args, out)
    r = _run(nc, [arrays], core_ids=[0])
    return r.results[0]["out"]
```

```python
from contextlib import ExitStack

import numpy as np
import concourse.bass as bass
from concourse import mybir

F32 = mybir.dt.float32
F32R = mybir.dt.float32r
I32 = mybir.dt.int32
U32 = mybir.dt.uint32
ALU = mybir.AluOpType
ACT = mybir.ActivationFunctionType
AX = mybir.AxisListType.X

P = 128
EPS = 1e-6
NR = 3
NH = 3
CH = 2048
SLOTS = 12

COLS = {}
_at = 0
for _name, _n in (("mix_norm_even", 8), ("conv_w", 48), ("conv_b", 12), ("ssd_norm", 8), ("gk_b", 4),
                  ("gla_norm", 2), ("ffn_norm", 16), ("mix_norm_odd", 8), ("q_lora", 3), ("kv_lora", 2),
                  ("qfull", 1), ("kfull", 1), ("mixer_norm_g", 16), ("ffn_norm_g", 16), ("ret_norm", 4),
                  ("pool_scale", 4), ("b_pw1", 16), ("w_dw", 248), ("b_dw", 8), ("ln_g", 8), ("ln_b", 8),
                  ("dt_bias", 16), ("a_log", 16), ("d_skip", 16), ("q_rope_norm", 32), ("k_rope_norm", 32)):
    COLS[_name] = (_at, _n)
    _at += _n
NCOL = _at
C0 = {"ident": (0, 128), "U": (128, 128), "gmask": (256, 128), "reset": (384, 256), "ones": (640, 128),
      "mhalf": (768, 1)}
NC0 = 769
C1 = {"maskadd": (0, 256), "cos": (256, 32), "sin": (288, 32)}
NC1 = 320
C2 = {"rmask": (0, 512), "kdec": (512, 4), "qdec": (516, 4), "invf": (520, 64), "bands": (584, 1536)}
NC2 = 2120


def weight_plan():
    plan = [("w_in_s", 0, 8, 0, 32)]

    def stationary(w, c0, n):
        return [(w, 0, 8, c0 + 256 * j, 256) for j in range(n // 256)]

    def moving(w, c0, n):
        return [(w, 4 * k, 4, c0 + 512 * j, 512) for j in range(n // 512) for k in range(2)]

    def rows(w, n):
        return [(w, 2 * k, 2, 0, 1024) for k in range(n)]

    def ffn(tag):
        out = []
        for j in range(11):
            out += [("gate" + tag, 0, 8, 256 * j, 256), ("up" + tag, 0, 8, 256 * j, 256)]
            if j:
                out.append(("down" + tag, 2 * (j - 1), 2, 0, 1024))
        return out + [("down" + tag, 20, 2, 0, 1024)]

    plan += stationary("w_in", 1024, 1536)
    plan += stationary("w_in", 3088, 512) + stationary("w_in", 2576, 512)
    plan += moving("w_in", 3600, 1024)
    plan += moving("w_in", 4624, 1024)
    plan += moving("w_in", 0, 1024)
    plan += rows("w_out", 8)[4:] + rows("w_out", 8)[:4] + ffn("0")
    plan += moving("w_dqkv", 0, 512) + [("w_dqkv", 0, 8, 512, 160)]
    plan += [("w_uq", 0, 3, 512 * j, 512) for j in range(3)]
    plan += [("w_ukv", 0, 2, 1024 * j, 1024) for j in range(2)]
    plan += rows("w_o", 4) + ffn("1")
    plan += moving("ret_w_in", 0, 2560) + rows("mix_w_out", 4)[2:] + rows("mix_w_out", 4)[:2] + ffn("2")
    for j in range(4):
        plan += stationary("pw1", 256 * j, 256) + stationary("pw1", 1024 + 256 * j, 256)
    plan += rows("pw2", 4) + ffn("3")
    return plan


PLAN = weight_plan()


class Lane:

    def __init__(self, sem, linked):
        self.sem, self.linked = sem, linked
        self.ops, self.n, self.seen = [], 0, {}

    def wait(self, *toks):
        for t in toks:
            if t is None:
                continue
            if isinstance(t, list):
                self.wait(*t)
                continue
            sem, v = t
            if self.seen.get(id(sem), 0) < v:
                self.seen[id(sem)] = v
                self.ops.append((None, sem, v))

    def quiet(self, fn, *toks):
        self.wait(*toks)
        self.ops.append((fn, None, 0))

    def do(self, fn, *toks):
        self.wait(*toks)
        if self.linked and self.n:
            self.wait((self.sem, self.n))
        self.n += 1
        self.ops.append((fn, self.sem, 1))
        return (self.sem, self.n)

    def emit(self, eng):
        for fn, sem, v in self.ops:
            if fn is None:
                eng.wait_ge(sem, v)
            else:
                i = fn(eng)
                if sem is not None:
                    i.then_inc(sem, v)


def build(nc, d_x, d_ws, d_cols, d_c0, d_c1, d_c2, d_gkw2, d_poolw, d_rows, d_pos, d_out, stop=99):
    ctx = ExitStack()
    with ctx:
        def sb(name, shape, dt=F32):
            return ctx.enter_context(nc.sbuf_tensor(name, shape, dt))

        def sem(name):
            return ctx.enter_context(nc.semaphore(name))

        raw = sb("raw", [P, NR, CH])
        whi = sb("whi", [P, NH, CH], F32R)
        wlo = sb("wlo", [P, NH, CH], F32R)
        ahi = sb("ahi", [P, SLOTS, 256], F32R)
        alo = sb("alo", [P, SLOTS, 256], F32R)
        xt = sb("xt", [P, 2, 1024])
        cols = sb("cols", [P, NCOL])
        c0 = sb("c0", [P, NC0])
        st = sb("st", [P, 256])
        NA = 24700
        arena = sb("arena", [P, NA])
        banks = [ctx.enter_context(nc.psum_tensor(f"pb{i}", [P, 512], F32)) for i in range(8)]

        PE, DV, AC, PO, SP = (Lane(sem("s_pe"), False), Lane(sem("s_dve"), True), Lane(sem("s_act"), True),
                              Lane(sem("s_pool"), True), Lane(None, False))
        s_raw = [sem(f"s_raw{i}") for i in range(NR)]
        dma_sems = iter([sem(f"s_in{i}") for i in range(12)])
        s_out = sem("s_out")

        def load(dst, src, *toks):
            s = next(dma_sems)
            SP.quiet(lambda e: e.dma_start(dst, src).then_inc(s, 16), *toks)
            return (s, 16)

        def col(name, i=0, n=1, parts=P):
            a = COLS[name][0] + i
            return cols[0:parts, a:a + n]

        def cst(name):
            a, n = C0[name]
            return c0[:, a:a + n]

        def tt(out, a, b, op, *w):
            return DV.do(lambda e: e.tensor_tensor(out, a, b, op), *w)

        def ts(out, a, s1, s2, op0, op1, *w):
            if op1 is None:
                return DV.do(lambda e: e.tensor_scalar(out, a, s1, None, op0), *w)
            return DV.do(lambda e: e.tensor_scalar(out, a, s1, s2, op0, op1), *w)

        def stt(out, a, s, b, op0, op1, *w):
            return DV.do(lambda e: e.scalar_tensor_tensor(out=out, in0=a, scalar=s, in1=b, op0=op0, op1=op1), *w)

        def vcopy(out, a, *w):
            return DV.do(lambda e: e.tensor_copy(out, a), *w)

        def act(out, a, func, *w, **kw):
            return AC.do(lambda e: e.activation(out, a, func, **kw), *w)

        def ptt(out, a, b, op, *w):
            return PO.do(lambda e: e.tensor_tensor(out, a, b, op), *w)

        def bc(ap, shape, axis):
            return ap.unsqueeze(axis).to_broadcast(shape)

        def f32(ap):
            return ap.bitcast(F32)

        def cut(ap, a, b=None):
            if b is None:
                return ap.rearrange("p (a b) -> p a b", a=a)
            return ap.rearrange("p (a b c) -> p a b c", a=a, b=b)

        def mm(out, l, r, start, stop, skip=False):
            PE.quiet(lambda e: e.matmul(out, l, r, start=start, stop=stop, skip_group_check=skip))

        def mms(out, l, r, start, stop, skip=False):
            return PE.do(lambda e: e.matmul(out, l, r, start=start, stop=stop, skip_group_check=skip))

        def mm3(out, lh, ll, rh, rl, start, stop):
            mm(out, lh, rh, start, False)
            mm(out, lh, rl, False, False)
            return PE.do(lambda e: e.matmul(out, ll, rh, start=False, stop=stop))

        ident = cst("ident")

        def tr(out, a, sig=False):
            k = a.shape[0]
            f = lambda e: e.transpose(out, a, ident[0:k, 0:k])
            return PE.do(f) if sig else PE.quiet(f)

        free = [[] for _ in range(8)]
        held = set()
        turn = [0]

        def take():
            while turn[0] % 8 in held:
                turn[0] += 1
            b = turn[0] % 8
            turn[0] += 1
            PE.wait(*free[b])
            free[b] = []
            return b

        t_x = [load(xt[:, t, :], d_x[0, t * P:(t + 1) * P, :]) for t in range(2)]
        t_cols = load(cols[:, :], d_cols)
        t_c0 = load(c0[:, :], d_c0)
        for lane in (PE, DV, AC, PO):
            lane.wait(t_c0, t_cols)

        sent = [0]
        split = [0]
        lo_tok, done = {}, {}

        def send(n):
            w = PLAN[n][2] * PLAN[n][4]
            SP.quiet(lambda e: e.dma_start(raw[:, n % NR, 0:w], d_ws[n, :, 0:w]).then_inc(s_raw[n % NR], 16),
                     lo_tok.get(n - NR))

        def split_chunk(n):
            w = PLAN[n][2] * PLAN[n][4]
            r, h, l = raw[:, n % NR, 0:w], whi[:, n % NH, 0:w], wlo[:, n % NH, 0:w]
            arrived = (s_raw[n % NR], 16 * (n // NR + 1))
            t = act(h, r, ACT.Copy, arrived, done.get(n - NH))
            lo_tok[n] = tt(l, r, f32(h), ALU.subtract, arrived, t)

        def ahead(n):
            while split[0] <= min(n, len(PLAN) - 1):
                while sent[0] <= min(split[0] + NR - 1, len(PLAN) - 1):
                    send(sent[0])
                    sent[0] += 1
                split_chunk(split[0])
                split[0] += 1

        used = [0]

        def chunk():
            n = used[0]
            used[0] += 1
            ahead(n + NH - 1)
            PE.wait(lo_tok[n])
            w = PLAN[n][2] * PLAN[n][4]
            k = PLAN[n][2]
            return n, cut(whi[:, n % NH, 0:w], k), cut(wlo[:, n % NH, 0:w], k)

        slot_ready = [None] * SLOTS
        slot_free = [[] for _ in range(SLOTS)]

        def rstd(ap, width, *w):
            PO.do(lambda e: e.tensor_scalar(ap, ap, 1.0 / width, EPS, ALU.mult, ALU.add), *w)
            n = ap.shape[1]
            return ptt(ap, ap, cst("mhalf").to_broadcast([P, n]), ALU.pow)

        def fill_slots(parts, *w):
            for s, src, gain in parts:
                kw = {} if gain is None else {"scale": gain}
                t_hi = act(ahi[:, s, :], src, ACT.Copy, slot_free[s], *w, **kw)
            for s, src, gain in parts:
                h, l = f32(ahi[:, s, :]), alo[:, s, :]
                if gain is None:
                    t_lo = tt(l, src, h, ALU.subtract, t_hi)
                else:
                    t_lo = stt(l, src, gain, h, ALU.mult, ALU.subtract, t_hi)
                slot_free[s] = []
                slot_ready[s] = t_lo
            return t_lo

        def turn_to_slot(srcs, gains, slots, *w):
            for j in range(0, len(slots), 2):
                b = take()
                PE.wait(*w)
                m = min(2, len(slots) - j)
                for i in range(m):
                    for t in range(2):
                        k = tr(banks[b][:, 256 * i + 128 * t:256 * i + 128 * t + 128], srcs(t, j + i),
                               sig=(i == m - 1 and t == 1))
                free[b] = [fill_slots([(slots[j + i], banks[b][:, 256 * i:256 * i + 256], gains(j + i))
                                       for i in range(m)], k)]

        t_sq = [None, None]

        def squares(t, c, b, *w):
            t_sq[t] = act(banks[b][:, :], xt[:, t, 512 * c:512 * c + 512], ACT.Square, *w,
                          accum_out=st[:, 2 * t + c:2 * t + c + 1])
            return t_sq[t]

        def x_rstd():
            out = []
            for t in range(2):
                a = tt(st[:, 4 + t:5 + t], st[:, 2 * t:2 * t + 1], st[:, 2 * t + 1:2 * t + 2], ALU.add, t_sq[t])
                out.append(rstd(st[:, 4 + t:5 + t], 1024, a))
            return out

        def turn_x(gname, g0, src, ready):
            bs = [take() for _ in range(4)]
            for t in range(2):
                for c in range(2):
                    PE.wait(ready[t][c])
                    for j in range(4 * c, 4 * c + 4):
                        o = 256 * (j % 2) + 128 * t
                        k = tr(banks[bs[j // 2]][:, o:o + 128], src[:, t, 128 * j:128 * j + 128], sig=(j % 2 == 1))
                        if t == 1 and j % 2 == 1:
                            free[bs[j // 2]] = [k]
            for i, b in enumerate(bs):
                free[b] = [fill_slots([(2 * i + j, banks[b][:, 256 * j:256 * j + 256], col(gname, g0 + 2 * i + j))
                                       for j in range(2)], *free[b])]

        def norm_x(gname, g0, xn):
            r = x_rstd()
            ready = []
            for t in range(2):
                ready.append([])
                for c in range(2):
                    h = slice(512 * c, 512 * c + 512)
                    if c:
                        k = ts(xn[:, t, h], xt[:, t, h], st[:, 4 + t:5 + t], None, ALU.mult, None, r[t])
                    else:
                        k = act(xn[:, t, h], xt[:, t, h], ACT.Copy, r[t], scale=st[:, 4 + t:5 + t])
                    ready[t].append(k)
            turn_x(gname, g0, xn, ready)

        def turn_raw(gname, g0):
            turn_x(gname, g0, xt, t_xh)
            return x_rstd()

        t_xh = [[None, None], [None, None]]

        for t in range(2):
            for c in range(2):
                b = 2 * t + c
                squares(t, c, b, t_x[t])
                free[b] = [t_sq[t]]
                t_xh[t][c] = t_x[t]
        ahead(0)

        def project_moving(ncols, between=None):
            bs = [take(), take()]
            k0, n_chunks = 0, 0
            while k0 < 8:
                n, wh, wl = chunk()
                kk = PLAN[n][2]
                for k in range(kk):
                    PE.wait(slot_ready[k0 + k])
                    for t in range(2):
                        t_done = mm3(banks[bs[t]][:, 0:ncols], ahi[:, k0 + k, 128 * t:128 * t + 128],
                                     alo[:, k0 + k, 128 * t:128 * t + 128], wh[:, k, :], wl[:, k, :],
                                     k0 + k == 0, k0 + k == 7)
                    slot_free[k0 + k] = [t_done]
                done[n] = t_done
                k0 += kk
                if between and k0 < 8:
                    between()
            return bs, t_done

        def project_stationary():
            b = take()
            n, wh, wl = chunk()
            for i in range(2):
                for k in range(8):
                    PE.wait(slot_ready[k])
                    t_done = mm3(banks[b][:, 256 * i:256 * i + 256], wh[:, k, 128 * i:128 * i + 128],
                                 wl[:, k, 128 * i:128 * i + 128], ahi[:, k, :], alo[:, k, :], k == 0, k == 7)
                    slot_free[k] = [t_done]
            done[n] = t_done
            return b, t_done

        def open_out():
            bs = [take() for _ in range(4)]
            held.update(bs)
            return bs

        def rows_out(bs, slots, first, last):
            n, wh, wl = chunk()
            t_end = []
            for t in range(2):
                for k, s in enumerate(slots):
                    PE.wait(slot_ready[s])
                    for c in range(2):
                        f, l = first and k == 0, last and k == len(slots) - 1
                        t_done = mm3(banks[bs[2 * t + c]][:, :], ahi[:, s, 128 * t:128 * t + 128],
                                     alo[:, s, 128 * t:128 * t + 128], wh[:, k, 512 * c:512 * c + 512],
                                     wl[:, k, 512 * c:512 * c + 512], f, l)
                t_end.append(t_done)
            for s in slots:
                slot_free[s] = [t_done]
            done[n] = t_done
            return t_end

        def close_out(bs, t_done):
            for t in range(2):
                for c in range(2):
                    b = bs[2 * t + c]
                    v = xt[:, t, 512 * c:512 * c + 512]
                    t_xh[t][c] = tt(v, v, banks[b][:, :], ALU.add, t_done[t])
                    free[b] = [squares(t, c, b, t_xh[t][c])]
                t_x[t] = t_xh[t][1]
            held.difference_update(bs)

        def ffn(gname, g0):
            gr, ur = arena[:, 0:512], arena[:, 512:1024]
            sg = cut(arena[:, 1024:2048], 2)
            hh = cut(arena[:, 2048:3072], 2)
            dg, rb = arena[:, 3072:3328], arena[:, 3328:3584]
            r = turn_raw(gname, g0)
            for t in range(2):
                k = ts(dg[:, 128 * t:128 * t + 128], ident, st[:, 4 + t:5 + t], None, ALU.mult, None, r[t])
            t_rb = None
            hf = [None, None]
            bs = open_out()
            for j in range(12):
                if j < 11:
                    bg, tg = project_stationary()
                    if j == 0:
                        b = take()
                        PE.wait(k)
                        k = mms(banks[b][:, 0:256], cst("ones"), dg, True, True)
                        t_rb = act(rb, banks[b][:, 0:256], ACT.Copy, k)
                        free[b] = [t_rb]
                        rb2 = bc(rb, [P, 2, 256], 1)
                    g = tt(cut(gr, 2), cut(banks[bg][:, :], 2), rb2, ALU.mult, tg, t_rb)
                    free[bg] = [g]
                    a = act(sg[:, j % 2, :], gr, ACT.Silu, g)
                    bu, tu = project_stationary()
                    h = tt(cut(ur, 2), cut(banks[bu][:, :], 2), rb2, ALU.mult, tu)
                    free[bu] = [h]
                    h = tt(hh[:, j % 2, :], sg[:, j % 2, :], ur, ALU.mult, a)
                    hf[j % 2] = fill_slots([(8 + (2 * j + i) % 4, hh[:, j % 2, 256 * i:256 * i + 256], None)
                                            for i in range(2)], h)
                if j:
                    s = 8 + (2 * (j - 1)) % 4
                    t_done = rows_out(bs, [s, s + 1], j == 1, j == 11)
            close_out(bs, t_done)

        class Room:
            def __init__(self):
                self.at = 0

            def __call__(self, n, *shape):
                a = arena[:, self.at:self.at + n]
                self.at += n
                assert self.at <= NA, self.at
                return cut(a, *shape) if shape else a

        def ssd_gla():
            room = Room()
            xbc = room(12 * 259, 12)
            xs = room(2048, 2)
            bt = room(256, 2)
            zs, gs, v = room(2048, 2), room(2048, 2), room(2048, 2)
            q, k, X, U_ = (room(1024) for _ in range(4))
            kend = room(1024, 2)
            S = room(1536, 2, 3)
            sT = room(1024)
            xdte = room(1024)
            M = room(1536, 3)
            pv = room(1024, 2)
            cb4 = room(128)
            glT = room(256)
            small = room(32 * 14)
            w2 = room(512)
            acc = cut(arena[:, 12 * 259 + 2304 + 2048:12 * 259 + 2304 + 2048 + 3072], 12)
            xdt = cut(arena[:, 0:2048], 2)
            t_w2 = load(w2[0:16, :], d_gkw2)
            UM = cst("U")
            dtr, nabs, u, w1, lw, dm, e0, dt, a_, ea, acol, eac, gl, dec = [small[:, 32 * i:32 * i + 32]
                                                                         for i in range(14)]
            z_pad = DV.do(lambda e: e.memset(xbc[:, :, 0:3], 0.0))
            z_sT = DV.do(lambda e: e.memset(sT[:, :], 0.0))
            norm_x("mix_norm_even", 0, zs)
            T = {}

            def early():
                b0, b1 = T["small"]
                t_done = T["t_small"]
                for t, b in enumerate((b0, b1)):
                    tt(dtr[:, 16 * t:16 * t + 16], banks[b][:, 0:16], col("dt_bias", 0, 16), ALU.add, t_done)
                    o = vcopy(gl[:, 16 * t:16 * t + 16], banks[b][:, 16:32])
                    free[b] = [o]
                n_ = stt(nabs, dtr, -1.0, dtr, ALU.mult, ALU.min)
                eu = act(u, nabs, ACT.Exp, n_)
                t_ea = act(ea[:, 0:16], col("a_log", 0, 16), ACT.Exp)
                yield
                b = take()
                PE.wait(o)
                for t in range(2):
                    ti = tr(banks[b][0:16, 128 * t:128 * t + 128], gl[:, 16 * t:16 * t + 16], sig=True)
                t_gl = vcopy(glT[0:16, :], banks[b][0:16, 0:256], ti)
                free[b] = [t_gl]
                t1 = ts(w1, u, 1.0, None, ALU.add, None, eu)
                t2 = act(lw, w1, ACT.Ln, t1)
                ts(dm, w1, 1.0, None, ALU.subtract, None)
                ts(e0, dm, 0.0, None, ALU.is_equal, None)
                tt(dm, dm, e0, ALU.add)
                DV.do(lambda e: e.reciprocal(dm, dm))
                tt(lw, lw, e0, ALU.add, t2)
                tt(lw, lw, u, ALU.mult)
                tt(lw, lw, dm, ALU.mult)
                stt(dt, dtr, 0.0, lw, ALU.max, ALU.add)
                T["a"] = stt(cut(a_, 2), cut(dt, 2), -1.0, bc(ea[:, 0:16], [P, 2, 16], 1), ALU.mult, ALU.mult, t_ea)
                yield
                gb = [take(), take()]
                PE.wait(t_gl, t_w2)
                for h in range(4):
                    t_g = mms(banks[gb[h // 2]][:, 256 * (h % 2):256 * (h % 2) + 256],
                              w2[0:16, 128 * h:128 * h + 128], glT[0:16, :], True, True)
                for h in range(4):
                    o = act(X[:, 256 * h:256 * h + 256], banks[gb[h // 2]][:, 256 * (h % 2):256 * (h % 2) + 256],
                            ACT.Identity, t_g, bias=col("gk_b", h))
                    free[gb[h // 2]] = [o]
                b = take()
                PE.wait(T["a"])
                ta = mms(banks[b][:, 0:32], UM, a_, True, True)
                o = stt(U_, X, -1.0, X, ALU.mult, ALU.min, o)
                T["acol"] = vcopy(acol, banks[b][:, 0:32], ta)
                free[b] = [T["acol"]]
                o = act(U_, U_, ACT.Exp, o)
                T["eac"] = act(eac, acol, ACT.Exp, T["acol"])
                T["x0"] = o
                yield
                o = ts(U_, U_, 1.0, None, ALU.add, None, T["x0"])
                o = act(U_, U_, ACT.Ln, o)
                ts(X, X, 0.0, None, ALU.min, None)
                tt(U_, X, U_, ALU.subtract, o)
                yield
                for h in range(4):
                    hs = slice(256 * h, 256 * h + 256)
                    T["cum"] = DV.do(lambda e, hs=hs: e.tensor_tensor_scan(X[:, hs], cst("reset"), U_[:, hs], 0.0,
                                                                           ALU.mult, ALU.add))
                yield

            def turn_xs(t, c):
                b = take()
                PE.wait(T["conv"])
                for i in range(4):
                    k_ = tr(banks[b][:, 128 * i:128 * i + 128], xbc[:, 4 * c + i, 3 + 128 * t:131 + 128 * t],
                            sig=(i == 3))
                T["xs"] = act(xs[:, t, 512 * c:512 * c + 512], banks[b][:, :], ACT.Copy, k_)
                free[b] = [T["xs"]]

            def ssd():
                yield
                turn_xs(0, 0)
                turn_xs(0, 1)
                yield
                turn_xs(1, 0)
                turn_xs(1, 1)
                b = take()
                for g in range(2):
                    k_ = tr(banks[b][:, 128 * g:128 * g + 128], xbc[:, 8 + g, 3:131], sig=True)
                T["bt"] = act(bt[:, :, :], cut(banks[b][:, 0:256], 2), ACT.Copy, k_)
                free[b] = [T["bt"]]
                yield
                for t in range(2):
                    T["xdt"] = tt(cut(xdt[:, t, :], 16), cut(xs[:, t, :], 16),
                                  bc(dt[:, 16 * t:16 * t + 16], [P, 16, 64], 2), ALU.mult, k_, T["xs"])
                    tt(cut(xs[:, t, :], 16), cut(xs[:, t, :], 16), bc(col("d_skip", 0, 16), [P, 16, 64], 2),
                       ALU.mult)
                t_m = [None] * 3
                units = [(c, g, hh) for c in range(2) for g in range(2) for hh in range(2)]
                t_e, cbs, by = {}, {}, {}

                def decays(n):
                    c, g, hh = units[n]
                    if hh == 0:
                        b = take()
                        cs = slice(3 + 128 * c, 131 + 128 * c)
                        tc = mms(banks[b][:, 0:128], xbc[:, 8 + g, cs], xbc[:, 10 + g, cs], True, True)
                        cbs[(c, g)] = (b, tc)
                    b = take()
                    PE.wait(T["a"])
                    for i in range(4):
                        h = 16 * c + 8 * g + 4 * hh + i
                        tb = mms(banks[b][:, 128 * i:128 * i + 128], a_[:, h:h + 1].to_broadcast([P, P]), UM,
                                 True, True)
                    m = M[:, n % 3, :]
                    for i in range(4):
                        h = 16 * c + 8 * g + 4 * hh + i
                        o = ts(m[:, 128 * i:128 * i + 128], banks[b][:, 128 * i:128 * i + 128],
                               acol[:, h:h + 1], 0.0, ALU.subtract, ALU.min, tb, t_m[n % 3])
                    free[b] = [o]
                    t_e[n] = act(m, m, ACT.Exp, o)

                def masked(n):
                    c, g, hh = units[n]
                    m = M[:, n % 3, :]
                    if hh == 0:
                        b, tc = cbs[(c, g)]
                        free[b] = [tt(cb4, banks[b][:, 0:128], UM, ALU.mult, tc)]
                    if c == 0:
                        w = slice(512 * g + 256 * hh, 512 * g + 256 * hh + 256)
                        t_xe[n] = tt(cut(xdte[:, w], 4), cut(xdt[:, 0, w], 4),
                                     cut(m, 4)[:, :, 127:128].to_broadcast([P, 4, 64]), ALU.mult, t_e[n])
                    t_e[n] = tt(cut(m, 4), cut(m, 4), bc(cb4, [P, 4, 128], 1), ALU.mult, t_e[n])

                def outputs(n):
                    c, g, hh = units[n]
                    m = M[:, n % 3, :]
                    if hh == 0:
                        by[(c, g)] = take()
                        held.add(by[(c, g)])
                    PE.wait(t_e[n], T["xdt"])
                    yb = banks[by[(c, g)]]
                    for i in range(4):
                        h = 8 * g + 4 * hh + i
                        ty = mms(yb[:, 64 * (4 * hh + i):64 * (4 * hh + i) + 64],
                                 m[:, 128 * i:128 * i + 128], xdt[:, c, 64 * h:64 * h + 64], True, True)
                    t_m[n % 3] = ty
                    if hh == 0:
                        return
                    gsl = slice(512 * g, 512 * g + 512)
                    b = take()
                    if c == 0:
                        PE.wait(t_xe[n], T["bt"])
                        tp = mms(banks[b][:, :], bt[:, g, :], xdte[:, gsl], True, True)
                        T["pv"] = act(pv[:, g, :], banks[b][:, :], ACT.Copy, tp)
                        free[b] = [T["pv"]]
                    else:
                        PE.wait(T["pv"])
                        to = mms(banks[b][:, :], xbc[:, 10 + g, 131:259], pv[:, g, :], True, True)
                        tmp = xdte[:, gsl]
                        o = tt(cut(tmp, 8), cut(banks[b][:, :], 8),
                               bc(eac[:, 16 + 8 * g:24 + 8 * g], [P, 8, 64], 2), ALU.mult, to, T["eac"], T["pv"])
                        free[b] = [o]
                        tt(xs[:, 1, gsl], xs[:, 1, gsl], tmp, ALU.add)
                    T["y"] = tt(xs[:, c, gsl], xs[:, c, gsl], yb[:, :], ALU.add, ty)
                    free[by[(c, g)]] = [T["y"]]
                    held.discard(by[(c, g)])

                t_xe = {}
                decays(0)
                yield
                masked(0)
                decays(1)
                yield
                for n in range(8):
                    outputs(n)
                    if n < 7:
                        masked(n + 1)
                    if n < 6:
                        decays(n + 2)
                    yield

            def gates():
                e1 = act(U_, X, ACT.Exp, T["cum"], scale=1.0 / 16)
                yield
                vcopy(dec[:, 0:16], cut(U_, 16)[:, :, 63], e1)
                T["q"] = stt(q, q, 128.0 ** -0.5, U_, ALU.mult, ALU.mult, T["kq"])
                o = tt(cut(U_, 16), cut(X, 16)[:, :, 63:64].to_broadcast([P, 16, 64]), cut(X, 16), ALU.subtract)
                e3 = act(U_, U_, ACT.Exp, o, scale=1.0 / 16)
                e2 = act(X, X, ACT.Exp, o, scale=-1.0 / 16)
                yield
                T["ke"] = tt(U_, U_, k, ALU.mult, e3)
                T["k"] = tt(k, k, X, ALU.mult, e2)
                yield

            def gla():
                for t in range(2):
                    b = take()
                    PE.wait(T["ke"])
                    for h in range(4):
                        k_ = tr(banks[b][:, 128 * h:128 * h + 128],
                                U_[:, 256 * h + 128 * t:256 * h + 128 * t + 128], sig=(h == 3))
                    t_kt = act(kend[:, t, :], banks[b][:, :], ACT.Copy, k_)
                    free[b] = [t_kt]
                yield
                gm = cst("gmask").bitcast(U32)
                for t in range(2):
                    b = take()
                    PE.wait(T["k"], T["q"])
                    for h in range(4):
                        sl = slice(256 * h + 128 * t, 256 * h + 128 * t + 128)
                        ti = mms(banks[b][:, 128 * h:128 * h + 128], k[:, sl], q[:, sl], True, True)
                    for h in range(4):
                        t_s = DV.do(lambda e, b=b, h=h, t=t: e.copy_predicated(
                            sT[:, 512 * t + 128 * h:512 * t + 128 * h + 128], gm,
                            banks[b][:, 128 * h:128 * h + 128]), ti, z_sT)
                    free[b] = [t_s]
                yield
                t_o, t_S = {}, {}

                def states(h):
                    vs = slice(256 * h, 256 * h + 256)
                    bb = [take(), take()]
                    PE.wait(t_kt, T["v"])
                    for c in (0, 2, 1):
                        rows = slice(64 * (c % 2), 64 * (c % 2) + 64)
                        tk = mms(banks[bb[c % 2]][:, 256 * (c // 2):256 * (c // 2) + 256],
                                 kend[rows, c // 2, 128 * h:128 * h + 128], v[rows, c // 2, vs], True, True)
                    s_ = S[:, h % 2]
                    vcopy(s_[:, 0, :], banks[bb[0]][:, 0:256], tk, t_o.get(h - 2))
                    stt(s_[:, 1, :], s_[:, 0, :], dec[:, 4 * h + 1:4 * h + 2], banks[bb[1]][:, 0:256], ALU.mult,
                        ALU.add)
                    t_S[h] = stt(s_[:, 2, :], s_[:, 1, :], dec[:, 4 * h + 2:4 * h + 3], banks[bb[0]][:, 256:512],
                                 ALU.mult, ALU.add)
                    free[bb[0]], free[bb[1]] = [t_S[h]], [t_S[h]]

                def head(h):
                    vs = slice(256 * h, 256 * h + 256)
                    s_ = S[:, h % 2]
                    b = take()
                    PE.wait(t_S[h], t_s)
                    for t in range(2):
                        mm(banks[b][:, 256 * t:256 * t + 256], sT[:, 512 * t + 128 * h:512 * t + 128 * h + 128],
                           v[:, t, vs], True, True, True)
                        for c in (2 * t, 2 * t + 1):
                            if c == 0:
                                continue
                            r0 = 64 * (c % 2)
                            to = mms(banks[b][r0:r0 + 64, 256 * t:256 * t + 256],
                                     q[:, 256 * h + 64 * c:256 * h + 64 * c + 64], s_[:, c - 1, :], False, True, True)
                    t_o[h] = to
                    for t in range(2):
                        i = 12 + 2 * h + t
                        a2 = act(X[:, 0:256], banks[b][:, 256 * t:256 * t + 256], ACT.Square, to, T["k"],
                                 accum_out=st[:, i:i + 1])
                    r = rstd(st[:, 12 + 2 * h:14 + 2 * h], 256, a2)
                    for t in range(2):
                        i = 12 + 2 * h + t
                        T["yg"] = stt(gs[:, t, vs], banks[b][:, 256 * t:256 * t + 256], st[:, i:i + 1],
                                      gs[:, t, vs], ALU.mult, ALU.mult, r, T["g"])
                    free[b] = [T["yg"]]

                states(0)
                yield
                for h in range(4):
                    if h < 3:
                        states(h + 1)
                    head(h)
                    yield

            def step(*gens):
                def go():
                    for g in gens:
                        next(g, None)
                return go

            b0, b1 = take(), take()
            n, wh, wl = chunk()
            for t, b in enumerate((b0, b1)):
                for kk in range(8):
                    PE.wait(slot_ready[kk])
                    t_done = mm3(banks[b][:, 0:32], ahi[:, kk, 128 * t:128 * t + 128],
                                 alo[:, kk, 128 * t:128 * t + 128], wh[:, kk, :], wl[:, kk, :], kk == 0, kk == 7)
            done[n] = t_done
            T["small"], T["t_small"] = (b0, b1), t_done
            ea_ = early()
            next(ea_)
            for j in range(6):
                b, td = project_stationary()
                fs = slice(2 * j, 2 * j + 2)
                o = act(xbc[:, fs, 3:259], cut(banks[b][:, :], 2), ACT.Copy, td, z_pad)
                for i in range(2):
                    ft = 2 * j + i
                    o = act(acc[:, ft, :], banks[b][:, 256 * i:256 * i + 256], ACT.Identity, td,
                            scale=col("conv_w", 36 + ft), bias=col("conv_b", ft))
                free[b] = [o]
                for i in range(2):
                    ft = 2 * j + i
                    for w in range(3):
                        c = stt(acc[:, ft, :], xbc[:, ft, w:w + 256], col("conv_w", 12 * w + ft), acc[:, ft, :],
                                ALU.mult, ALU.add, o)
                next(ea_, None)
            for _ in ea_:
                pass
            sd = ssd()
            nxt = step(sd)
            for i, dst in enumerate((k, k, q, q)):
                b, td = project_stationary()
                o = act(dst[:, 512 * (i % 2):512 * (i % 2) + 512], banks[b][:, :], ACT.Copy, td)
                free[b] = [o]
                if i == 0:
                    for j in range(3):
                        T["conv"] = act(xbc[:, 4 * j:4 * j + 4, 3:259], acc[:, 4 * j:4 * j + 4, :], ACT.Silu, c)
                nxt()
            T["kq"] = o
            gt = gates()
            nxt = step(sd, gt)
            for c in range(2):
                bs, td = project_moving(512, nxt)
                for t in range(2):
                    o = act(v[:, t, 512 * c:512 * c + 512], banks[bs[t]][:, :], ACT.Copy, td)
                    free[bs[t]] = [o]
                nxt()
            T["v"] = o
            gg = gla()
            nxt = step(sd, gg)
            for dst in (gs, zs):
                for c in range(2):
                    bs, td = project_moving(512, nxt)
                    for t in range(2):
                        o = act(dst[:, t, 512 * c:512 * c + 512], banks[bs[t]][:, :], ACT.Silu, td)
                        free[bs[t]] = [o]
                    if dst is gs:
                        T["g"] = o
                    nxt()
            for _ in sd:
                pass
            for _ in gg:
                pass

            def turn(j):
                src, base = (gs, 8) if j < 4 else (zs, 0)
                kt = 2 * (j + 4) if j < 4 else 2 * (j - 4)
                slots = [(8 + 2 * j) % 12, (9 + 2 * j) % 12]
                turn_to_slot(lambda t, i: src[:, t, 128 * (kt + i - base):128 * (kt + i - base) + 128],
                             lambda i: col("gla_norm", i) if j < 4 else col("ssd_norm", kt + i),
                             slots, T["yg"] if j < 4 else T["ys"])
                return slots

            nx = turn(0)
            nx2 = turn(1)
            for c in range(2):
                for g in range(2):
                    gsl = slice(512 * g, 512 * g + 512)
                    i = 8 + 2 * c + g
                    o2 = tt(zs[:, c, gsl], zs[:, c, gsl], xs[:, c, gsl], ALU.mult, o, T["y"])
                    t_ss = act(xs[:, c, gsl], zs[:, c, gsl], ACT.Square, o2, accum_out=st[:, i:i + 1])
            r = rstd(st[:, 8:12], 512, t_ss)
            for c in range(2):
                for g in range(2):
                    gsl = slice(512 * g, 512 * g + 512)
                    T["ys"] = ts(zs[:, c, gsl], zs[:, c, gsl], st[:, 8 + 2 * c + g:9 + 2 * c + g], None,
                                 ALU.mult, None, r)
            bs = open_out()
            for j in range(8):
                td = rows_out(bs, nx, j == 0, j == 7)
                nx, nx2 = nx2, turn(j + 2) if j < 6 else None
            close_out(bs, td)

        def mla():
            room = Room()
            c1 = room(NC1)
            cq = room(1344, 2)
            qt = room(3072, 2, 16)
            kf = room(3072, 2, 16)
            v = room(2048, 2)
            o_ = room(2048, 2)
            qT = room(4096, 16)
            kT = room(4096, 16)
            Sb = [room(512) for _ in range(3)]
            PT = [room(512) for _ in range(2)]
            sqb = [room(512) for _ in range(2)]
            stats = room(32 * 4)
            kr = room(64, 2)
            tabs = [room(32, 2) for _ in range(8)]
            t_c1 = load(c1[:, :], d_c1, t_x)
            maskadd = c1[:, 0:256]
            cos, sin = cut(c1[:, 256:288], 2), cut(c1[:, 288:320], 2)
            r = turn_raw("mix_norm_odd", 0)
            DV.wait(t_c1)
            for base, g in ((0, "q_rope_norm"), (4, "k_rope_norm")):
                for i, (tab, half) in enumerate(((cos, 0), (sin, 16), (cos, 16), (sin, 0))):
                    t_tab = tt(tabs[base + i], tab, bc(col(g, half, 16), [P, 2, 16], 1), ALU.mult)
            for c, n in ((0, 512), (512, 160)):
                bs, td = project_moving(n)
                for t in range(2):
                    o = act(cq[:, t, c:c + n], banks[bs[t]][:, 0:n], ACT.Copy, td, r[t], scale=st[:, 4 + t:5 + t])
                    free[bs[t]] = [o]
                    if c == 0:
                        a_ = act(sqb[0][:, 0:384], cq[:, t, 0:384], ACT.Square, accum_out=st[:, 8 + t:9 + t])
            r_q = rstd(st[:, 8:10], 384, a_)
            for t in range(2):
                n_q = ts(cq[:, t, 0:384], cq[:, t, 0:384], st[:, 8 + t:9 + t], None, ALU.mult, None, r_q)
            for t in range(2):
                a_ = act(sqb[0][:, 0:256], cq[:, t, 384:640], ACT.Square, o, accum_out=st[:, 10 + t:11 + t])
                b_ = act(sqb[1][:, 0:32], cq[:, t, 640:672], ACT.Square, accum_out=st[:, 12 + t:13 + t])
            rstd(st[:, 10:12], 256, b_)
            r_k = rstd(st[:, 12:14], 32)
            sl5 = [8, 9, 10, 11, 0]
            turn_to_slot(lambda t, j: cq[:, t, 128 * j:128 * j + 128], lambda j: col("q_lora", j), sl5[:3], n_q)
            for t in range(2):
                n_ = ts(cq[:, t, 384:640], cq[:, t, 384:640], st[:, 10 + t:11 + t], None, ALU.mult, None, r_k)
                k_r = ts(kr[:, t, :], cq[:, t, 640:672], st[:, 12 + t:13 + t], None, ALU.mult, None)
            turn_to_slot(lambda t, j: cq[:, t, 384 + 128 * j:512 + 128 * j], lambda j: col("kv_lora", j), sl5[3:],
                         n_)

            def rope(x1, x2, tab, ra, rb):
                cg1, sg2, cg2, sg1 = tab
                tt(ra, x2, sg2, ALU.mult)
                tt(rb, x1, sg1, ALU.mult)
                tt(x1, x1, cg1, ALU.mult)
                tt(x1, x1, ra, ALU.subtract)
                tt(x2, x2, cg2, ALU.mult)
                return tt(x2, x2, rb, ALU.add)

            blocks = [("q", 0, 16, 32, 64), ("q", 0, 8, 64, 0), ("q", 8, 8, 64, 0), ("k", 0, 8, 64, 0),
                      ("k", 8, 8, 64, 0), ("v", 0, 8, 64, 0), ("v", 8, 8, 64, 0)]
            t_red = [None, None]
            pend = []
            cur = {}
            at_col = [0]

            def finish(item):
                kind, t, b, h0, nh, d, o0, sc_, r_ = item
                dst = (qt if kind == "q" else kf)[:, t, h0:h0 + nh, o0:o0 + d]
                k_ = tt(dst, cut(banks[b][:, :], nh), bc(sc_, [P, nh, d], 2), ALU.mult, r_)
                free[b] = [k_]
                if (kind, o0) == ("q", 64) and t == 1:
                    rope(qt[:, :, :, 64:80], qt[:, :, :, 80:96],
                         [bc(x, [P, 2, 16, 16], 2) for x in tabs[0:4]], ra4, rb4)
                return k_

            ra4 = Sb[0].rearrange("p (t h e) -> p t h e", t=2, h=16)
            rb4 = Sb[1].rearrange("p (t h e) -> p t h e", t=2, h=16)
            for bi, (kind, h0, nh, d, o0) in enumerate(blocks):
                kk = 3 if kind == "q" else 2
                base = 0 if kind == "q" else 3
                if kind == "q" or bi in (3, 5):
                    cur["n"], cur["h"], cur["l"] = chunk()
                    c0_ = 0
                else:
                    c0_ = 512
                wh, wl = cur["h"], cur["l"]
                for t in range(2):
                    b = take()
                    for k_ in range(kk):
                        s = sl5[base + k_]
                        PE.wait(slot_ready[s])
                        td = mm3(banks[b][:, :], ahi[:, s, 128 * t:128 * t + 128], alo[:, s, 128 * t:128 * t + 128],
                                 wh[:, k_, c0_:c0_ + 512], wl[:, k_, c0_:c0_ + 512], k_ == 0, k_ == kk - 1)
                        slot_free[s] = [td]
                    if kind == "v":
                        t_v = act(v[:, t, 64 * h0:64 * h0 + 512], banks[b][:, :], ACT.Copy, td)
                        free[b] = [t_v]
                        continue
                    i = (2 * bi + t) % 2
                    a_ = act(sqb[i], banks[b][:, :], ACT.Square, td, t_red[i])
                    sc_ = stats[:, at_col[0]:at_col[0] + nh]
                    at_col[0] += nh
                    t_red[i] = DV.do(lambda e, i=i, sc_=sc_, nh=nh: e.tensor_reduce(sc_, cut(sqb[i], nh), AX,
                                                                                    ALU.add), a_)
                    r_ = rstd(sc_, d, t_red[i])
                    pend.append((kind, t, b, h0, nh, d, o0, sc_, r_))
                    if len(pend) > 2:
                        finish(pend.pop(0))
                done[cur["n"]] = td
                if bi == 4:
                    while pend:
                        t_fin = finish(pend.pop(0))
                    rope(kr[:, :, 0:16], kr[:, :, 16:32], tabs[4:8], cut(PT[0][:, 0:32], 2), cut(PT[1][:, 0:32], 2))
                    for t in range(2):
                        t_r = vcopy(kf[:, t, :, 64:96], bc(kr[:, t, :], [P, 16, 32], 1))
            t_T = {}

            def turn_heads(hp):
                for src, dst, g in ((qt, qT, "qfull"), (kf, kT, "kfull")):
                    b = take()
                    PE.wait(t_r)
                    for i in range(2):
                        for t in range(2):
                            k_ = tr(banks[b][0:96, 256 * i + 128 * t:256 * i + 128 * t + 128],
                                    src[:, t, 2 * hp + i, :], sig=(i == 1 and t == 1))
                    o = dst[0:96, 2 * hp:2 * hp + 2, :]
                    pb = cut(banks[b][0:96, :], 2)
                    if g == "qfull":
                        o = act(o, pb, ACT.Copy, k_, scale=col(g, 0, 1, 96))
                    else:
                        o = ts(o, pb, col(g, 0, 1, 96), None, ALU.mult, None, k_)
                    free[b] = [o]
                    t_T[(hp, g)] = o

            sc = 96.0 ** -0.5
            mx, sums = st[:, 32:64], st[:, 64:96]
            bo = {}
            t_pt = [None, None]
            rounds = [x for h in range(0, 16, 4) for x in ((0, h, 4), (1, h, 2), (1, h + 2, 2))]
            t_sb = [None] * 3
            t_exp, t_cp = {}, {}

            def attend(i):
                t, h0, nh = rounds[i]
                nk = 128 * (t + 1)
                b = take()
                for h in range(nh):
                    for g in ("qfull", "kfull"):
                        PE.wait(t_T[((h0 + h) // 2, g)])
                    ti = mms(banks[b][:, nk * h:nk * h + nk], qT[0:96, h0 + h, 128 * t:128 * t + 128],
                             kT[0:96, h0 + h, 0:nk], True, True)
                S_ = Sb[i % 3]
                o = tt(cut(S_, nh), cut(banks[b][:, :], nh), bc(maskadd[:, 256 - nk:256], [P, nh, nk], 1), ALU.add,
                       ti, t_sb[i % 3])
                free[b] = [o]
                m = mx[:, 16 * t + h0:16 * t + h0 + nh]
                DV.do(lambda e: e.tensor_reduce(m, cut(S_, nh), AX, ALU.max))
                o = ts(m, m, -sc, None, ALU.mult, None)
                for h in range(nh):
                    c = 16 * t + h0 + h
                    o = act(S_[:, nk * h:nk * h + nk], S_[:, nk * h:nk * h + nk], ACT.Exp, o,
                            bias=mx[:, c:c + 1], scale=sc, accum_out=sums[:, c:c + 1])
                t_exp[i] = o

            def turn_p(i):
                b = take()
                PE.wait(t_exp[i])
                for j in range(4):
                    k_ = tr(banks[b][:, 128 * j:128 * j + 128], Sb[i % 3][:, 128 * j:128 * j + 128], sig=(j == 3))
                t_sb[i % 3] = k_
                if i % 2:
                    o = vcopy(PT[i % 2], banks[b][:, :], k_, t_pt[i % 2])
                else:
                    o = act(PT[i % 2], banks[b][:, :], ACT.Copy, k_, t_pt[i % 2])
                free[b] = [o]
                t_cp[i] = o

            def mix(i):
                t, h0, nh = rounds[i]
                g = h0 // 8
                if (t, g) not in bo:
                    bo[(t, g)] = take()
                    held.add(bo[(t, g)])
                ob = banks[bo[(t, g)]]
                PE.wait(t_cp[i], t_v)
                for h in range(nh):
                    hh = (h0 + h) % 8
                    for kt in range(t + 1):
                        j = h * (t + 1) + kt
                        to = mms(ob[:, 64 * hh:64 * hh + 64], PT[i % 2][:, 128 * j:128 * j + 128],
                                 v[:, kt, 64 * (h0 + h):64 * (h0 + h) + 64], kt == 0, kt == t)
                t_pt[i % 2] = to
                if (h0 + nh) % 8 == 0:
                    c = 16 * t + 8 * g
                    DV.do(lambda e: e.reciprocal(sums[:, c:c + 8], sums[:, c:c + 8]), to)
                    o = tt(cut(o_[:, t, 512 * g:512 * g + 512], 8), cut(ob[:, :], 8),
                           bc(sums[:, c:c + 8], [P, 8, 64], 2), ALU.mult)
                    free[bo[(t, g)]] = [o]
                    held.discard(bo[(t, g)])
                    return o

            turn_heads(0)
            turn_heads(1)
            t_on = {}
            for i in range(15):
                if i < 12:
                    attend(i)
                if 1 <= i < 12 and i % 3 != 0 and i < 10:
                    turn_heads(2 + 2 * (i // 3) + (i % 3 - 1))
                if 2 <= i < 14:
                    turn_p(i - 2)
                if i >= 3:
                    o = mix(i - 3)
                    if o is not None:
                        t_on[rounds[i - 3][1] // 8] = o
            bs = open_out()

            def turn(j):
                slots = [8 + (2 * j) % 4, 9 + (2 * j) % 4]
                turn_to_slot(lambda t, i: o_[:, t, 128 * (2 * j + i):128 * (2 * j + i) + 128],
                             lambda i: None, slots, t_on[j // 2])
                return slots

            nx = turn(0)
            for j in range(4):
                cur_s, nx = nx, (turn(j + 1) if j < 3 else None)
                td = rows_out(bs, cur_s, j == 0, j == 3)
            close_out(bs, td)

        def ret_pool():
            room = Room()
            c2 = room(NC2)
            xn = room(2048, 2)
            q, k, v, g, u, tq, tk = (room(1024, 2) for _ in range(7))
            qT, kT = room(1024, 4), room(1024, 4)
            Ms = room(1024, 2)
            kd, sta = room(512), room(512)
            tmp = room(512)
            pw = room(512)
            yT = room(1024, 4)
            cs, sn = room(128, 2), room(128, 2)
            ang, kk = room(128), room(128)
            ps = room(4)
            bst = room(48)
            mv = room(16)
            t_c2 = load(c2[:, :], d_c2, t_x)
            t_pw = load(pw, d_poolw, t_x)
            pi = ps[:, 0:2].bitcast(I32)
            t_ps = load(pi, d_pos, t_x)

            def c2s(name):
                a, n = C2[name]
                return c2[:, a:a + n]

            r = turn_raw("mixer_norm_g", 0)
            DV.wait(t_c2, t_ps)
            vcopy(ps[:, 2:4], pi)
            for t in range(2):
                ts(ang[:, 64 * t:64 * t + 64], c2s("invf"), ps[:, 2 + t:3 + t], None, ALU.mult, None)
            big = 12582912.0
            p1, p2 = 6.28125, 0.0019340515136718750
            p3 = 2 * np.pi - p1 - p2
            for off, dst in ((0.0, sn), (0.25, cs)):
                fl = dst.rearrange("p a b -> p (a b)")
                ts(kk, ang, 1 / (2 * np.pi), off, ALU.mult, ALU.add)
                ts(kk, kk, big, None, ALU.add, None)
                ts(kk, kk, big, None, ALU.subtract, None)
                stt(fl, kk, -p1, ang, ALU.mult, ALU.add)
                stt(fl, kk, -p2, fl, ALU.mult, ALU.add)
                stt(fl, kk, -p3, fl, ALU.mult, ALU.add)
                ts(fl, fl, off * 2 * np.pi, None, ALU.add, None)
                o = ts(fl, fl, 3.1415925, -3.1415925, ALU.min, ALU.max)
                t_sc = act(fl, fl, ACT.Sin, o)
            for dst, f in ((q, ACT.Copy), (k, ACT.Copy), (v, ACT.Copy), (g, ACT.Silu), (u, ACT.Copy)):
                bs, td = project_moving(512)
                for t in range(2):
                    o = act(dst[:, t, :], banks[bs[t]][:, :], f, td, r[t], scale=st[:, 4 + t:5 + t])
                    free[bs[t]] = [o]
                if dst is q or dst is k:
                    rot = tq if dst is q else tk
                    for t in range(2):
                        s4, r4 = cut(dst[:, t, :], 4), cut(rot[:, t, :], 4)
                        x1, x2 = s4[:, :, 0:64], s4[:, :, 64:128]
                        cb, sb_ = bc(cs[:, t, :], [P, 4, 64], 1), bc(sn[:, t, :], [P, 4, 64], 1)
                        tmp4 = cut(tmp[:, 0:256], 4)
                        tt(r4[:, :, 0:64], x1, cb, ALU.mult, o, t_sc)
                        tt(tmp4, x2, sb_, ALU.mult)
                        tt(r4[:, :, 0:64], r4[:, :, 0:64], tmp4, ALU.subtract)
                        tt(r4[:, :, 64:128], x1, sb_, ALU.mult)
                        tt(tmp4, x2, cb, ALU.mult)
                        t_rot = tt(r4[:, :, 64:128], r4[:, :, 64:128], tmp4, ALU.add)
            t_u = o
            for src, dst in ((tq, qT), (tk, kT)):
                for hp in range(2):
                    b = take()
                    PE.wait(t_rot)
                    for i in range(2):
                        for t in range(2):
                            h = 2 * hp + i
                            k_ = tr(banks[b][:, 256 * i + 128 * t:256 * i + 128 * t + 128],
                                    src[:, t, 128 * h:128 * h + 128], sig=(i == 1 and t == 1))
                    t_T = act(dst[:, 2 * hp:2 * hp + 2, :], cut(banks[b][:, :], 2), ACT.Copy, k_)
                    free[b] = [t_T]
            bi = []
            for t in range(2):
                b = take()
                PE.wait(t_T)
                for h in range(4):
                    sl = slice(128 * t, 128 * t + 128)
                    to = mms(banks[b][:, 128 * h:128 * h + 128], kT[:, h, sl], qT[:, h, sl], True, True)
                o = tt(Ms[:, t, :], banks[b][:, :], c2s("rmask"), ALU.mult, to)
                free[b] = [o]
                b = take()
                held.add(b)
                bi.append(b)
                PE.wait(o)
                for h in range(4):
                    t_in = mms(banks[b][:, 128 * h:128 * h + 128], Ms[:, t, 128 * h:128 * h + 128],
                               v[:, t, 128 * h:128 * h + 128], True, True)
                if t == 0:
                    t_in0 = t_in
            o = tt(cut(kd, 4), cut(tk[:, 0, :], 4), bc(c2s("kdec"), [P, 4, 128], 2), ALU.mult)
            b = take()
            PE.wait(o)
            for h in range(4):
                to = mms(banks[b][:, 128 * h:128 * h + 128], kd[:, 128 * h:128 * h + 128],
                         v[:, 0, 128 * h:128 * h + 128], True, True)
            o = act(sta, banks[b][:, :], ACT.Copy, to)
            free[b] = [o]
            b = take()
            PE.wait(o)
            for h in range(4):
                to = mms(banks[b][:, 128 * h:128 * h + 128], qT[:, h, 128:256], sta[:, 128 * h:128 * h + 128],
                         True, True)
            ro = q
            o = vcopy(ro[:, 0, :], banks[bi[0]][:, :], t_in0)
            free[bi[0]] = [o]

            def stats_of(t):
                for h in range(4):
                    i = 4 * t + h
                    DV.do(lambda e, i=i, h=h: e.bn_stats(bst[:, 6 * i:6 * i + 6], ro[:, t, 128 * h:128 * h + 128]))
                for h in range(4):
                    i = 4 * t + h
                    o = DV.do(lambda e, i=i: e.bn_aggr(mv[:, 2 * i:2 * i + 2], bst[:, 6 * i:6 * i + 6]))
                vv = cut(mv[:, 8 * t:8 * t + 8], 4)[:, :, 1]
                PO.do(lambda e: e.tensor_scalar(vv, vv, EPS, None, ALU.add), o)
                return ptt(vv, vv, cst("mhalf").to_broadcast([P, 4]), ALU.pow)

            rs = [stats_of(0)]
            o = tt(cut(ro[:, 1, :], 4), cut(banks[b][:, :], 4), bc(c2s("qdec"), [P, 4, 128], 2), ALU.mult, to)
            free[b] = [o]
            o = tt(ro[:, 1, :], ro[:, 1, :], banks[bi[1]][:, :], ALU.add, t_in)
            free[bi[1]] = [o]
            held.difference_update(bi)
            rs.append(stats_of(1))
            bd = c2s("bands")
            for i in range(4):
                b = take()
                PE.wait(t_u, t_c2)
                mm(banks[b][:, 0:256], u[:, 0, 128 * i:128 * i + 128], bd[:, 384 * i:384 * i + 256], True, False)
                to = mms(banks[b][:, 128:256], u[:, 1, 128 * i:128 * i + 128], bd[:, 384 * i + 256:384 * i + 384],
                         False, True)
                o = vcopy(yT[:, i, :], banks[b][:, 0:256], to)
                free[b] = [o]
            for i in range(4):
                b = take()
                PE.wait(o, t_pw)
                to = mms(banks[b][:, 0:256], pw[:, 128 * i:128 * i + 128], yT[:, i, :], True, True)
                free[b] = [fill_slots([(4 + i, banks[b][:, 0:256], col("pool_scale", i))], to)]
            bs = open_out()
            for j in range(2):
                td = rows_out(bs, [4 + 2 * j, 5 + 2 * j], j == 0, False)
            for t in range(2):
                for h in range(4):
                    i = 4 * t + h
                    a = ro[:, t, 128 * h:128 * h + 128]
                    ts(a, a, mv[:, 2 * i:2 * i + 1], mv[:, 2 * i + 1:2 * i + 2], ALU.subtract, ALU.mult, rs[t])
                o = tt(ro[:, t, :], ro[:, t, :], g[:, t, :], ALU.mult)
            turn_to_slot(lambda t, j: ro[:, t, 128 * j:128 * j + 128], lambda j: col("ret_norm", j),
                         [0, 1, 2, 3], o)
            for j in range(2):
                td = rows_out(bs, [2 * j, 2 * j + 1], False, j == 1)
            close_out(bs, td)

        def conformer():
            room = Room()
            rows = room(1024)
            up = room(8 * 286, 8)
            cv = room(2048, 8)
            dn = room(2048, 2)
            xn = dn
            sg = room(512, 2)
            bst = room(24)
            mv = room(4)
            NG = 12
            diag = room(128 * NG, NG)
            t_r = load(rows, d_rows[:, 0:1024], t_x)
            z = DV.do(lambda e: e.memset(up[:, :, 0:30], 0.0))
            norm_x("mixer_norm_g", 8, xn)
            t_sg = [None, None]
            t_dg = [None] * NG
            t_pe, pb = {}, {}
            on_pe = [9, 9, 9, 9, 9, 9, 15, 15]
            nd = [0]
            t_u, t_cv = {}, {}

            def taps_pe(ft):
                n = on_pe[ft]
                b = take()
                held.add(b)
                PE.wait(t_u[ft])
                for w in range(31 - n, 31):
                    s = nd[0] % NG
                    nd[0] += 1
                    a = act(diag[:, s, :], ident, ACT.Copy, t_dg[s], scale=col("w_dw", 8 * w + ft))
                    PE.wait(a)
                    t_dg[s] = mms(banks[b][:, 0:256], diag[:, s, :], up[:, ft, w:w + 256], w == 31 - n, w == 30)
                t_pe[ft], pb[ft] = t_dg[s], b

            def taps_dve(ft):
                n = 31 - on_pe[ft]
                ac = cv[:, ft, :]
                ts(ac, up[:, ft, 0:256], col("w_dw", ft), col("b_dw", ft), ALU.mult, ALU.add)
                for w in range(1, n):
                    stt(ac, up[:, ft, w:w + 256], col("w_dw", 8 * w + ft), ac, ALU.mult, ALU.add)
                t_cv[ft] = tt(ac, ac, banks[pb[ft]][:, 0:256], ALU.add, t_pe[ft])
                free[pb[ft]] = [t_cv[ft]]
                held.discard(pb[ft])

            for j in range(5):
                if j < 4:
                    ba, ta = project_stationary()
                if j:
                    taps_pe(2 * j - 2)
                    taps_dve(2 * j - 2)
                if j < 4:
                    bg, tg = project_stationary()
                if j == 4:
                    taps_pe(7)
                    taps_dve(7)
                    break
                for i in range(2):
                    ft = 2 * j + i
                    o = act(sg[:, i, :], banks[bg][:, 256 * i:256 * i + 256], ACT.Sigmoid, tg, t_sg[i],
                            bias=col("b_pw1", 8 + ft))
                    t_sg[i] = t_u[ft] = stt(up[:, ft, 30:286], banks[ba][:, 256 * i:256 * i + 256],
                                            col("b_pw1", ft), sg[:, i, :], ALU.add, ALU.mult, o, ta)
                free[bg], free[ba] = [o], [t_sg[1]]
                if j:
                    taps_pe(2 * j - 1)
                    taps_dve(2 * j - 1)
            bb = {}
            for t in range(2):
                for c in range(2):
                    b = take()
                    for i in range(4):
                        PE.wait(t_cv[4 * c + i])
                        k_ = tr(banks[b][:, 128 * i:128 * i + 128], cv[:, 4 * c + i, 128 * t:128 * t + 128],
                                sig=(i == 3))
                    bb[(t, c)] = b
                    DV.do(lambda e, t=t, c=c, b=b: e.bn_stats(bst[:, 12 * t + 6 * c:12 * t + 6 * c + 6],
                                                              banks[b][:, :]), k_)
                o = DV.do(lambda e, t=t: e.bn_aggr(mv[:, 2 * t:2 * t + 2], bst[:, 12 * t:12 * t + 12]))
            vv = cut(mv, 2)[:, :, 1]
            PO.do(lambda e: e.tensor_scalar(vv, vv, EPS, None, ALU.add), o)
            r = ptt(vv, vv, cst("mhalf").to_broadcast([P, 2]), ALU.pow)
            t_dn = {}
            for c in range(2):
                for t in range(2):
                    b = bb[(t, c)]
                    t_dn[c] = ts(dn[:, t, 512 * c:512 * c + 512], banks[b][:, :], mv[:, 2 * t:2 * t + 1],
                                 mv[:, 2 * t + 1:2 * t + 2], ALU.subtract, ALU.mult, r)
                    free[b] = [t_dn[c]]
            bs = open_out()

            def turn(j):
                b = take()
                PE.wait(t_dn[j // 2])
                for i in range(2):
                    for t in range(2):
                        ft = 2 * j + i
                        k_ = tr(banks[b][:, 256 * i + 128 * t:256 * i + 128 * t + 128],
                                dn[:, t, 128 * ft:128 * ft + 128], sig=(i == 1 and t == 1))
                for i in range(2):
                    ft = 2 * j + i
                    a = act(cv[:, ft, :], banks[b][:, 256 * i:256 * i + 256], ACT.Silu, k_,
                            scale=col("ln_g", ft), bias=col("ln_b", ft))
                free[b] = [a]
                fill_slots([(2 * j + i, cv[:, 2 * j + i, :], None) for i in range(2)], a)

            turn(0)
            for j in range(4):
                if j < 3:
                    turn(j + 1)
                if j == 2:
                    for t in range(2):
                        t_x[t] = tt(xt[:, t, :], xt[:, t, :], rows, ALU.add, t_r)
                td = rows_out(bs, [2 * j, 2 * j + 1], j == 0, j == 3)
            close_out(bs, td)

        def final():
            room = Room()
            xn = room(2048, 2)
            rows = room(1024)
            t_r = load(rows, d_rows[:, 1024:2048], t_x)
            r = x_rstd()
            for t in range(2):
                o = stt(xn[:, t, :], xt[:, t, :], st[:, 4 + t:5 + t], rows, ALU.mult, ALU.mult, r[t], t_r)
                SP.quiet(lambda e, t=t: e.dma_start(d_out[0, t * P:(t + 1) * P, :], xn[:, t, :]).then_inc(s_out, 16),
                         o)
            SP.wait((s_out, 32))

        stages = [ssd_gla, lambda: ffn("ffn_norm", 0), mla, lambda: ffn("ffn_norm", 8), ret_pool,
                  lambda: ffn("ffn_norm_g", 0), conformer, lambda: ffn("ffn_norm_g", 8), final]
        for i, f in enumerate(stages):
            if i < stop or (stop == 99):
                f()
        if stop != 99:
            for t in range(2):
                SP.quiet(lambda e, t=t: e.dma_start(d_out[0, t * P:(t + 1) * P, :], xt[:, t, :]).then_inc(s_out, 16),
                         t_x)
            for s in range(NR):
                SP.wait((s_raw[s], 16 * ((sent[0] - s + NR - 1) // NR)))
            SP.wait((s_out, 32))

        block = ctx.enter_context(nc.Block())

        @block.sync
        def _(e):
            SP.emit(e)

        @block.tensor
        def _(e):
            PE.emit(e)

        @block.vector
        def _(e):
            DV.emit(e)

        @block.scalar
        def _(e):
            AC.emit(e)

        @block.gpsimd
        def _(e):
            PO.emit(e)


def shape_constants():
    i = np.arange(P)
    c0 = np.zeros((P, NC0), np.float32)
    c0[:, 0:128] = np.eye(P)
    c0[:, 128:256] = i[:, None] <= i[None, :]
    c0[:, 256:384] = (i[:, None] <= i[None, :]) & (i[:, None] // 64 == i[None, :] // 64)
    c0[:, 384:640] = (np.arange(256) % 64 != 0)[None, :]
    c0[:, 640:768] = 1.0
    c0[:, 768] = -0.5
    c1 = np.zeros((P, NC1), np.float32)
    c1[:, 128:256] = np.where(i[None, :] <= i[:, None], 0.0, -1e30)
    inv = (1.0 / (np.float32(10000.0) ** (np.arange(0, 32, 2, dtype=np.float32) / np.float32(32)))).astype(np.float32)
    ang = (np.arange(256, dtype=np.float32)[:, None] * inv[None, :]).astype(np.float32).astype(np.float64)
    c1[:, 256:288] = np.cos(ang).reshape(2, P, 16).transpose(1, 0, 2).reshape(P, 32)
    c1[:, 288:320] = np.sin(ang).reshape(2, P, 16).transpose(1, 0, 2).reshape(P, 32)
    c2 = np.zeros((P, NC2), np.float32)
    lg = np.log1p(-(2.0 ** (-5.0 - np.arange(4))))
    rel = i[None, :] - i[:, None]
    for h in range(4):
        c2[:, 128 * h:128 * h + 128] = np.where(rel >= 0, np.exp(lg[h] * np.maximum(rel, 0)), 0.0) * 128.0 ** -0.5
        c2[:, 512 + h] = np.exp(lg[h] * (127.0 - i)) * 128.0 ** -0.5
        c2[:, 516 + h] = np.exp(lg[h] * (i + 1.0))
    f = np.arange(64, dtype=np.float32)
    c2[:, 520:584] = (np.float32(10000.0) ** (-f / np.float32(64)))[None, :]
    t = np.arange(256)
    for gi, w in enumerate((2, 4, 8, 16)):
        s = t[:, None]
        band = ((s <= t[None, :]) & (s > t[None, :] - w)) / np.minimum(t + 1, w)[None, :] - (s == t[None, :])
        c2[:, 584 + 384 * gi:584 + 384 * gi + 256] = band[0:128]
        c2[:, 584 + 384 * gi + 256:584 + 384 * gi + 384] = band[128:256, 128:256]
    return c0, c1, c2


def pack_inputs(a):
    w = {
        "w_in": a["w_in_even"][0], "w_out": a["w_out_even"][0], "w_dqkv": a["w_dqkv"][0], "w_uq": a["w_uq"][0],
        "w_ukv": a["w_ukv"][0], "w_o": a["w_o_mla"][0], "ret_w_in": a["ret_w_in_2"][0],
        "mix_w_out": a["mix_w_out_2"][0], "pw1": a["conv_w_pw1_2"][0], "pw2": a["conv_w_pw2_2"][0],
    }
    w["w_in_s"] = np.concatenate([w["w_in"][:, 2560:2576], w["w_in"][:, 5648:5664]], axis=1)
    uq = w["w_uq"].reshape(384, 16, 96)
    w["w_uq"] = np.concatenate([uq[:, :, 64:].reshape(384, 512), uq[:, :, :64].reshape(384, 1024)], axis=1)
    ukv = w["w_ukv"].reshape(256, 16, 128)
    w["w_ukv"] = np.concatenate([ukv[:, :, :64].reshape(256, 1024), ukv[:, :, 64:].reshape(256, 1024)], axis=1)
    for i in range(4):
        src = ("w_gate", "w_up", "w_down") if i < 2 else ("ffn_w_gate_2", "ffn_w_up_2", "ffn_w_down_2")
        for tag, name in zip(("gate", "up", "down"), src):
            w[f"{tag}{i}"] = a[name][i % 2]
    ws = np.zeros((len(PLAN), P, CH), np.float32)
    for n, (name, k0, kn, c0, cn) in enumerate(PLAN):
        part = w[name][128 * k0:128 * (k0 + kn), c0:c0 + cn].reshape(kn, P, cn)
        ws[n, :, 0:kn * cn] = part.transpose(1, 0, 2).reshape(P, kn * cn)
    cols = np.zeros((P, NCOL), np.float32)

    def put(name, v, off=0):
        o = COLS[name][0] + off
        v = np.asarray(v).reshape(-1, P).T
        cols[:, o:o + v.shape[1]] = v

    put("mix_norm_even", a["mix_norm_even"])
    put("conv_w", a["conv_w"])
    put("conv_b", a["conv_b"])
    put("ssd_norm", a["ssd_norm"])
    put("gk_b", a["gla_gk_b"])
    put("gla_norm", a["gla_norm"])
    put("ffn_norm", a["ffn_norm"])
    put("mix_norm_odd", a["mix_norm_odd"])
    put("q_lora", a["q_lora_norm"])
    put("kv_lora", a["kv_lora_norm"])
    put("mixer_norm_g", a["mixer_norm_g_2"])
    put("ffn_norm_g", a["ffn_norm_g_2"])
    put("ret_norm", a["ret_norm_g_2"])
    put("pool_scale", a["pool_scale_2"])
    put("b_pw1", a["conv_b_pw1_2"])
    put("w_dw", a["conv_w_dw_2"])
    put("b_dw", a["conv_b_dw_2"])
    put("ln_g", a["conv_ln_g_2"])
    put("ln_b", a["conv_ln_b_2"])
    for name, key in (("qfull", "q_nope_norm"), ("kfull", "k_nope_norm")):
        cols[:, COLS[name][0]] = 1.0
        cols[0:64, COLS[name][0]] = a[key][0]
    for name in ("dt_bias", "a_log", "d_skip", "q_rope_norm", "k_rope_norm"):
        o, n = COLS[name]
        cols[:, o:o + n] = a[name][0][None, :]
    rows = np.zeros((P, 2048), np.float32)
    rows[:, 0:1024] = a["conv_b_pw2_2"][0][None, :]
    rows[:, 1024:2048] = a["final_norm_g_2"][None, :]
    c0, c1, c2 = shape_constants()
    return {
        "d_x": np.ascontiguousarray(a["x"]), "d_ws": ws, "d_cols": cols, "d_c0": c0, "d_c1": c1, "d_c2": c2,
        "d_gkw2": np.ascontiguousarray(a["gla_gk_w2"][0]),
        "d_poolw": np.ascontiguousarray(a["pool_w_2"][0].transpose(1, 0, 2).reshape(P, 512)),
        "d_rows": rows,
        "d_pos": np.ascontiguousarray(a["positions_2"].reshape(2, P).T),
    }


def kernel(**inputs):
    import concourse.bacc as _bacc
    from concourse.bass_utils import run_bass_kernel_spmd as _run

    nc = _bacc.Bacc("TRN2", target_bir_lowering=False, num_devices=1)
    arrays = pack_inputs({n: np.asarray(v) for n, v in inputs.items()})
    args = [nc.dram_tensor(n, v.shape, mybir.dt.from_np(v.dtype), kind="ExternalInput").ap()
            for n, v in arrays.items()]
    out = nc.dram_tensor("out", (1, 256, 1024), F32, kind="ExternalOutput").ap()
    build(nc, *args, out)
    r = _run(nc, [arrays], core_ids=[0])
    return r.results[0]["out"]
```

```python
from contextlib import ExitStack

import numpy as np
import concourse.bass as bass
from concourse import mybir

F32 = mybir.dt.float32
F32R = mybir.dt.float32r
I32 = mybir.dt.int32
U32 = mybir.dt.uint32
ALU = mybir.AluOpType
ACT = mybir.ActivationFunctionType
AX = mybir.AxisListType.X

P = 128
EPS = 1e-6
NR = 3
NH = 3
CH = 2048
SLOTS = 12

COLS = {}
_at = 0
for _name, _n in (("mix_norm_even", 8), ("conv_w", 48), ("conv_b", 12), ("ssd_norm", 8), ("gk_b", 4),
                  ("gla_norm", 2), ("ffn_norm", 16), ("mix_norm_odd", 8), ("q_lora", 3), ("kv_lora", 2),
                  ("qfull", 1), ("kfull", 1), ("mixer_norm_g", 16), ("ffn_norm_g", 16), ("ret_norm", 4),
                  ("pool_scale", 4), ("b_pw1", 16), ("w_dw", 248), ("b_dw", 8), ("ln_g", 8), ("ln_b", 8),
                  ("dt_bias", 16), ("a_log", 16), ("d_skip", 16), ("q_rope_norm", 32), ("k_rope_norm", 32)):
    COLS[_name] = (_at, _n)
    _at += _n
NCOL = _at
C0 = {"ident": (0, 128), "U": (128, 128), "gmask": (256, 128), "reset": (384, 256), "ones": (640, 128),
      "mhalf": (768, 1), "eps": (769, 1)}
NC0 = 770
C1 = {"maskadd": (0, 256), "cos": (256, 32), "sin": (288, 32)}
NC1 = 320
C2 = {"rmask": (0, 512), "kdec": (512, 4), "qdec": (516, 4), "invf": (520, 64), "bands": (584, 1536)}
NC2 = 2120


def weight_plan():
    plan = [("w_in_s", 0, 8, 0, 32)]

    def stationary(w, c0, n):
        return [(w, 0, 8, c0 + 256 * j, 256) for j in range(n // 256)]

    def moving(w, c0, n):
        return [(w, 4 * k, 4, c0 + 512 * j, 512) for j in range(n // 512) for k in range(2)]

    def rows(w, n):
        return [(w, 2 * k, 2, 0, 1024) for k in range(n)]

    def ffn(tag):
        out = []
        for j in range(11):
            out += [("gate" + tag, 0, 8, 256 * j, 256), ("up" + tag, 0, 8, 256 * j, 256)]
            if j:
                out.append(("down" + tag, 2 * (j - 1), 2, 0, 1024))
        return out + [("down" + tag, 20, 2, 0, 1024)]

    plan += stationary("w_in", 1024, 1536)
    plan += stationary("w_in", 3088, 512) + stationary("w_in", 2576, 512)
    plan += moving("w_in", 3600, 1024)
    plan += moving("w_in", 4624, 1024)
    plan += moving("w_in", 0, 1024)
    plan += rows("w_out", 8)[4:] + rows("w_out", 8)[:4] + ffn("0")
    plan += moving("w_dqkv", 0, 512) + [("w_dqkv", 0, 8, 512, 160)]
    plan += [("w_uq", 0, 3, 512 * j, 512) for j in range(3)]
    plan += [("w_ukv", 0, 2, 1024 * j, 1024) for j in range(2)]
    plan += rows("w_o", 4) + ffn("1")
    plan += moving("ret_w_in", 0, 2560) + rows("mix_w_out", 4)[2:] + rows("mix_w_out", 4)[:2] + ffn("2")
    for j in range(4):
        plan += stationary("pw1", 256 * j, 256) + stationary("pw1", 1024 + 256 * j, 256)
    plan += rows("pw2", 4) + ffn("3")
    return plan


PLAN = weight_plan()


class Lane:

    def __init__(self, sem, linked):
        self.sem, self.linked = sem, linked
        self.ops, self.n, self.seen = [], 0, {}

    def wait(self, *toks):
        for t in toks:
            if t is None:
                continue
            if isinstance(t, list):
                self.wait(*t)
                continue
            sem, v = t
            if self.seen.get(id(sem), 0) < v:
                self.seen[id(sem)] = v
                self.ops.append((None, sem, v))

    def quiet(self, fn, *toks):
        self.wait(*toks)
        self.ops.append((fn, None, 0))

    def do(self, fn, *toks):
        self.wait(*toks)
        if self.linked and self.n:
            self.wait((self.sem, self.n))
        return self.loose(fn)

    def loose(self, fn, *toks):
        self.wait(*toks)
        self.n += 1
        self.ops.append((fn, self.sem, 1))
        return (self.sem, self.n)

    def emit(self, eng):
        for fn, sem, v in self.ops:
            if fn is None:
                eng.wait_ge(sem, v)
            else:
                i = fn(eng)
                if sem is not None:
                    i.then_inc(sem, v)


def build(nc, d_x, d_ws, d_cols, d_c0, d_c1, d_c2, d_gkw2, d_poolw, d_rows, d_pos, d_out):
    ctx = ExitStack()
    with ctx:
        def sb(name, shape, dt=F32):
            return ctx.enter_context(nc.sbuf_tensor(name, shape, dt))

        def sem(name):
            return ctx.enter_context(nc.semaphore(name))

        raw = sb("raw", [P, NR, CH])
        whi = sb("whi", [P, NH, CH], F32R)
        wlo = sb("wlo", [P, NH, CH], F32R)
        ahi = sb("ahi", [P, SLOTS, 256], F32R)
        alo = sb("alo", [P, SLOTS, 256], F32R)
        xt = sb("xt", [P, 2, 1024])
        cols = sb("cols", [P, NCOL])
        c0 = sb("c0", [P, NC0])
        st = sb("st", [P, 256])
        NA = 24700
        arena = sb("arena", [P, NA])
        banks = [ctx.enter_context(nc.psum_tensor(f"pb{i}", [P, 512], F32)) for i in range(8)]

        PE, DV, AC, PO, SP = (Lane(sem("s_pe"), False), Lane(sem("s_dve"), True), Lane(sem("s_act"), True),
                              Lane(sem("s_pool"), True), Lane(None, False))
        s_raw = [sem(f"s_raw{i}") for i in range(NR)]
        dma_sems = iter([sem(f"s_in{i}") for i in range(12)])
        s_out = sem("s_out")

        def load(dst, src, *toks):
            s = next(dma_sems)
            SP.quiet(lambda e: e.dma_start(dst, src).then_inc(s, 16), *toks)
            return (s, 16)

        def col(name, i=0, n=1, parts=P):
            a = COLS[name][0] + i
            return cols[0:parts, a:a + n]

        def cst(name):
            a, n = C0[name]
            return c0[:, a:a + n]

        def tt(out, a, b, op, *w):
            return DV.do(lambda e: e.tensor_tensor(out, a, b, op), *w)

        def ts(out, a, s1, s2, op0, op1, *w):
            if op1 is None:
                return DV.do(lambda e: e.tensor_scalar(out, a, s1, None, op0), *w)
            return DV.do(lambda e: e.tensor_scalar(out, a, s1, s2, op0, op1), *w)

        def stt(out, a, s, b, op0, op1, *w):
            return DV.do(lambda e: e.scalar_tensor_tensor(out=out, in0=a, scalar=s, in1=b, op0=op0, op1=op1), *w)

        def vcopy(out, a, *w):
            return DV.do(lambda e: e.tensor_copy(out, a), *w)

        def act(out, a, func, *w, **kw):
            return AC.do(lambda e: e.activation(out, a, func, **kw), *w)

        def ptt(out, a, b, op, *w):
            return PO.do(lambda e: e.tensor_tensor(out, a, b, op), *w)

        def bc(ap, shape, axis):
            return ap.unsqueeze(axis).to_broadcast(shape)

        def f32(ap):
            return ap.bitcast(F32)

        def cut(ap, a, b=None):
            if b is None:
                return ap.rearrange("p (a b) -> p a b", a=a)
            return ap.rearrange("p (a b c) -> p a b c", a=a, b=b)

        def mm(out, l, r, start, stop, skip=False):
            PE.quiet(lambda e: e.matmul(out, l, r, start=start, stop=stop, skip_group_check=skip))

        def mms(out, l, r, start, stop, skip=False):
            return PE.do(lambda e: e.matmul(out, l, r, start=start, stop=stop, skip_group_check=skip))

        def mm3(out, lh, ll, rh, rl, start, stop):
            mm(out, lh, rh, start, False)
            mm(out, lh, rl, False, False)
            return PE.do(lambda e: e.matmul(out, ll, rh, start=False, stop=stop))

        ident = cst("ident")

        def tr(out, a, sig=False):
            k = a.shape[0]
            f = lambda e: e.transpose(out, a, ident[0:k, 0:k])
            return PE.do(f) if sig else PE.quiet(f)

        free = [[] for _ in range(8)]
        held = set()
        turn = [0]

        def claim(b):
            PE.wait(*free[b])
            free[b] = []

        def take(claimed=True):
            while turn[0] % 8 in held:
                turn[0] += 1
            b = turn[0] % 8
            turn[0] += 1
            if claimed:
                claim(b)
            return b

        t_x = [load(xt[:, t, :], d_x[0, t * P:(t + 1) * P, :]) for t in range(2)]
        t_c0 = load(c0[:, :], d_c0)
        t_cols = load(cols[:, :], d_cols)
        for lane in (PE, DV, PO):
            lane.wait(t_c0)

        sent = [0]
        split = [0]
        lo_tok, done = {}, {}

        def send(n):
            w = PLAN[n][2] * PLAN[n][4]
            SP.quiet(lambda e: e.dma_start(raw[:, n % NR, 0:w], d_ws[n, :, 0:w]).then_inc(s_raw[n % NR], 16),
                     lo_tok.get(n - NR))

        def split_chunk(n):
            w = PLAN[n][2] * PLAN[n][4]
            r, h, l = raw[:, n % NR, 0:w], whi[:, n % NH, 0:w], wlo[:, n % NH, 0:w]
            arrived = (s_raw[n % NR], 16 * (n // NR + 1))
            t = AC.loose(lambda e: e.activation(h, r, ACT.Copy), arrived, done.get(n - NH))
            lo_tok[n] = DV.loose(lambda e: e.tensor_tensor(l, r, f32(h), ALU.subtract), arrived, t)

        def ahead(n):
            while split[0] <= min(n, len(PLAN) - 1):
                while sent[0] <= min(split[0] + NR - 1, len(PLAN) - 1):
                    send(sent[0])
                    sent[0] += 1
                split_chunk(split[0])
                split[0] += 1

        used = [0]

        def chunk():
            n = used[0]
            used[0] += 1
            ahead(n + NH - 1)
            PE.wait(lo_tok[n])
            w = PLAN[n][2] * PLAN[n][4]
            k = PLAN[n][2]
            return n, cut(whi[:, n % NH, 0:w], k), cut(wlo[:, n % NH, 0:w], k)

        slot_ready = [None] * SLOTS
        slot_free = [[] for _ in range(SLOTS)]

        def rstd(ap, width, *w):
            PO.do(lambda e: e.tensor_scalar(ap, ap, 1.0 / width, EPS, ALU.mult, ALU.add), *w)
            n = ap.shape[1]
            return ptt(ap, ap, cst("mhalf").to_broadcast([P, n]), ALU.pow)

        def fill_slots(parts, *w):
            for s, src, gain in parts:
                kw = {} if gain is None else {"scale": gain}
                t_hi = act(ahi[:, s, :], src, ACT.Copy, slot_free[s], *w, **kw)
            for s, src, gain in parts:
                h, l = f32(ahi[:, s, :]), alo[:, s, :]
                if gain is None:
                    t_lo = tt(l, src, h, ALU.subtract, t_hi)
                else:
                    t_lo = stt(l, src, gain, h, ALU.mult, ALU.subtract, t_hi)
                slot_free[s] = []
                slot_ready[s] = t_lo
            return t_lo

        def turn_to_slot(srcs, gains, slots, *w):
            for j in range(0, len(slots), 2):
                b = take()
                PE.wait(*w)
                m = min(2, len(slots) - j)
                for i in range(m):
                    for t in range(2):
                        k = tr(banks[b][:, 256 * i + 128 * t:256 * i + 128 * t + 128], srcs(t, j + i),
                               sig=(i == m - 1 and t == 1))
                free[b] = [fill_slots([(slots[j + i], banks[b][:, 256 * i:256 * i + 256], gains(j + i))
                                       for i in range(m)], k)]

        t_sq = [None, None]

        def squares(t, c, b, *w):
            t_sq[t] = act(banks[b][:, :], xt[:, t, 512 * c:512 * c + 512], ACT.Square, *w,
                          accum_out=st[:, 2 * t + c:2 * t + c + 1])
            return t_sq[t]

        def x_rstd():
            late_squares()
            for t in range(2):
                if r_x[t] is None:
                    r_x[t] = tile_rstd(t)
            out = list(r_x)
            r_x[:] = [None, None]
            return out

        r_x = [None, None]

        def tile_rstd(t):
            a = tt(st[:, 4 + t:5 + t], st[:, 2 * t:2 * t + 1], st[:, 2 * t + 1:2 * t + 2], ALU.add, t_sq[t])
            return rstd(st[:, 4 + t:5 + t], 1024, a)

        def turn_x(gname, g0, src, ready):
            bs = [take() for _ in range(4)]
            turned[:] = bs
            for t in range(2):
                for c in range(2):
                    PE.wait(ready[t][c])
                    for j in range(4 * c, 4 * c + 4):
                        o = 256 * (j % 2) + 128 * t
                        k = tr(banks[bs[j // 2]][:, o:o + 128], src[:, t, 128 * j:128 * j + 128], sig=(j % 2 == 1))
                        if t == 1 and j % 2 == 1:
                            free[bs[j // 2]] = [k]
            for i, b in enumerate(bs):
                free[b] = [fill_slots([(2 * i + j, banks[b][:, 256 * j:256 * j + 256], col(gname, g0 + 2 * i + j))
                                       for j in range(2)], *free[b])]

        def norm_x(gname, g0, xn, r):
            ready = []
            for t in range(2):
                ready.append([])
                for c in range(2):
                    h = slice(512 * c, 512 * c + 512)
                    if c:
                        k = ts(xn[:, t, h], xt[:, t, h], st[:, 4 + t:5 + t], None, ALU.mult, None, r[t])
                    else:
                        k = act(xn[:, t, h], xt[:, t, h], ACT.Copy, r[t], scale=st[:, 4 + t:5 + t])
                    ready[t].append(k)
            turn_x(gname, g0, xn, ready)

        def turn_raw(gname, g0):
            turn_x(gname, g0, xt, t_xh)
            out = x_rstd()
            turn[0] = turned[0]
            return out

        t_xh = [[None, None], [None, None]]

        for t in range(2):
            for c in range(2):
                b = 2 * t + c
                squares(t, c, b, t_x[t])
                free[b] = [t_sq[t]]
                t_xh[t][c] = t_x[t]

        def project_moving(ncols, between=None):
            bs = [take(), take()]
            k0, n_chunks = 0, 0
            while k0 < 8:
                n, wh, wl = chunk()
                kk = PLAN[n][2]
                for k in range(kk):
                    PE.wait(slot_ready[k0 + k])
                    for t in range(2):
                        t_done = mm3(banks[bs[t]][:, 0:ncols], ahi[:, k0 + k, 128 * t:128 * t + 128],
                                     alo[:, k0 + k, 128 * t:128 * t + 128], wh[:, k, :], wl[:, k, :],
                                     k0 + k == 0, k0 + k == 7)
                    slot_free[k0 + k] = [t_done]
                done[n] = t_done
                k0 += kk
                if between and k0 < 8:
                    between()
            return bs, t_done

        def project_stationary():
            b = take()
            n, wh, wl = chunk()
            for i in range(2):
                for k in range(8):
                    PE.wait(slot_ready[k])
                    t_done = mm3(banks[b][:, 256 * i:256 * i + 256], wh[:, k, 128 * i:128 * i + 128],
                                 wl[:, k, 128 * i:128 * i + 128], ahi[:, k, :], alo[:, k, :], k == 0, k == 7)
                    slot_free[k] = [t_done]
            done[n] = t_done
            return b, t_done

        def open_out():
            bs = [take(False) for _ in range(4)]
            held.update(bs)
            return bs

        def rows_out(bs, slots, first, last):
            n, wh, wl = chunk()
            if first:
                for b in bs:
                    claim(b)
            t_end = []
            for t in range(2):
                for c in range(2):
                    for k, s in enumerate(slots):
                        PE.wait(slot_ready[s])
                        f, l = first and k == 0, last and k == len(slots) - 1
                        t_done = mm3(banks[bs[2 * t + c]][:, :], ahi[:, s, 128 * t:128 * t + 128],
                                     alo[:, s, 128 * t:128 * t + 128], wh[:, k, 512 * c:512 * c + 512],
                                     wl[:, k, 512 * c:512 * c + 512], f, l)
                    t_end.append(t_done)
            for s in slots:
                slot_free[s] = [t_done]
            done[n] = t_done
            return t_end

        def close_out(bs, t_done, early=False):
            for t in range(2):
                for c in range(2):
                    b = bs[2 * t + c]
                    v = xt[:, t, 512 * c:512 * c + 512]
                    t_xh[t][c] = tt(v, v, banks[b][:, :], ALU.add, t_done[2 * t + c])
                    if t == 0:
                        free[b] = [squares(t, c, b, t_xh[t][c])]
                    else:
                        late.append((t, c, b, t_xh[t][c]))
                t_x[t] = t_xh[t][1]
                if t == 0 and early:
                    r_x[0] = tile_rstd(0)
            kept[:] = bs

        late, kept, turned = [], [], []

        def late_squares():
            for t, c, b, tok in late:
                free[b] = [squares(t, c, b, tok)]
            late.clear()
            held.difference_update(kept)

        def ffn(gname, g0, midway=None, early=False):
            gr, ur = arena[:, 0:512], arena[:, 512:1024]
            sg = cut(arena[:, 1024:2048], 2)
            hh = cut(arena[:, 2048:3072], 2)
            dg, rb = arena[:, 3072:3328], arena[:, 3328:3584]
            r = turn_raw(gname, g0)
            for t in range(2):
                k = ts(dg[:, 128 * t:128 * t + 128], ident, st[:, 4 + t:5 + t], None, ALU.mult, None, r[t])
            t_rb = None
            hf = [None, None]
            turn[0] = kept[0]
            bs = open_out()
            turn[0] = turned[0]
            for j in range(12):
                if j == 6 and midway:
                    midway()
                if j < 11:
                    bg, tg = project_stationary()
                    if j == 0:
                        b = take()
                        PE.wait(k)
                        k = mms(banks[b][:, 0:256], cst("ones"), dg, True, True)
                        t_rb = act(rb, banks[b][:, 0:256], ACT.Copy, k)
                        free[b] = [t_rb]
                        rb2 = bc(rb, [P, 2, 256], 1)
                    g = tt(cut(gr, 2), cut(banks[bg][:, :], 2), rb2, ALU.mult, tg, t_rb)
                    free[bg] = [g]
                    a = act(sg[:, j % 2, :], gr, ACT.Silu, g)
                    bu, tu = project_stationary()
                    h = tt(cut(ur, 2), cut(banks[bu][:, :], 2), rb2, ALU.mult, tu)
                    free[bu] = [h]
                    h = tt(hh[:, j % 2, :], sg[:, j % 2, :], ur, ALU.mult, a)
                    hf[j % 2] = fill_slots([(8 + (2 * j + i) % 4, hh[:, j % 2, 256 * i:256 * i + 256], None)
                                            for i in range(2)], h)
                if j:
                    s = 8 + (2 * (j - 1)) % 4
                    t_done = rows_out(bs, [s, s + 1], j == 1, j == 11)
            close_out(bs, t_done, early)

        class Room:
            def __init__(self):
                self.at = 0

            def __call__(self, n, *shape):
                a = arena[:, self.at:self.at + n]
                self.at += n
                assert self.at <= NA, self.at
                return cut(a, *shape) if shape else a

        def ssd_gla():
            room = Room()
            xbc = room(12 * 259, 12)
            xs = room(2048, 2)
            bt = room(256, 2)
            zs, gs, v = room(2048, 2), room(2048, 2), room(2048, 2)
            q, k, X, U_ = (room(1024) for _ in range(4))
            kend = room(1024, 2)
            S = room(1536, 2, 3)
            sT = room(1024)
            xdte = room(1024)
            M = room(1536, 3)
            pv = room(1024, 2)
            cb4 = room(128)
            glT = room(256)
            small = room(32 * 14)
            w2 = room(512)
            acc = cut(arena[:, 12 * 259 + 2304 + 2048:12 * 259 + 2304 + 2048 + 3072], 12)
            xdt = cut(arena[:, 0:2048], 2)
            t_w2 = load(w2[0:16, :], d_gkw2)
            UM = cst("U")
            dtr, nabs, u, w1, lw, dm, e0, dt, a_, ea, acol, eac, dec = [small[:, 32 * i:32 * i + 32]
                                                                         for i in range(13)]
            r = x_rstd()
            ahead(0)
            for lane in (PE, DV, AC, PO):
                lane.wait(t_cols)
            norm_x("mix_norm_even", 0, zs, r)
            z_pad = PO.do(lambda e: e.memset(xbc[:, :, 0:3], 0.0))
            z_sT = PO.do(lambda e: e.memset(sT[:, :], 0.0))
            T = {}

            def early():
                b, t_done = T["small"]
                t_gl = vcopy(glT[0:32, :], banks[b][0:32, 0:256], t_done)
                free[b] = [t_gl]
                yield
                b = take()
                PE.wait(t_gl)
                for t in range(2):
                    ti = tr(banks[b][:, 32 * t:32 * t + 32], glT[0:32, 128 * t:128 * t + 128], sig=True)
                for t in range(2):
                    o = tt(dtr[:, 16 * t:16 * t + 16], banks[b][:, 32 * t + 16:32 * t + 32], col("dt_bias", 0, 16),
                           ALU.add, ti)
                free[b] = [o]
                n_ = stt(nabs, dtr, -1.0, dtr, ALU.mult, ALU.min)
                yield
                eu = act(u, nabs, ACT.Exp, n_)
                t_ea = act(ea[:, 0:16], col("a_log", 0, 16), ACT.Exp)
                t1 = ts(w1, u, 1.0, None, ALU.add, None, eu)
                ts(dm, w1, 1.0, None, ALU.subtract, None)
                ts(e0, dm, 0.0, None, ALU.is_equal, None)
                tt(dm, dm, e0, ALU.add)
                DV.do(lambda e: e.reciprocal(dm, dm))
                yield
                t2 = act(lw, w1, ACT.Ln, t1)
                gb = [take(), take()]
                PE.wait(t_gl, t_w2)
                for h in range(4):
                    t_g = mms(banks[gb[h // 2]][:, 256 * (h % 2):256 * (h % 2) + 256],
                              w2[0:16, 128 * h:128 * h + 128], glT[0:16, :], True, True)
                for h in range(4):
                    t_X = act(X[:, 256 * h:256 * h + 256], banks[gb[h // 2]][:, 256 * (h % 2):256 * (h % 2) + 256],
                              ACT.Identity, t_g, bias=col("gk_b", h))
                    free[gb[h // 2]] = [t_X]
                tt(lw, lw, e0, ALU.add, t2)
                tt(lw, lw, u, ALU.mult)
                tt(lw, lw, dm, ALU.mult)
                stt(dt, dtr, 0.0, lw, ALU.max, ALU.add)
                T["a"] = stt(cut(a_, 2), cut(dt, 2), -1.0, bc(ea[:, 0:16], [P, 2, 16], 1), ALU.mult, ALU.mult, t_ea)
                yield
                o = stt(U_, X, -1.0, X, ALU.mult, ALU.min, t_X)
                b = take()
                PE.wait(T["a"])
                ta = mms(banks[b][:, 0:32], UM, a_, True, True)
                T["acol"] = vcopy(acol, banks[b][:, 0:32], ta)
                free[b] = [T["acol"]]
                yield
                o = act(U_, U_, ACT.Exp, o)
                T["eac"] = act(eac, acol, ACT.Exp, T["acol"])
                ts(X, X, 0.0, None, ALU.min, None)
                o = ts(U_, U_, 1.0, None, ALU.add, None, o)
                yield
                o = act(U_, U_, ACT.Ln, o)
                tt(U_, X, U_, ALU.subtract, o)
                yield
                for h in range(4):
                    hs = slice(256 * h, 256 * h + 256)
                    T["cum"] = DV.do(lambda e, hs=hs: e.tensor_tensor_scan(X[:, hs], cst("reset"), U_[:, hs], 0.0,
                                                                           ALU.mult, ALU.add))
                yield

            def turn_xs(t, c):
                b = take()
                PE.wait(T["conv"])
                for i in range(4):
                    k_ = tr(banks[b][:, 128 * i:128 * i + 128], xbc[:, 4 * c + i, 3 + 128 * t:131 + 128 * t],
                            sig=(i == 3))
                T["xs"] = act(xs[:, t, 512 * c:512 * c + 512], banks[b][:, :], ACT.Copy, k_)
                free[b] = [T["xs"]]

            def ssd():
                yield
                yield
                turn_xs(0, 0)
                turn_xs(0, 1)
                yield
                turn_xs(1, 0)
                turn_xs(1, 1)
                b = take()
                for g in range(2):
                    k_ = tr(banks[b][:, 128 * g:128 * g + 128], xbc[:, 8 + g, 3:131], sig=True)
                T["bt"] = act(bt[:, :, :], cut(banks[b][:, 0:256], 2), ACT.Copy, k_)
                free[b] = [T["bt"]]
                yield
                for t in range(2):
                    T["xdt"] = tt(cut(xdt[:, t, :], 16), cut(xs[:, t, :], 16),
                                  bc(dt[:, 16 * t:16 * t + 16], [P, 16, 64], 2), ALU.mult, k_, T["xs"])
                    tt(cut(xs[:, t, :], 16), cut(xs[:, t, :], 16), bc(col("d_skip", 0, 16), [P, 16, 64], 2),
                       ALU.mult)
                t_m = [None] * 3
                units = [(c, g, hh) for c in range(2) for g in range(2) for hh in range(2)]
                t_d, t_e, cbs, by = {}, {}, {}, {}

                def decays(n):
                    c, g, hh = units[n]
                    if hh == 0:
                        b = take()
                        cs = slice(3 + 128 * c, 131 + 128 * c)
                        tc = mms(banks[b][:, 0:128], xbc[:, 8 + g, cs], xbc[:, 10 + g, cs], True, True)
                        cbs[(c, g)] = (b, tc)
                    b = take()
                    PE.wait(T["a"])
                    for i in range(4):
                        h = 16 * c + 8 * g + 4 * hh + i
                        tb = mms(banks[b][:, 128 * i:128 * i + 128], a_[:, h:h + 1].to_broadcast([P, P]), UM,
                                 True, True)
                    m = M[:, n % 3, :]
                    for i in range(4):
                        h = 16 * c + 8 * g + 4 * hh + i
                        o = ts(m[:, 128 * i:128 * i + 128], banks[b][:, 128 * i:128 * i + 128],
                               acol[:, h:h + 1], 0.0, ALU.subtract, ALU.min, tb, t_m[n % 3])
                    free[b] = [o]
                    t_d[n] = o

                def exps(n):
                    t_e[n] = act(M[:, n % 3, :], M[:, n % 3, :], ACT.Exp, t_d[n])

                def masked(n):
                    c, g, hh = units[n]
                    m = M[:, n % 3, :]
                    if hh == 0:
                        b, tc = cbs[(c, g)]
                        free[b] = [tt(cb4, banks[b][:, 0:128], UM, ALU.mult, tc)]
                    if c == 0:
                        w = slice(512 * g + 256 * hh, 512 * g + 256 * hh + 256)
                        t_xe[n] = tt(cut(xdte[:, w], 4), cut(xdt[:, 0, w], 4),
                                     cut(m, 4)[:, :, 127:128].to_broadcast([P, 4, 64]), ALU.mult, t_e[n])
                    t_e[n] = tt(cut(m, 4), cut(m, 4), bc(cb4, [P, 4, 128], 1), ALU.mult, t_e[n])

                def outputs(n):
                    c, g, hh = units[n]
                    m = M[:, n % 3, :]
                    if hh == 0:
                        by[(c, g)] = take()
                        held.add(by[(c, g)])
                    PE.wait(t_e[n], T["xdt"])
                    yb = banks[by[(c, g)]]
                    for i in range(4):
                        h = 8 * g + 4 * hh + i
                        ty = mms(yb[:, 64 * (4 * hh + i):64 * (4 * hh + i) + 64],
                                 m[:, 128 * i:128 * i + 128], xdt[:, c, 64 * h:64 * h + 64], True, True)
                    t_m[n % 3] = ty
                    if hh == 0:
                        return
                    gsl = slice(512 * g, 512 * g + 512)
                    b = take()
                    if c == 0:
                        PE.wait(t_xe[n], T["bt"])
                        tp = mms(banks[b][:, :], bt[:, g, :], xdte[:, gsl], True, True)
                        T["pv"] = act(pv[:, g, :], banks[b][:, :], ACT.Copy, tp)
                        free[b] = [T["pv"]]
                    else:
                        PE.wait(T["pv"])
                        to = mms(banks[b][:, :], xbc[:, 10 + g, 131:259], pv[:, g, :], True, True)
                        tmp = xdte[:, gsl]
                        o = tt(cut(tmp, 8), cut(banks[b][:, :], 8),
                               bc(eac[:, 16 + 8 * g:24 + 8 * g], [P, 8, 64], 2), ALU.mult, to, T["eac"], T["pv"])
                        free[b] = [o]
                        tt(xs[:, 1, gsl], xs[:, 1, gsl], tmp, ALU.add)
                    T["y"] = tt(xs[:, c, gsl], xs[:, c, gsl], yb[:, :], ALU.add, ty)
                    free[by[(c, g)]] = [T["y"]]
                    held.discard(by[(c, g)])

                t_xe = {}
                decays(0)
                yield
                exps(0)
                masked(0)
                decays(1)
                yield
                for n in range(8):
                    if n < 7:
                        exps(n + 1)
                    outputs(n)
                    if n < 7:
                        masked(n + 1)
                    if n < 6:
                        decays(n + 2)
                    yield

            def gates():
                e1 = act(U_, X, ACT.Exp, T["cum"], scale=1.0 / 16)
                yield
                vcopy(dec[:, 0:16], cut(U_, 16)[:, :, 63], e1)
                T["q"] = stt(q, q, 128.0 ** -0.5, U_, ALU.mult, ALU.mult, T["kq"])
                o = tt(cut(U_, 16), cut(X, 16)[:, :, 63:64].to_broadcast([P, 16, 64]), cut(X, 16), ALU.subtract)
                yield
                e3 = act(U_, U_, ACT.Exp, o, scale=1.0 / 16)
                e2 = act(X, X, ACT.Exp, o, scale=-1.0 / 16)
                yield
                T["ke"] = tt(U_, U_, k, ALU.mult, e3)
                T["k"] = tt(k, k, X, ALU.mult, e2)
                yield

            def gla():
                for t in range(2):
                    b = take()
                    PE.wait(T["ke"])
                    for h in range(4):
                        k_ = tr(banks[b][:, 128 * h:128 * h + 128],
                                U_[:, 256 * h + 128 * t:256 * h + 128 * t + 128], sig=(h == 3))
                    t_kt = act(kend[:, t, :], banks[b][:, :], ACT.Copy, k_)
                    free[b] = [t_kt]
                yield
                gm = cst("gmask").bitcast(U32)
                for t in range(2):
                    b = take()
                    PE.wait(T["k"], T["q"])
                    for h in range(4):
                        sl = slice(256 * h + 128 * t, 256 * h + 128 * t + 128)
                        ti = mms(banks[b][:, 128 * h:128 * h + 128], k[:, sl], q[:, sl], True, True)
                    for h in range(4):
                        t_s = DV.do(lambda e, b=b, h=h, t=t: e.copy_predicated(
                            sT[:, 512 * t + 128 * h:512 * t + 128 * h + 128], gm,
                            banks[b][:, 128 * h:128 * h + 128]), ti, z_sT)
                    free[b] = [t_s]
                yield
                t_o, t_S = {}, {}

                def states(h):
                    vs = slice(256 * h, 256 * h + 256)
                    bb = [take(), take()]
                    PE.wait(t_kt, T["v"])
                    for c in (0, 2, 1):
                        rows = slice(64 * (c % 2), 64 * (c % 2) + 64)
                        tk = mms(banks[bb[c % 2]][:, 256 * (c // 2):256 * (c // 2) + 256],
                                 kend[rows, c // 2, 128 * h:128 * h + 128], v[rows, c // 2, vs], True, True)
                    s_ = S[:, h % 2]
                    vcopy(s_[:, 0, :], banks[bb[0]][:, 0:256], tk, t_o.get(h - 2))
                    stt(s_[:, 1, :], s_[:, 0, :], dec[:, 4 * h + 1:4 * h + 2], banks[bb[1]][:, 0:256], ALU.mult,
                        ALU.add)
                    t_S[h] = stt(s_[:, 2, :], s_[:, 1, :], dec[:, 4 * h + 2:4 * h + 3], banks[bb[0]][:, 256:512],
                                 ALU.mult, ALU.add)
                    free[bb[0]], free[bb[1]] = [t_S[h]], [t_S[h]]

                def head(h):
                    vs = slice(256 * h, 256 * h + 256)
                    s_ = S[:, h % 2]
                    b = take()
                    PE.wait(t_S[h], t_s)
                    for t in range(2):
                        mm(banks[b][:, 256 * t:256 * t + 256], sT[:, 512 * t + 128 * h:512 * t + 128 * h + 128],
                           v[:, t, vs], True, True, True)
                        for c in (2 * t, 2 * t + 1):
                            if c == 0:
                                continue
                            r0 = 64 * (c % 2)
                            to = mms(banks[b][r0:r0 + 64, 256 * t:256 * t + 256],
                                     q[:, 256 * h + 64 * c:256 * h + 64 * c + 64], s_[:, c - 1, :], False, True, True)
                    t_o[h] = to
                    for t in range(2):
                        i = 12 + 2 * h + t
                        a2 = act(X[:, 0:256], banks[b][:, 256 * t:256 * t + 256], ACT.Square, to, T["k"],
                                 accum_out=st[:, i:i + 1])
                    r = rstd(st[:, 12 + 2 * h:14 + 2 * h], 256, a2)
                    for t in range(2):
                        i = 12 + 2 * h + t
                        T["yg"] = stt(gs[:, t, vs], banks[b][:, 256 * t:256 * t + 256], st[:, i:i + 1],
                                      gs[:, t, vs], ALU.mult, ALU.mult, r, T["g"])
                    free[b] = [T["yg"]]

                states(0)
                yield
                for h in range(4):
                    if h < 3:
                        states(h + 1)
                    head(h)
                    yield

            def step(*gens):
                def go():
                    for g in gens:
                        next(g, None)
                return go

            b = take()
            n, wh, wl = chunk()
            for kk in range(8):
                PE.wait(slot_ready[kk])
                t_done = mm3(banks[b][0:32, 0:256], wh[:, kk, :], wl[:, kk, :], ahi[:, kk, :], alo[:, kk, :],
                             kk == 0, kk == 7)
            done[n] = t_done
            T["small"] = (b, t_done)
            ea_ = early()
            next(ea_)
            for j in range(6):
                b, td = project_stationary()
                fs = slice(2 * j, 2 * j + 2)
                o = act(xbc[:, fs, 3:259], cut(banks[b][:, :], 2), ACT.Copy, td, z_pad)
                for i in range(2):
                    ft = 2 * j + i
                    o = act(acc[:, ft, :], banks[b][:, 256 * i:256 * i + 256], ACT.Identity, td,
                            scale=col("conv_w", 36 + ft), bias=col("conv_b", ft))
                free[b] = [o]
                for i in range(2):
                    ft = 2 * j + i
                    for w in range(3):
                        c = stt(acc[:, ft, :], xbc[:, ft, w:w + 256], col("conv_w", 12 * w + ft), acc[:, ft, :],
                                ALU.mult, ALU.add, o)
                next(ea_, None)
            sd = ssd()
            nxt = step(sd)
            for i, dst in enumerate((k, k, q, q)):
                b, td = project_stationary()
                o = act(dst[:, 512 * (i % 2):512 * (i % 2) + 512], banks[b][:, :], ACT.Copy, td)
                free[b] = [o]
                if i < 2:
                    next(ea_, None)
                    for j in ((0,), (1, 2))[i]:
                        T["conv"] = act(xbc[:, 4 * j:4 * j + 4, 3:259], acc[:, 4 * j:4 * j + 4, :], ACT.Silu, c)
                nxt()
            T["kq"] = o
            gt = gates()
            nxt = step(sd, gt)
            for c in range(2):
                bs, td = project_moving(512, nxt)
                for t in range(2):
                    o = act(v[:, t, 512 * c:512 * c + 512], banks[bs[t]][:, :], ACT.Copy, td)
                    free[bs[t]] = [o]
                nxt()
            T["v"] = o
            gg = gla()
            nxt = step(sd, gg)
            for dst in (gs, zs):
                for c in range(2):
                    bs, td = project_moving(512, nxt)
                    for t in range(2):
                        o = act(dst[:, t, 512 * c:512 * c + 512], banks[bs[t]][:, :], ACT.Silu, td)
                        free[bs[t]] = [o]
                    if dst is gs:
                        T["g"] = o
                    nxt()
            for _ in sd:
                pass
            for _ in gg:
                pass

            def turn(j):
                src, base = (gs, 8) if j < 4 else (zs, 0)
                kt = 2 * (j + 4) if j < 4 else 2 * (j - 4)
                slots = [(8 + 2 * j) % 12, (9 + 2 * j) % 12]
                turn_to_slot(lambda t, i: src[:, t, 128 * (kt + i - base):128 * (kt + i - base) + 128],
                             lambda i: col("gla_norm", i) if j < 4 else col("ssd_norm", kt + i),
                             slots, T["yg"] if j < 4 else T["ys"])
                return slots

            nx = turn(0)
            nx2 = turn(1)
            for c in range(2):
                for g in range(2):
                    gsl = slice(512 * g, 512 * g + 512)
                    i = 8 + 2 * c + g
                    o2 = tt(zs[:, c, gsl], zs[:, c, gsl], xs[:, c, gsl], ALU.mult, o, T["y"])
                    t_ss = act(xs[:, c, gsl], zs[:, c, gsl], ACT.Square, o2, accum_out=st[:, i:i + 1])
            r = rstd(st[:, 8:12], 512, t_ss)
            for c in range(2):
                for g in range(2):
                    gsl = slice(512 * g, 512 * g + 512)
                    T["ys"] = ts(zs[:, c, gsl], zs[:, c, gsl], st[:, 8 + 2 * c + g:9 + 2 * c + g], None,
                                 ALU.mult, None, r)
            bs = open_out()
            for j in range(8):
                td = rows_out(bs, nx, j == 0, j == 7)
                nx, nx2 = nx2, turn(j + 2) if j < 6 else None
            close_out(bs, td)

        def mla():
            room = Room()
            c1 = room(NC1)
            cq = room(1344, 2)
            qt = room(3072, 2, 16)
            kf = room(3072, 2, 16)
            v = room(2048, 2)
            o_ = room(2048, 2)
            qT = room(4096, 16)
            kT = room(4096, 16)
            Sb = [room(512) for _ in range(3)]
            PT = [room(512) for _ in range(2)]
            sqb = [room(512) for _ in range(2)]
            stats = room(32 * 4)
            kr = room(64, 2)
            tabs = [room(32, 2) for _ in range(8)]
            t_c1 = load(c1[:, :], d_c1, t_x)
            maskadd = c1[:, 0:256]
            cos, sin = cut(c1[:, 256:288], 2), cut(c1[:, 288:320], 2)
            r = turn_raw("mix_norm_odd", 0)
            DV.wait(t_c1)
            for base, g in ((0, "q_rope_norm"), (4, "k_rope_norm")):
                for i, (tab, half) in enumerate(((cos, 0), (sin, 16), (cos, 16), (sin, 0))):
                    t_tab = tt(tabs[base + i], tab, bc(col(g, half, 16), [P, 2, 16], 1), ALU.mult)
            for c, n in ((0, 512), (512, 160)):
                bs, td = project_moving(n)
                for t in range(2):
                    o = act(cq[:, t, c:c + n], banks[bs[t]][:, 0:n], ACT.Copy, td, r[t], scale=st[:, 4 + t:5 + t])
                    free[bs[t]] = [o]
                    if c == 0:
                        a_ = act(sqb[0][:, 0:384], cq[:, t, 0:384], ACT.Square, accum_out=st[:, 8 + t:9 + t])
            r_q = rstd(st[:, 8:10], 384, a_)
            for t in range(2):
                n_q = ts(cq[:, t, 0:384], cq[:, t, 0:384], st[:, 8 + t:9 + t], None, ALU.mult, None, r_q)
            for t in range(2):
                a_ = act(sqb[0][:, 0:256], cq[:, t, 384:640], ACT.Square, o, accum_out=st[:, 10 + t:11 + t])
                b_ = act(sqb[1][:, 0:32], cq[:, t, 640:672], ACT.Square, accum_out=st[:, 12 + t:13 + t])
            rstd(st[:, 10:12], 256, b_)
            r_k = rstd(st[:, 12:14], 32)
            sl5 = [8, 9, 10, 11, 0]
            turn_to_slot(lambda t, j: cq[:, t, 128 * j:128 * j + 128], lambda j: col("q_lora", j), sl5[:3], n_q)
            for t in range(2):
                n_ = ts(cq[:, t, 384:640], cq[:, t, 384:640], st[:, 10 + t:11 + t], None, ALU.mult, None, r_k)
                k_r = ts(kr[:, t, :], cq[:, t, 640:672], st[:, 12 + t:13 + t], None, ALU.mult, None)

            def rope(x1, x2, tab, ra, rb, *w):
                cg1, sg2, cg2, sg1 = tab
                for out, a, b_, op in ((ra, x2, sg2, ALU.mult), (rb, x1, sg1, ALU.mult), (x1, x1, cg1, ALU.mult),
                                       (x1, x1, ra, ALU.subtract), (x2, x2, cg2, ALU.mult), (x2, x2, rb, ALU.add)):
                    yield ptt(out, a, b_, op, *w)

            for k_rr in rope(kr[:, :, 0:16], kr[:, :, 16:32], tabs[4:8], cut(PT[0][:, 0:32], 2),
                             cut(PT[1][:, 0:32], 2), k_r, t_tab):
                pass
            t_r = []
            for t in range(2):
                t_r.append(PO.do(lambda e, t=t: e.tensor_copy(kf[:, t, :, 64:96], bc(kr[:, t, :], [P, 16, 32], 1))))

            blocks = [("q", 0, 16, 32, 64), ("q", 0, 8, 64, 0), ("q", 8, 8, 64, 0), ("k", 0, 8, 64, 0),
                      ("k", 8, 8, 64, 0), ("v", 0, 8, 64, 0), ("v", 8, 8, 64, 0)]
            t_red = [None, None]
            pend = []
            cur = {}
            at_col = [0]

            def finish(item):
                kind, t, b, h0, nh, d, o0, sc_, r_, _ = item
                if len(pend) < 2:
                    turn_up(item)
                r_ = item[8]
                dst = (qt if kind == "q" else kf)[:, t, h0:h0 + nh, o0:o0 + d]
                k_ = DV.loose(lambda e: e.tensor_tensor(dst, cut(banks[b][:, :], nh), bc(sc_, [P, nh, d], 2),
                                                        ALU.mult), r_)
                free[b] = [k_]
                if o0 == 0:
                    t_heads[h0 // 8].append(k_)
                if (kind, o0) == ("q", 64) and t == 1:
                    ropes.append(rope(qt[:, :, :, 64:80], qt[:, :, :, 80:96],
                                      [bc(x, [P, 2, 16, 16], 2) for x in tabs[0:4]], ra4, rb4, k_))
                return k_

            def root():
                if pend and not pend[-1][9]:
                    a_ = pend[-1]
                    a_[8:] = act(a_[7], a_[7], ACT.Sqrt, a_[8], scale=1.0 / a_[5], bias=cst("eps")), True

            t_heads = [[], []]

            def turn_up(item):
                sc_ = item[7]
                item[8] = DV.loose(lambda e: e.reciprocal(sc_, sc_), item[8])

            ropes = []
            ra4 = Sb[0].rearrange("p (t h e) -> p t h e", t=2, h=16)
            rb4 = Sb[1].rearrange("p (t h e) -> p t h e", t=2, h=16)
            for bi, (kind, h0, nh, d, o0) in enumerate(blocks):
                kk = 3 if kind == "q" else 2
                base = 0 if kind == "q" else 3
                if kind == "q" or bi in (3, 5):
                    cur["n"], cur["h"], cur["l"] = chunk()
                    c0_ = 0
                else:
                    c0_ = 512
                wh, wl = cur["h"], cur["l"]
                for t in range(2):
                    b = take()
                    for k_ in range(kk):
                        s = sl5[base + k_]
                        PE.wait(slot_ready[s])
                        td = mm3(banks[b][:, :], ahi[:, s, 128 * t:128 * t + 128], alo[:, s, 128 * t:128 * t + 128],
                                 wh[:, k_, c0_:c0_ + 512], wl[:, k_, c0_:c0_ + 512], k_ == 0, k_ == kk - 1)
                        slot_free[s] = [td]
                    if kind == "v":
                        t_v = act(v[:, t, 64 * h0:64 * h0 + 512], banks[b][:, :], ACT.Copy, td)
                        free[b] = [t_v]
                        continue
                    i = (2 * bi + t) % 2
                    a_ = act(sqb[i], banks[b][:, :], ACT.Square, td, t_red[i])
                    sc_ = stats[:, at_col[0]:at_col[0] + nh]
                    at_col[0] += nh
                    root()
                    if len(pend) > 1:
                        turn_up(pend[0])
                    t_red[i] = DV.loose(lambda e, i=i, sc_=sc_, nh=nh: e.tensor_reduce(sc_, cut(sqb[i], nh), AX,
                                                                                       ALU.add), a_)
                    pend.append([kind, t, b, h0, nh, d, o0, sc_, t_red[i], False])
                    for g_ in ropes:
                        for _ in range(3):
                            k_ = next(g_, None)
                            t_r.append(k_)
                    if len(pend) > 2:
                        finish(pend.pop(0))
                done[cur["n"]] = td
                if bi == 0:
                    turn_to_slot(lambda t, j: cq[:, t, 384 + 128 * j:512 + 128 * j], lambda j: col("kv_lora", j),
                                 sl5[3:], n_)
                if bi == 4:
                    root()
                    while pend:
                        finish(pend.pop(0))
            t_T = {}

            def turn_heads(hp):
                for src, dst, g in ((qt, qT, "qfull"), (kf, kT, "kfull")):
                    b = take()
                    PE.wait(*t_r, *t_heads[hp // 4])
                    for i in range(2):
                        for t in range(2):
                            k_ = tr(banks[b][0:96, 256 * i + 128 * t:256 * i + 128 * t + 128],
                                    src[:, t, 2 * hp + i, :], sig=(i == 1 and t == 1))
                    o = dst[0:96, 2 * hp:2 * hp + 2, :]
                    pb = cut(banks[b][0:96, :], 2)
                    if g == "qfull":
                        o = act(o, pb, ACT.Copy, k_, scale=col(g, 0, 1, 96))
                    else:
                        o = ts(o, pb, col(g, 0, 1, 96), None, ALU.mult, None, k_)
                    free[b] = [o]
                    t_T[(hp, g)] = o

            sc = 96.0 ** -0.5
            mx, sums = st[:, 32:64], st[:, 64:96]
            bo = {}
            t_pt = [None, None]
            rounds = [x for h in range(0, 16, 4) for x in ((0, h, 4), (1, h, 2), (1, h + 2, 2))]
            t_sb = [None] * 3
            t_exp, t_cp = {}, {}

            def attend(i):
                t, h0, nh = rounds[i]
                nk = 128 * (t + 1)
                b = take()
                for h in range(nh):
                    for g in ("qfull", "kfull"):
                        PE.wait(t_T[((h0 + h) // 2, g)])
                    ti = mms(banks[b][:, nk * h:nk * h + nk], qT[0:96, h0 + h, 128 * t:128 * t + 128],
                             kT[0:96, h0 + h, 0:nk], True, True)
                S_ = Sb[i % 3]
                o = tt(cut(S_, nh), cut(banks[b][:, :], nh), bc(maskadd[:, 256 - nk:256], [P, nh, nk], 1), ALU.add,
                       ti, t_sb[i % 3])
                free[b] = [o]
                m = mx[:, 16 * t + h0:16 * t + h0 + nh]
                DV.do(lambda e: e.tensor_reduce(m, cut(S_, nh), AX, ALU.max))
                o = ts(m, m, -sc, None, ALU.mult, None)
                for h in range(nh):
                    c = 16 * t + h0 + h
                    o = act(S_[:, nk * h:nk * h + nk], S_[:, nk * h:nk * h + nk], ACT.Exp, o,
                            bias=mx[:, c:c + 1], scale=sc, accum_out=sums[:, c:c + 1])
                t_exp[i] = o

            def turn_p(i):
                b = take()
                PE.wait(t_exp[i])
                for j in range(4):
                    k_ = tr(banks[b][:, 128 * j:128 * j + 128], Sb[i % 3][:, 128 * j:128 * j + 128], sig=(j == 3))
                t_sb[i % 3] = k_
                if i % 2:
                    o = vcopy(PT[i % 2], banks[b][:, :], k_, t_pt[i % 2])
                else:
                    o = act(PT[i % 2], banks[b][:, :], ACT.Copy, k_, t_pt[i % 2])
                free[b] = [o]
                t_cp[i] = o

            def mix(i):
                t, h0, nh = rounds[i]
                g = h0 // 8
                if (t, g) not in bo:
                    bo[(t, g)] = take()
                    held.add(bo[(t, g)])
                ob = banks[bo[(t, g)]]
                PE.wait(t_cp[i], t_v)
                for h in range(nh):
                    hh = (h0 + h) % 8
                    for kt in range(t + 1):
                        j = h * (t + 1) + kt
                        to = mms(ob[:, 64 * hh:64 * hh + 64], PT[i % 2][:, 128 * j:128 * j + 128],
                                 v[:, kt, 64 * (h0 + h):64 * (h0 + h) + 64], kt == 0, kt == t)
                t_pt[i % 2] = to
                if (h0 + nh) % 8 == 0:
                    c = 16 * t + 8 * g
                    DV.do(lambda e: e.reciprocal(sums[:, c:c + 8], sums[:, c:c + 8]), to)
                    o = tt(cut(o_[:, t, 512 * g:512 * g + 512], 8), cut(ob[:, :], 8),
                           bc(sums[:, c:c + 8], [P, 8, 64], 2), ALU.mult)
                    free[bo[(t, g)]] = [o]
                    held.discard(bo[(t, g)])
                    return o

            turn_heads(0)
            turn_heads(1)
            t_on = {}
            for i in range(15):
                if i < 12:
                    attend(i)
                if 1 <= i < 12 and i % 3 != 0 and i < 10:
                    turn_heads(2 + 2 * (i // 3) + (i % 3 - 1))
                if 2 <= i < 14:
                    turn_p(i - 2)
                if i >= 3:
                    o = mix(i - 3)
                    if o is not None:
                        t_on[rounds[i - 3][1] // 8] = o
            bs = open_out()

            def turn(j):
                slots = [8 + (2 * j) % 4, 9 + (2 * j) % 4]
                turn_to_slot(lambda t, i: o_[:, t, 128 * (2 * j + i):128 * (2 * j + i) + 128],
                             lambda i: None, slots, t_on[j // 2])
                return slots

            nx = turn(0)
            for j in range(4):
                cur_s, nx = nx, (turn(j + 1) if j < 3 else None)
                td = rows_out(bs, cur_s, j == 0, j == 3)
            close_out(bs, td)

        def ret_pool():
            room = Room()
            c2 = room(NC2)
            xn = room(2048, 2)
            q, k, v, g, u, tq, tk = (room(1024, 2) for _ in range(7))
            qT, kT = room(1024, 4), room(1024, 4)
            Ms = room(1024, 2)
            kd, sta = room(512), room(512)
            tmp = room(512)
            pw = room(512)
            yT = room(1024, 4)
            cs, sn = room(128, 2), room(128, 2)
            ang, kk = room(128), room(128)
            ps = room(4)
            bst = room(48)
            mv = room(16)
            t_c2 = load(c2[:, :], d_c2, t_x)
            t_pw = load(pw, d_poolw, t_x)
            pi = ps[:, 0:2].bitcast(I32)
            t_ps = load(pi, d_pos, t_x)

            def c2s(name):
                a, n = C2[name]
                return c2[:, a:a + n]

            r = turn_raw("mixer_norm_g", 0)
            DV.wait(t_c2, t_ps)
            vcopy(ps[:, 2:4], pi)
            for t in range(2):
                ts(ang[:, 64 * t:64 * t + 64], c2s("invf"), ps[:, 2 + t:3 + t], None, ALU.mult, None)
            big = 12582912.0
            p1, p2 = 6.28125, 0.0019340515136718750
            p3 = 2 * np.pi - p1 - p2

            def trig(off, dst):
                fl = dst.rearrange("p a b -> p (a b)")
                ts(kk, ang, 1 / (2 * np.pi), off, ALU.mult, ALU.add)
                ts(kk, kk, big, None, ALU.add, None)
                ts(kk, kk, big, None, ALU.subtract, None)
                stt(fl, kk, -p1, ang, ALU.mult, ALU.add)
                stt(fl, kk, -p2, fl, ALU.mult, ALU.add)
                stt(fl, kk, -p3, fl, ALU.mult, ALU.add)
                ts(fl, fl, off * 2 * np.pi, None, ALU.add, None)
                o = ts(fl, fl, 3.1415925, -3.1415925, ALU.min, ALU.max)
                return act(fl, fl, ACT.Sin, o)
            R = {}

            def retention():
                for src, dst in ((tq, qT), (tk, kT)):
                    for hp in range(2):
                        b = take()
                        PE.wait(R["rq" if src is tq else "rk"])
                        for i in range(2):
                            for t in range(2):
                                h = 2 * hp + i
                                k_ = tr(banks[b][:, 256 * i + 128 * t:256 * i + 128 * t + 128],
                                        src[:, t, 128 * h:128 * h + 128], sig=(i == 1 and t == 1))
                        t_T = act(dst[:, 2 * hp:2 * hp + 2, :], cut(banks[b][:, :], 2), ACT.Copy, k_)
                        free[b] = [t_T]
                    if src is tk:
                        t_kd = tt(cut(kd, 4), cut(tk[:, 0, :], 4), bc(c2s("kdec"), [P, 4, 128], 2), ALU.mult)
                    yield
                t_m = {}
                for t in range(2):
                    b = take()
                    PE.wait(t_T)
                    for h in range(4):
                        sl = slice(128 * t, 128 * t + 128)
                        to = mms(banks[b][:, 128 * h:128 * h + 128], kT[:, h, sl], qT[:, h, sl], True, True)
                    t_m[t] = tt(Ms[:, t, :], banks[b][:, :], c2s("rmask"), ALU.mult, to)
                    free[b] = [t_m[t]]
                b = take()
                PE.wait(t_kd, R["v"])
                for h in range(4):
                    to = mms(banks[b][:, 128 * h:128 * h + 128], kd[:, 128 * h:128 * h + 128],
                             v[:, 0, 128 * h:128 * h + 128], True, True)
                t_sta = act(sta, banks[b][:, :], ACT.Copy, to)
                free[b] = [t_sta]
                yield
                R["bi"], R["in"] = [], []
                for t in range(2):
                    b = take()
                    held.add(b)
                    R["bi"].append(b)
                    PE.wait(t_m[t], R["v"])
                    for h in range(4):
                        t_in = mms(banks[b][:, 128 * h:128 * h + 128], Ms[:, t, 128 * h:128 * h + 128],
                                   v[:, t, 128 * h:128 * h + 128], True, True)
                    R["in"].append(t_in)
                b = take()
                held.add(b)
                PE.wait(t_sta)
                for h in range(4):
                    to = mms(banks[b][:, 128 * h:128 * h + 128], qT[:, h, 128:256], sta[:, 128 * h:128 * h + 128],
                             True, True)
                R["cross"] = (b, to)
                yield

            def rotate(dst, rot, t):
                s4, r4 = cut(dst[:, t, :], 4), cut(rot[:, t, :], 4)
                x1, x2 = s4[:, :, 0:64], s4[:, :, 64:128]
                cb, sb_ = bc(cs[:, t, :], [P, 4, 64], 1), bc(sn[:, t, :], [P, 4, 64], 1)
                tmp4 = cut(tmp[:, 0:256], 4)
                tt(r4[:, :, 0:64], x1, cb, ALU.mult, R["raw"], R["sin"], R["cos"])
                tt(tmp4, x2, sb_, ALU.mult)
                tt(r4[:, :, 0:64], r4[:, :, 0:64], tmp4, ALU.subtract)
                tt(r4[:, :, 64:128], x1, sb_, ALU.mult)
                tt(tmp4, x2, cb, ALU.mult)
                return tt(r4[:, :, 64:128], r4[:, :, 64:128], tmp4, ALU.add)

            def steps():
                R["sin"] = trig(0.0, sn)
                yield
                R["cos"] = trig(0.25, cs)
                yield
                for src, rot, name in ((q, tq, "rq"), (k, tk, "rk")):
                    for t in range(2):
                        R[name] = rotate(src, rot, t)
                        if rot is tk and t == 1:
                            next(rt)
                        yield
                for _ in range(3):
                    next(rt)
                    yield

            rt = retention()
            sp = steps()
            for dst, f in ((q, ACT.Copy), (k, ACT.Copy), (v, ACT.Copy), (g, ACT.Silu), (u, ACT.Copy)):
                bs, td = project_moving(512, lambda: next(sp))
                for t in range(2):
                    o = act(dst[:, t, :], banks[bs[t]][:, :], f, td, r[t], scale=st[:, 4 + t:5 + t])
                    free[bs[t]] = [o]
                if dst is v:
                    R["v"] = o
                if dst is q or dst is k:
                    R["raw"] = o
                next(sp, None)
            t_u = o
            bi = R["bi"]
            b, to = R["cross"]
            t_in0, t_in = R["in"]
            ro = q
            o = vcopy(ro[:, 0, :], banks[bi[0]][:, :], t_in0)
            free[bi[0]] = [o]

            def stats_of(t):
                for h in range(4):
                    i = 4 * t + h
                    DV.do(lambda e, i=i, h=h: e.bn_stats(bst[:, 6 * i:6 * i + 6], ro[:, t, 128 * h:128 * h + 128]))
                for h in range(4):
                    i = 4 * t + h
                    o = DV.do(lambda e, i=i: e.bn_aggr(mv[:, 2 * i:2 * i + 2], bst[:, 6 * i:6 * i + 6]))
                vv = cut(mv[:, 8 * t:8 * t + 8], 4)[:, :, 1]
                PO.do(lambda e: e.tensor_scalar(vv, vv, EPS, None, ALU.add), o)
                return ptt(vv, vv, cst("mhalf").to_broadcast([P, 4]), ALU.pow)

            rs = [stats_of(0)]
            o = tt(cut(ro[:, 1, :], 4), cut(banks[b][:, :], 4), bc(c2s("qdec"), [P, 4, 128], 2), ALU.mult, to)
            free[b] = [o]
            o = tt(ro[:, 1, :], ro[:, 1, :], banks[bi[1]][:, :], ALU.add, t_in)
            free[bi[1]] = [o]
            held.difference_update(bi + [b])
            rs.append(stats_of(1))
            bd = c2s("bands")
            for i in range(4):
                b = take()
                PE.wait(t_u, t_c2)
                mm(banks[b][:, 0:256], u[:, 0, 128 * i:128 * i + 128], bd[:, 384 * i:384 * i + 256], True, False)
                to = mms(banks[b][:, 128:256], u[:, 1, 128 * i:128 * i + 128], bd[:, 384 * i + 256:384 * i + 384],
                         False, True)
                o = act(yT[:, i, :], banks[b][:, 0:256], ACT.Copy, to)
                free[b] = [o]
            for i in range(4):
                b = take()
                PE.wait(o, t_pw)
                to = mms(banks[b][:, 0:256], pw[:, 128 * i:128 * i + 128], yT[:, i, :], True, True)
                free[b] = [fill_slots([(4 + i, banks[b][:, 0:256], col("pool_scale", i))], to)]
            for t in range(2):
                for h in range(4):
                    i = 4 * t + h
                    a = ro[:, t, 128 * h:128 * h + 128]
                    ts(a, a, mv[:, 2 * i:2 * i + 1], mv[:, 2 * i + 1:2 * i + 2], ALU.subtract, ALU.mult, rs[t])
                t_ro = tt(ro[:, t, :], ro[:, t, :], g[:, t, :], ALU.mult)
            bs = open_out()
            for j in range(2):
                td = rows_out(bs, [4 + 2 * j, 5 + 2 * j], j == 0, False)
            turn_to_slot(lambda t, j: ro[:, t, 128 * j:128 * j + 128], lambda j: col("ret_norm", j),
                         [0, 1, 2, 3], t_ro)
            for j in range(2):
                td = rows_out(bs, [2 * j, 2 * j + 1], False, j == 1)
            close_out(bs, td)

        def conformer():
            room = Room()
            rows = room(1024)
            up = room(8 * 286, 8)
            cv = room(2048, 8)
            dn = room(2048, 2)
            xn = dn
            sg = room(512, 2)
            bst = room(24)
            mv = room(4)
            NG = 12
            diag = room(128 * NG, NG)
            t_r = load(rows, d_rows[:, 0:1024], t_x)
            z = DV.do(lambda e: e.memset(up[:, :, 0:30], 0.0))
            norm_x("mixer_norm_g", 8, xn, x_rstd())
            t_sg = [None, None]
            t_dg = [None] * NG
            t_pe, pb = {}, {}
            on_pe = [12, 12, 12, 12, 12, 12, 17, 17]
            nd, now = [0], [0]
            t_u, t_cv = {}, {}

            def taps_pe(ft):
                n = on_pe[ft]
                b = take()
                held.add(b)
                PE.wait(t_u[ft])
                for w in range(31 - n, 31):
                    s = nd[0] % NG
                    nd[0] += 1
                    a = AC.loose(lambda e, s=s, w=w: e.activation(diag[:, s, :], ident, ACT.Copy,
                                                                  scale=col("w_dw", 8 * w + ft)), t_dg[s])
                    PE.wait(a)
                    t_dg[s] = mms(banks[b][:, 0:256], diag[:, s, :], up[:, ft, w:w + 256], w == 31 - n, w == 30)
                t_pe[ft], pb[ft] = t_dg[s], b

            def first_tap(ft):
                t_cv[ft] = act(cv[:, ft, :], up[:, ft, 0:256], ACT.Identity, t_u[ft], scale=col("w_dw", ft),
                               bias=col("b_dw", ft))

            def taps_dve(pair):
                for w in range(1, 31):
                    for ft in pair:
                        if w < 31 - on_pe[ft]:
                            ac = cv[:, ft, :]
                            t_cv[ft] = DV.loose(
                                lambda e, ac=ac, ft=ft, w=w: e.scalar_tensor_tensor(
                                    out=ac, in0=up[:, ft, w:w + 256], scalar=col("w_dw", 8 * w + ft), in1=ac,
                                    op0=ALU.mult, op1=ALU.add), t_cv[ft])
                            yield
                while now[0] < min(pair[1] + 3, 9):
                    yield
                for ft in pair:
                    ac = cv[:, ft, :]
                    bk = pb[ft]
                    t_cv[ft] = DV.loose(lambda e, ac=ac, bk=bk: e.tensor_tensor(ac, ac, banks[bk][:, 0:256], ALU.add),
                                        t_cv[ft], t_pe[ft])
                    free[bk] = [t_cv[ft]]
                    held.discard(bk)

            def pump(gens, n):
                for _ in range(n):
                    while gens:
                        try:
                            next(gens[0])
                            break
                        except StopIteration:
                            gens.pop(0)

            bb = {}

            def stats_of(t, c):
                b = take()
                for i in range(4):
                    PE.wait(t_cv[4 * c + i])
                    k_ = tr(banks[b][:, 128 * i:128 * i + 128], cv[:, 4 * c + i, 128 * t:128 * t + 128],
                            sig=(i == 3))
                bb[(t, c)] = b
                DV.loose(lambda e: e.bn_stats(bst[:, 12 * t + 6 * c:12 * t + 6 * c + 6], banks[b][:, :]), k_)

            work = []
            for p in range(10):
                now[0] = p
                if p < 8:
                    b, td = project_stationary()
                if p == 8:
                    for t in range(2):
                        stats_of(t, 0)
                if p >= 2:
                    taps_pe(p - 2)
                if p < 8 and p % 2 == 0:
                    ba, ta = b, td
                elif p < 8:
                    j = p // 2
                    for i in range(2):
                        ft = 2 * j + i
                        o = act(sg[:, i, :], banks[b][:, 256 * i:256 * i + 256], ACT.Sigmoid, td, t_sg[i],
                                bias=col("b_pw1", 8 + ft))
                        t_sg[i] = t_u[ft] = stt(up[:, ft, 30:286], banks[ba][:, 256 * i:256 * i + 256],
                                                col("b_pw1", ft), sg[:, i, :], ALU.add, ALU.mult, o, ta)
                    free[b], free[ba] = [o], [t_sg[1]]
                    for i in range(2):
                        first_tap(2 * j + i)
                if p < 8 and p % 2:
                    work.append(taps_dve((p - 1, p)))
                pump(work, 22 if p < 8 else 1000 if p == 9 else 0)
            r = []
            for t in range(2):
                stats_of(t, 1)
                o = DV.do(lambda e, t=t: e.bn_aggr(mv[:, 2 * t:2 * t + 2], bst[:, 12 * t:12 * t + 12]))
                vv = mv[:, 2 * t + 1:2 * t + 2]
                PO.do(lambda e, vv=vv: e.tensor_scalar(vv, vv, EPS, None, ALU.add), o)
                r.append(ptt(vv, vv, cst("mhalf"), ALU.pow))
            t_dn = {}
            for c in range(2):
                for t in range(2):
                    b = bb[(t, c)]
                    t_dn[c] = ts(dn[:, t, 512 * c:512 * c + 512], banks[b][:, :], mv[:, 2 * t:2 * t + 1],
                                 mv[:, 2 * t + 1:2 * t + 2], ALU.subtract, ALU.mult, r[t])
                    free[b] = [t_dn[c]]
            bs = open_out()

            def turn(j):
                b = take()
                PE.wait(t_dn[j // 2])
                for i in range(2):
                    for t in range(2):
                        ft = 2 * j + i
                        k_ = tr(banks[b][:, 256 * i + 128 * t:256 * i + 128 * t + 128],
                                dn[:, t, 128 * ft:128 * ft + 128], sig=(i == 1 and t == 1))
                for i in range(2):
                    ft = 2 * j + i
                    a = act(cv[:, ft, :], banks[b][:, 256 * i:256 * i + 256], ACT.Silu, k_,
                            scale=col("ln_g", ft), bias=col("ln_b", ft))
                    fill_slots([(ft, cv[:, ft, :], None)], a)
                free[b] = [a]

            turn(0)
            for j in range(4):
                if j < 3:
                    turn(j + 1)
                if j == 2:
                    for t in range(2):
                        t_x[t] = tt(xt[:, t, :], xt[:, t, :], rows, ALU.add, t_r)
                td = rows_out(bs, [2 * j, 2 * j + 1], j == 0, j == 3)
            close_out(bs, td)

        def final():
            xn = cut(arena[:, 4096:6144], 2)
            r = x_rstd()
            for t in range(2):
                o = stt(xn[:, t, :], xt[:, t, :], st[:, 4 + t:5 + t], final_g, ALU.mult, ALU.mult, r[t], t_fg[0])
                SP.quiet(lambda e, t=t: e.dma_start(d_out[0, t * P:(t + 1) * P, :], xn[:, t, :]).then_inc(s_out, 16),
                         o)
            SP.wait((s_out, 32))

        ssd_gla()
        ffn("ffn_norm", 0)
        mla()
        ffn("ffn_norm", 8)
        ret_pool()
        ffn("ffn_norm_g", 0)
        conformer()
        final_g = arena[:, 6144:7168]
        t_fg = []
        ffn("ffn_norm_g", 8, lambda: t_fg.append(load(final_g, d_rows[:, 1024:2048], t_x)), early=True)
        final()

        block = ctx.enter_context(nc.Block())

        @block.sync
        def _(e):
            SP.emit(e)

        @block.tensor
        def _(e):
            PE.emit(e)

        @block.vector
        def _(e):
            DV.emit(e)

        @block.scalar
        def _(e):
            AC.emit(e)

        @block.gpsimd
        def _(e):
            PO.emit(e)


def shape_constants():
    i = np.arange(P)
    c0 = np.zeros((P, NC0), np.float32)
    c0[:, 0:128] = np.eye(P)
    c0[:, 128:256] = i[:, None] <= i[None, :]
    c0[:, 256:384] = (i[:, None] <= i[None, :]) & (i[:, None] // 64 == i[None, :] // 64)
    c0[:, 384:640] = (np.arange(256) % 64 != 0)[None, :]
    c0[:, 640:768] = 1.0
    c0[:, 768] = -0.5
    c0[:, 769] = EPS
    c1 = np.zeros((P, NC1), np.float32)
    c1[:, 128:256] = np.where(i[None, :] <= i[:, None], 0.0, -1e30)
    inv = (1.0 / (np.float32(10000.0) ** (np.arange(0, 32, 2, dtype=np.float32) / np.float32(32)))).astype(np.float32)
    ang = (np.arange(256, dtype=np.float32)[:, None] * inv[None, :]).astype(np.float32).astype(np.float64)
    c1[:, 256:288] = np.cos(ang).reshape(2, P, 16).transpose(1, 0, 2).reshape(P, 32)
    c1[:, 288:320] = np.sin(ang).reshape(2, P, 16).transpose(1, 0, 2).reshape(P, 32)
    c2 = np.zeros((P, NC2), np.float32)
    lg = np.log1p(-(2.0 ** (-5.0 - np.arange(4))))
    rel = i[None, :] - i[:, None]
    for h in range(4):
        c2[:, 128 * h:128 * h + 128] = np.where(rel >= 0, np.exp(lg[h] * np.maximum(rel, 0)), 0.0) * 128.0 ** -0.5
        c2[:, 512 + h] = np.exp(lg[h] * (127.0 - i)) * 128.0 ** -0.5
        c2[:, 516 + h] = np.exp(lg[h] * (i + 1.0))
    f = np.arange(64, dtype=np.float32)
    c2[:, 520:584] = (np.float32(10000.0) ** (-f / np.float32(64)))[None, :]
    t = np.arange(256)
    for gi, w in enumerate((2, 4, 8, 16)):
        s = t[:, None]
        band = ((s <= t[None, :]) & (s > t[None, :] - w)) / np.minimum(t + 1, w)[None, :] - (s == t[None, :])
        c2[:, 584 + 384 * gi:584 + 384 * gi + 256] = band[0:128]
        c2[:, 584 + 384 * gi + 256:584 + 384 * gi + 384] = band[128:256, 128:256]
    return c0, c1, c2


def pack_inputs(a):
    w = {
        "w_in": a["w_in_even"][0], "w_out": a["w_out_even"][0], "w_dqkv": a["w_dqkv"][0], "w_uq": a["w_uq"][0],
        "w_ukv": a["w_ukv"][0], "w_o": a["w_o_mla"][0], "ret_w_in": a["ret_w_in_2"][0],
        "mix_w_out": a["mix_w_out_2"][0], "pw1": a["conv_w_pw1_2"][0], "pw2": a["conv_w_pw2_2"][0],
    }
    w["w_in_s"] = np.concatenate([w["w_in"][:, 5648:5664], w["w_in"][:, 2560:2576]], axis=1)
    uq = w["w_uq"].reshape(384, 16, 96)
    w["w_uq"] = np.concatenate([uq[:, :, 64:].reshape(384, 512), uq[:, :, :64].reshape(384, 1024)], axis=1)
    ukv = w["w_ukv"].reshape(256, 16, 128)
    w["w_ukv"] = np.concatenate([ukv[:, :, :64].reshape(256, 1024), ukv[:, :, 64:].reshape(256, 1024)], axis=1)
    for i in range(4):
        src = ("w_gate", "w_up", "w_down") if i < 2 else ("ffn_w_gate_2", "ffn_w_up_2", "ffn_w_down_2")
        for tag, name in zip(("gate", "up", "down"), src):
            w[f"{tag}{i}"] = a[name][i % 2]
    ws = np.zeros((len(PLAN), P, CH), np.float32)
    for n, (name, k0, kn, c0, cn) in enumerate(PLAN):
        part = w[name][128 * k0:128 * (k0 + kn), c0:c0 + cn].reshape(kn, P, cn)
        ws[n, :, 0:kn * cn] = part.transpose(1, 0, 2).reshape(P, kn * cn)
    cols = np.zeros((P, NCOL), np.float32)

    def put(name, v, off=0):
        o = COLS[name][0] + off
        v = np.asarray(v).reshape(-1, P).T
        cols[:, o:o + v.shape[1]] = v

    put("mix_norm_even", a["mix_norm_even"])
    put("conv_w", a["conv_w"])
    put("conv_b", a["conv_b"])
    put("ssd_norm", a["ssd_norm"])
    put("gk_b", a["gla_gk_b"])
    put("gla_norm", a["gla_norm"])
    put("ffn_norm", a["ffn_norm"])
    put("mix_norm_odd", a["mix_norm_odd"])
    put("q_lora", a["q_lora_norm"])
    put("kv_lora", a["kv_lora_norm"])
    put("mixer_norm_g", a["mixer_norm_g_2"])
    put("ffn_norm_g", a["ffn_norm_g_2"])
    put("ret_norm", a["ret_norm_g_2"])
    put("pool_scale", a["pool_scale_2"])
    put("b_pw1", a["conv_b_pw1_2"])
    put("w_dw", a["conv_w_dw_2"])
    put("b_dw", a["conv_b_dw_2"])
    put("ln_g", a["conv_ln_g_2"])
    put("ln_b", a["conv_ln_b_2"])
    for name, key in (("qfull", "q_nope_norm"), ("kfull", "k_nope_norm")):
        cols[:, COLS[name][0]] = 1.0
        cols[0:64, COLS[name][0]] = a[key][0]
    for name in ("dt_bias", "a_log", "d_skip", "q_rope_norm", "k_rope_norm"):
        o, n = COLS[name]
        cols[:, o:o + n] = a[name][0][None, :]
    rows = np.zeros((P, 2048), np.float32)
    rows[:, 0:1024] = a["conv_b_pw2_2"][0][None, :]
    rows[:, 1024:2048] = a["final_norm_g_2"][None, :]
    c0, c1, c2 = shape_constants()
    return {
        "d_x": np.ascontiguousarray(a["x"]), "d_ws": ws, "d_cols": cols, "d_c0": c0, "d_c1": c1, "d_c2": c2,
        "d_gkw2": np.ascontiguousarray(a["gla_gk_w2"][0]),
        "d_poolw": np.ascontiguousarray(a["pool_w_2"][0].transpose(1, 0, 2).reshape(P, 512)),
        "d_rows": rows,
        "d_pos": np.ascontiguousarray(a["positions_2"].reshape(2, P).T),
    }


def kernel(**inputs):
    import concourse.bacc as _bacc
    from concourse.bass_utils import run_bass_kernel_spmd as _run

    nc = _bacc.Bacc("TRN2", target_bir_lowering=False, num_devices=1)
    arrays = pack_inputs({n: np.asarray(v) for n, v in inputs.items()})
    args = [nc.dram_tensor(n, v.shape, mybir.dt.from_np(v.dtype), kind="ExternalInput").ap()
            for n, v in arrays.items()]
    out = nc.dram_tensor("out", (1, 256, 1024), F32, kind="ExternalOutput").ap()
    build(nc, *args, out)
    r = _run(nc, [arrays], core_ids=[0])
    return r.results[0]["out"]
```
